# Optimizing a Trainium2 kernel written in Bass

```python
import math
import jax
import jax.numpy as jnp
from jax import lax
import numpy as np

D_MODEL = 1024
BATCH = 1
SEQ = 512
DEPTH = 2

GRID_W = 64
CTX_LEN = 256
EPS = 1e-6
ROPE_THETA = 10000.0
BLOCK_Q = 128
RET_CHUNK = 128
N_GROUPS = 4
GROUP_W = D_MODEL // N_GROUPS
MIX_W = N_GROUPS * GROUP_W

HY_W = GROUP_W
HY_ORDER = 2
HY_SHORT = 3
HY_EMB = 33
HY_BANDS = (HY_EMB - 1) // 2
HY_FFN = 64
HY_NFILT = HY_ORDER * 2 * HY_W
HY_DECAY_SHIFT = 0.05
HY_FAST_PCT = 0.3
HY_SLOW_PCT = 1.5
HY_TARGET = 1e-2
HY_COLS = (HY_ORDER + 1) * HY_W

MLA_HEADS = 4
MLA_Q_RANK = GROUP_W
MLA_KV_RANK = GROUP_W // 2
MLA_NOPE = 64
MLA_ROPE = 32
MLA_V = GROUP_W // MLA_HEADS
MLA_COLS = MLA_Q_RANK + MLA_KV_RANK + MLA_ROPE
MLA_SCALE = (MLA_NOPE + MLA_ROPE) ** -0.5

RET_HEADS = 4
RET_DK = GROUP_W // RET_HEADS
RET_DV = GROUP_W // RET_HEADS
RET_COLS = 2 * RET_HEADS * RET_DK + RET_HEADS * RET_DV + GROUP_W

GQA_HEADS = 4
GQA_KV_HEADS = 2
GQA_HD = GROUP_W // GQA_HEADS
GQA_COLS = (GQA_HEADS + 2 * GQA_KV_HEADS) * GQA_HD
GQA_SCALE = GQA_HD ** -0.5

IN_COLS = HY_COLS + MLA_COLS + RET_COLS + GQA_COLS
D_FF = ((8 * D_MODEL + 3 * 256 - 1) // (3 * 256)) * 256
F32 = jnp.float32

kernel_name = 'hymba_style_hybrid_dit_block'

def rms_norm(x, g):
    xf = x.astype(F32)
    y = xf * lax.rsqrt(jnp.mean(xf * xf, axis=-1, keepdims=True) + EPS)
    return (y * g.astype(F32)).astype(x.dtype)

def modulated_norm(x, g, shift, scale):
    return rms_norm(x, g) * (1.0 + scale) + shift

def ada_mod(cond, w, b):
    return jnp.split(jax.nn.silu(cond) @ w + b, 6, axis=-1)

def axial_rope_tables(rows, cols, dim):
    quarter = dim // 4
    inv = ROPE_THETA ** (-jnp.arange(quarter, dtype=F32) / quarter)
    ang = jnp.concatenate([rows.astype(F32)[:, None] * inv, cols.astype(F32)[:, None] * inv], axis=-1)
    return jnp.cos(ang), jnp.sin(ang)

def apply_rope(x, cos, sin):
    xf = x.astype(F32)
    x1, x2 = jnp.split(xf, 2, axis=-1)
    c = cos[None, :, None, :]
    s = sin[None, :, None, :]
    return jnp.concatenate([x1 * c - x2 * s, x2 * c + x1 * s], axis=-1).astype(x.dtype)

def block_attention(q, k, v, scale):
    b, lq, h, dk = q.shape
    g = k.shape[2]
    r = h // g
    dv = v.shape[-1]
    nb = lq // BLOCK_Q
    qb = q.reshape(b, nb, BLOCK_Q, g, r, dk).transpose(1, 0, 2, 3, 4, 5)

    def one_block(qblk):
        s = jnp.einsum('bqgrd,bkgd->bgrqk', qblk, k, preferred_element_type=F32) * scale
        p = jax.nn.softmax(s, axis=-1)
        return jnp.einsum('bgrqk,bkge->bqgre', p.astype(v.dtype), v)

    o = lax.map(one_block, qb)
    return o.transpose(1, 0, 2, 3, 4, 5).reshape(b, lq, h, dv)

def split_projection(p):
    sizes = (HY_COLS, MLA_Q_RANK, MLA_KV_RANK, MLA_ROPE, RET_COLS, GQA_COLS)
    offs = np.cumsum((0,) + sizes)
    return tuple(p[..., int(offs[i]):int(offs[i + 1])] for i in range(len(sizes)))

def short_conv(u, w, b):
    ch = u.shape[-1]
    y = lax.conv_general_dilated(u, w.astype(u.dtype)[:, None, :], window_strides=(1,),
                                 padding=((HY_SHORT // 2, HY_SHORT // 2),),
                                 dimension_numbers=('NWC', 'WIO', 'NWC'), feature_group_count=ch)
    return y + b.astype(u.dtype)

def hyena_filters(n_tok, w1, b1, w2, b2, w3, b3, freq, w4):
    t = jnp.linspace(0.0, 1.0, n_tok, dtype=F32)[:, None]
    wpos = 2.0 * math.pi * jnp.arange(n_tok, dtype=F32)[:, None] / n_tok
    fb = jnp.linspace(1e-4, HY_BANDS - 1, HY_BANDS, dtype=F32)[None, :]
    z = jnp.concatenate([t, jnp.cos(fb * wpos), -jnp.sin(fb * wpos)], axis=-1)
    fr = freq.astype(F32)
    hdn = jnp.sin(fr * (z @ w1.astype(F32) + b1.astype(F32)))
    hdn = jnp.sin(fr * (hdn @ w2.astype(F32) + b2.astype(F32)))
    hdn = jnp.sin(fr * (hdn @ w3.astype(F32) + b3.astype(F32)))
    filt = hdn @ w4.astype(F32)
    deltas = jnp.linspace(math.log(HY_TARGET) / HY_FAST_PCT, math.log(HY_TARGET) / HY_SLOW_PCT, HY_NFILT, dtype=F32)
    filt = filt * (jnp.exp(-t * jnp.abs(deltas)) + HY_DECAY_SHIFT)
    filt = filt.reshape(n_tok, HY_ORDER, 2, HY_W)
    k_full = jnp.concatenate([filt[:, :, 0], jnp.zeros((1, HY_ORDER, HY_W), F32), filt[:0:-1, :, 1]], axis=0)
    return k_full / jnp.sum(jnp.abs(k_full), axis=0, keepdims=True)

def fft_long_conv(u, kf, d):
    n_tok = u.shape[1]
    y = jnp.fft.irfft(jnp.fft.rfft(u, n=2 * n_tok, axis=1) * kf[None], n=2 * n_tok, axis=1)[:, :n_tok]
    return y + u * d.astype(F32)

def hyena_mixer(u, conv_w, conv_b, w1, b1, w2, b2, w3, b3, freq, w4, bias):
    n_tok = u.shape[1]
    uc = short_conv(u, conv_w, conv_b).astype(F32)
    v, x1, x2 = jnp.split(uc, 3, axis=-1)
    kf = jnp.fft.rfft(hyena_filters(n_tok, w1, b1, w2, b2, w3, b3, freq, w4), axis=0)
    zz = x1 * fft_long_conv(v, kf[:, 0], bias[0])
    y = x2 * fft_long_conv(zz, kf[:, 1], bias[1])
    return y.astype(u.dtype)

def mla_qkv(cq, ckv, kr, gq, wuq, gkv, wukv, rope):
    b, n_tok, _ = cq.shape
    q = (rms_norm(cq, gq) @ wuq).reshape(b, n_tok, MLA_HEADS, MLA_NOPE + MLA_ROPE)
    kv = (rms_norm(ckv, gkv) @ wukv).reshape(b, n_tok, MLA_HEADS, MLA_NOPE + MLA_V)
    q_nope, q_pe = q[..., :MLA_NOPE], q[..., MLA_NOPE:]
    k_nope, v = kv[..., :MLA_NOPE], kv[..., MLA_NOPE:]
    k_pe = kr[:, :, None, :]
    if rope is not None:
        q_pe = apply_rope(q_pe, *rope)
        k_pe = apply_rope(k_pe, *rope)
    q = jnp.concatenate([q_nope, q_pe], axis=-1)
    k = jnp.concatenate([k_nope, jnp.broadcast_to(k_pe, (b, n_tok, MLA_HEADS, MLA_ROPE))], axis=-1)
    return q, k, v

def retention_qkvg(u, rope):
    b, n_tok, _ = u.shape
    qk = RET_HEADS * RET_DK
    q = u[..., :qk].reshape(b, n_tok, RET_HEADS, RET_DK)
    k = u[..., qk:2 * qk].reshape(b, n_tok, RET_HEADS, RET_DK) * (RET_DK ** -0.5)
    v = u[..., 2 * qk:2 * qk + RET_HEADS * RET_DV].reshape(b, n_tok, RET_HEADS, RET_DV)
    g = u[..., 2 * qk + RET_HEADS * RET_DV:]
    if rope is not None:
        q = apply_rope(q, *rope)
        k = apply_rope(k, *rope)
    return q, k, v, g

def retention_chunked(q, k, v, log_g, state0):
    b, n_tok, h, _ = q.shape
    dv = v.shape[-1]
    n_chunks = n_tok // RET_CHUNK
    idx = jnp.arange(RET_CHUNK, dtype=F32)
    diff = idx[:, None] - idx[None, :]
    inner = jnp.where(diff >= 0, jnp.exp(log_g[:, None, None] * jnp.maximum(diff, 0.0)), 0.0)
    q_dec = jnp.exp((idx[:, None] + 1.0) * log_g[None, :])[None, :, :, None]
    k_dec = jnp.exp((RET_CHUNK - 1.0 - idx[:, None]) * log_g[None, :])[None, :, :, None]
    c_dec = jnp.exp(RET_CHUNK * log_g)[None, :, None, None]

    def chunks(t):
        return t.astype(F32).reshape(b, n_chunks, RET_CHUNK, h, t.shape[-1]).transpose(1, 0, 2, 3, 4)

    def step(state, qkv):
        qc, kc, vc = qkv
        s = jnp.einsum('bihd,bjhd->bhij', qc, kc) * inner
        o = jnp.einsum('bhij,bjhe->bihe', s, vc) + jnp.einsum('bihd,bhde->bihe', qc, state) * q_dec
        state = state * c_dec + jnp.einsum('bjhd,bjhe->bhde', kc * k_dec, vc)
        return state, o

    state, o = lax.scan(step, state0, (chunks(q), chunks(k), chunks(v)))
    return o.transpose(1, 0, 2, 3, 4).reshape(b, n_tok, h, dv), state

def retention_final_state(k, v, log_g):
    n_tok = k.shape[1]
    w = jnp.exp((n_tok - 1.0 - jnp.arange(n_tok, dtype=F32))[:, None] * log_g[None, :])
    return jnp.einsum('bjhd,bjhe,jh->bhde', k.astype(F32), v.astype(F32), w)

def bidir_retention(q, k, v, log_g, s_f0, s_b0):
    o_f, s_f = retention_chunked(q, k, v, log_g[0], s_f0)
    o_b, s_b = retention_chunked(q[:, ::-1], k[:, ::-1], v[:, ::-1], log_g[1], s_b0)
    return o_f + o_b[:, ::-1], s_f, s_b

def retention_output(o, g, norm_g):
    b, n_tok = o.shape[0], o.shape[1]
    o = rms_norm(o, norm_g.reshape(RET_HEADS, RET_DV)).reshape(b, n_tok, GROUP_W)
    return (o * jax.nn.silu(g.astype(F32))).astype(g.dtype)

def gqa_qkv(u, gq, gk, rope):
    b, n_tok, _ = u.shape
    nq = GQA_HEADS * GQA_HD
    nk = GQA_KV_HEADS * GQA_HD
    q = rms_norm(u[..., :nq].reshape(b, n_tok, GQA_HEADS, GQA_HD), gq)
    k = rms_norm(u[..., nq:nq + nk].reshape(b, n_tok, GQA_KV_HEADS, GQA_HD), gk)
    v = u[..., nq + nk:].reshape(b, n_tok, GQA_KV_HEADS, GQA_HD)
    if rope is not None:
        q = apply_rope(q, *rope)
        k = apply_rope(k, *rope)
    return q, k, v

def merge_groups(ya, yb, yc, yd, g_out, w_out):
    b, n_tok = ya.shape[0], ya.shape[1]
    y = jnp.stack([ya, yb.astype(ya.dtype), yc.astype(ya.dtype), yd.astype(ya.dtype)], axis=-2)
    y = rms_norm(y, g_out.reshape(N_GROUPS, GROUP_W)).reshape(b, n_tok, MIX_W)
    return y @ w_out

def swiglu(h, w_in, w_out):
    a, g = jnp.split(h @ w_in, 2, axis=-1)
    return (jax.nn.silu(a) * g) @ w_out

def setup_inputs(seed: int = 0) -> dict:
    key = jax.random.key(seed)
    keys = iter(jax.random.split(key, 48))

    def nrm(shape, scale):
        return jax.random.normal(next(keys), shape, F32) * scale

    def gain(shape):
        return 1.0 + nrm(shape, 0.02)

    ret_logit = jnp.asarray(np.log(2.0 ** (5.0 + np.arange(RET_HEADS)) - 1.0), F32)
    return {
        'x': nrm((BATCH, SEQ, D_MODEL), 1.0),
        'c': nrm((BATCH, D_MODEL), 1.0),
        'ctx': nrm((BATCH, CTX_LEN, D_MODEL), 1.0),
        'c_ctx': nrm((D_MODEL,), 1.0),
        'w_mod': nrm((DEPTH, D_MODEL, 6 * D_MODEL), 0.5 * D_MODEL ** -0.5),
        'b_mod': nrm((DEPTH, 6 * D_MODEL), 0.01),
        'norm_attn_g': gain((DEPTH, D_MODEL)),
        'norm_ffn_g': gain((DEPTH, D_MODEL)),
        'w_in': nrm((DEPTH, D_MODEL, IN_COLS), D_MODEL ** -0.5),
        'hy_conv_w': nrm((DEPTH, HY_SHORT, HY_COLS), HY_SHORT ** -0.5),
        'hy_conv_b': nrm((DEPTH, HY_COLS), 0.01),
        'hy_w1': nrm((DEPTH, HY_EMB, HY_FFN), HY_EMB ** -0.5),
        'hy_b1': nrm((DEPTH, HY_FFN), 0.1),
        'hy_w2': nrm((DEPTH, HY_FFN, HY_FFN), HY_FFN ** -0.5),
        'hy_b2': nrm((DEPTH, HY_FFN), 0.1),
        'hy_w3': nrm((DEPTH, HY_FFN, HY_FFN), HY_FFN ** -0.5),
        'hy_b3': nrm((DEPTH, HY_FFN), 0.1),
        'hy_freq': 1.0 + nrm((DEPTH, HY_FFN), 0.1),
        'hy_w4': nrm((DEPTH, HY_FFN, HY_NFILT), HY_FFN ** -0.5),
        'hy_bias': nrm((DEPTH, HY_ORDER, HY_W), 0.1),
        'mla_q_norm_g': gain((DEPTH, MLA_Q_RANK)),
        'mla_w_uq': nrm((DEPTH, MLA_Q_RANK, MLA_HEADS * (MLA_NOPE + MLA_ROPE)), MLA_Q_RANK ** -0.5),
        'mla_kv_norm_g': gain((DEPTH, MLA_KV_RANK)),
        'mla_w_ukv': nrm((DEPTH, MLA_KV_RANK, MLA_HEADS * (MLA_NOPE + MLA_V)), MLA_KV_RANK ** -0.5),
        'ret_decay': ret_logit + nrm((DEPTH, 2, RET_HEADS), 0.05),
        'ret_norm_g': gain((DEPTH, RET_HEADS * RET_DV)),
        'gqa_q_norm_g': gain((DEPTH, GQA_HD)),
        'gqa_k_norm_g': gain((DEPTH, GQA_HD)),
        'out_norm_g': gain((DEPTH, MIX_W)),
        'w_out': nrm((DEPTH, MIX_W, D_MODEL), MIX_W ** -0.5),
        'w_ffn_in': nrm((DEPTH, D_MODEL, 2 * D_FF), D_MODEL ** -0.5),
        'w_ffn_out': nrm((DEPTH, D_FF, D_MODEL), D_FF ** -0.5),
        'final_norm_g': gain((D_MODEL,)),
    }

def reference(x, c, ctx, c_ctx, w_mod, b_mod, norm_attn_g, norm_ffn_g, w_in, hy_conv_w, hy_conv_b,
              hy_w1, hy_b1, hy_w2, hy_b2, hy_w3, hy_b3, hy_freq, hy_w4, hy_bias,
              mla_q_norm_g, mla_w_uq, mla_kv_norm_g, mla_w_ukv, ret_decay, ret_norm_g,
              gqa_q_norm_g, gqa_k_norm_g, out_norm_g, w_out, w_ffn_in, w_ffn_out, final_norm_g):
    b, n_lat = x.shape[0], x.shape[1]
    ROWS = n_lat // GRID_W
    rows = jnp.repeat(jnp.arange(ROWS, dtype=jnp.int32), GRID_W)
    cols = jnp.tile(jnp.arange(GRID_W, dtype=jnp.int32), ROWS)
    rope_mla = axial_rope_tables(rows, cols, MLA_ROPE)
    rope_ret = axial_rope_tables(rows, cols, RET_DK)
    rope_gqa = axial_rope_tables(rows, cols, GQA_HD)
    zero_state = jnp.zeros((b, RET_HEADS, RET_DK, RET_DV), F32)

    xl, xc = x, ctx
    for l in range(DEPTH):
        update_ctx = l < DEPTH - 1
        sh_a, sc_a, g_a, sh_f, sc_f, g_f = ada_mod(c[:, None, :], w_mod[l], b_mod[l])
        csh_a, csc_a, cg_a, csh_f, csc_f, cg_f = ada_mod(c_ctx[None, None, :], w_mod[l], b_mod[l])
        pl = modulated_norm(xl, norm_attn_g[l], sh_a, sc_a) @ w_in[l]
        pc = modulated_norm(xc, norm_attn_g[l], csh_a, csc_a) @ w_in[l]
        hy_l, cq_l, ckv_l, kr_l, ret_in_l, gqa_in_l = split_projection(pl)
        hy_c, cq_c, ckv_c, kr_c, ret_in_c, gqa_in_c = split_projection(pc)

        hy_args = (hy_conv_w[l], hy_conv_b[l], hy_w1[l], hy_b1[l], hy_w2[l], hy_b2[l],
                   hy_w3[l], hy_b3[l], hy_freq[l], hy_w4[l], hy_bias[l])
        ya_l = hyena_mixer(hy_l, *hy_args)

        mla_args = (mla_q_norm_g[l], mla_w_uq[l], mla_kv_norm_g[l], mla_w_ukv[l])
        q_l, k_l, v_l = mla_qkv(cq_l, ckv_l, kr_l, *mla_args, rope_mla)
        q_c, k_c, v_c = mla_qkv(cq_c, ckv_c, kr_c, *mla_args, None)
        yb_l = block_attention(q_l, jnp.concatenate([k_c, k_l], axis=1), jnp.concatenate([v_c, v_l], axis=1),
                               MLA_SCALE).reshape(b, n_lat, GROUP_W)

        log_g = jax.nn.log_sigmoid(ret_decay[l].astype(F32))
        rq_l, rk_l, rv_l, rg_l = retention_qkvg(ret_in_l, rope_ret)
        rq_c, rk_c, rv_c, rg_c = retention_qkvg(ret_in_c, None)
        if update_ctx:
            ro_c, s_f, s_b = bidir_retention(rq_c, rk_c, rv_c, log_g, zero_state, zero_state)
        else:
            s_f = retention_final_state(rk_c, rv_c, log_g[0])
            s_b = retention_final_state(rk_c[:, ::-1], rv_c[:, ::-1], log_g[1])
        ro_l, _, _ = bidir_retention(rq_l, rk_l, rv_l, log_g, s_f, s_b)
        yc_l = retention_output(ro_l, rg_l, ret_norm_g[l])

        gq_l, gk_l, gv_l = gqa_qkv(gqa_in_l, gqa_q_norm_g[l], gqa_k_norm_g[l], rope_gqa)
        gq_c, gk_c, gv_c = gqa_qkv(gqa_in_c, gqa_q_norm_g[l], gqa_k_norm_g[l], None)
        yd_l = block_attention(gq_l, jnp.concatenate([gk_c, gk_l], axis=1), jnp.concatenate([gv_c, gv_l], axis=1),
                               GQA_SCALE).reshape(b, n_lat, GROUP_W)

        xl = xl + g_a * merge_groups(ya_l, yb_l, yc_l, yd_l, out_norm_g[l], w_out[l])
        xl = xl + g_f * swiglu(modulated_norm(xl, norm_ffn_g[l], sh_f, sc_f), w_ffn_in[l], w_ffn_out[l])

        if update_ctx:
            n_ctx = xc.shape[1]
            ya_c = hyena_mixer(hy_c, *hy_args)
            yb_c = block_attention(q_c, k_c, v_c, MLA_SCALE).reshape(b, n_ctx, GROUP_W)
            yc_c = retention_output(ro_c, rg_c, ret_norm_g[l])
            yd_c = block_attention(gq_c, gk_c, gv_c, GQA_SCALE).reshape(b, n_ctx, GROUP_W)
            xc = xc + cg_a * merge_groups(ya_c, yb_c, yc_c, yd_c, out_norm_g[l], w_out[l])
            xc = xc + cg_f * swiglu(modulated_norm(xc, norm_ffn_g[l], csh_f, csc_f), w_ffn_in[l], w_ffn_out[l])

    return rms_norm(xl, final_norm_g)


_drawn_inputs = setup_inputs


def setup_inputs(seed=0):
    import zlib

    import numpy as np

    out = dict(_drawn_inputs(seed))
    spreads = {}
    factors = {'norm_attn_g': 4.876,
     'norm_ffn_g': 6.801,
     'hy_conv_b': 6.501,
     'mla_q_norm_g': 8.0,
     'mla_kv_norm_g': 8.0,
     'ret_norm_g': 8.0,
     'gqa_q_norm_g': 8.0,
     'gqa_k_norm_g': 8.0,
     'out_norm_g': 6.679,
     'final_norm_g': 2.714}
    for name, (base, spread) in spreads.items():
        noise = np.random.default_rng([zlib.crc32(name.encode()), seed]).standard_normal(out[name].shape)
        drawn = base * np.exp(spread * noise) if base else spread * noise
        out[name] = jnp.asarray(drawn.astype(out[name].dtype))
    for name, factor in factors.items():
        out[name] = (out[name] * factor).astype(out[name].dtype)
    return out
```

```python
from contextlib import ExitStack

import numpy as np

import concourse.bass as bass
from concourse import mybir

F32 = mybir.dt.float32
F32R = mybir.dt.float32r
ACT = mybir.ActivationFunctionType
ALU = mybir.AluOpType
AX = mybir.AxisListType.X

P = 128
D = 1024
KT = D // P
LAT, CTX = 512, 256
TOK = LAT + CTX
DEPTH = 2
GRID_W = 64
EPS = 1e-6
THETA = 10000.0
GROUP = 256
DFF = 2816
NF = DFF // P
HEADS = 4
HD = 64
MLA_ROPE = 32
MLA_D = HD + MLA_ROPE
MLA_SCALE = MLA_D ** -0.5
GQA_SCALE = HD ** -0.5
RET_K_SCALE = HD ** -0.5
N_MOD = 6 * KT
HY_EMB = 33
HY_FFN = 64
HY_COLS = 2 * GROUP
NET_LEN = {"lat": LAT, "ctx": CTX}
NET_AT = {"lat": 0, "ctx": LAT}
RING = 4
SPLITS = 2
GRAN = 1024
PAIRS = 4
MAGIC = 1.5 * 2.0 ** 23
INV_2PI = 1.0 / (2.0 * np.pi)
TWO_PI_HI = 6.28125
TWO_PI_LO = 2.0 * np.pi - TWO_PI_HI
PI_BELOW = 3.1415925

PARAM = {}
for _name, _n in (("b_mod", N_MOD), ("g_attn", KT), ("g_ffn", KT), ("conv_b", 6), ("conv_w", 18),
                  ("hy_bias", 4), ("g_q", 2), ("g_kv", 1), ("g_ret", 2), ("g_out", 8), ("g_gq", 1),
                  ("g_gk", 1), ("decay", 8), ("b1", 1), ("b2", 1), ("b3", 1), ("freq", 1)):
    PARAM[_name] = (sum(n for _, n in PARAM.values()), _n)
N_PARAM = sum(n for _, n in PARAM.values())


def lay(at, *parts):
    places = {}
    for name, n in parts:
        places[name] = at
        at += n
    return places, at


AT, R2 = lay(0, ("retq", 2 * TOK), ("retk", 2 * TOK), ("retg", 2 * TOK), ("gq", 2 * TOK), ("gk", TOK),
             ("cq", 2 * TOK), ("ckv", TOK), ("kr", TOK), ("vret", 6 * GROUP), ("vgqa", 6 * P), ("hy", 6 * TOK))
_split, WORK = lay(R2, ("hh", KT * TOK), ("hl", KT * TOK), ("yraw", KT * TOK))
AT.update(_split)
AT["wsplit"] = AT["yraw"]
_hyena, _end = lay(R2, ("klat", 8 * HY_COLS), ("kctx", 4 * HY_COLS), ("scratch", 0), ("vtok", 4 * GROUP),
                   ("y", 8 * GROUP), ("t0", 512), ("t1", 512))
assert _end <= AT["yraw"]
AT.update(_hyena)
_filt, _end = lay(AT["scratch"], ("absd", 1024), ("w4", 1024), ("edec", 2048), ("f", 2048), ("sumabs", 512),
                  ("rn", 512), ("fa", 2048), ("fb", 2048))
assert _end <= WORK
AT.update(_filt)
_ret, _end = lay(AT["hy"], ("rpt", 2 * 6 * LAT), ("dec", 2 * (896 + 640)), ("delta", 896))
assert _end <= AT["yraw"]
AT.update(_ret)
_att, _end = lay(AT["hy"], ("mq", HEADS * TOK), ("mk", HEADS * TOK), ("vmla", 6 * GROUP), ("prob", 3 * TOK),
                 ("pt", 2 * TOK))
assert _end <= AT["yraw"]
AT.update(_att)
AT["cond"], AT["unused"] = AT["wsplit"] + SPLITS * 2 * GRAN, AT["vret"] + TOK
assert AT["cond"] + 2 * D <= WORK and AT["unused"] + D <= AT["hy"]
AT["ha"], AT["ht"] = AT["hy"], AT["hy"] + TOK
_ffn, _end = lay(0, ("uh", 6 * TOK), ("ul", 6 * TOK), ("ut", 2 * TOK))
assert _end <= AT["unused"]
AT.update(_ffn)

NORM_TILES = {"n1": 8, "cq": 2, "ckv": 1, "gq0": 1, "gq1": 1, "gk": 1, "hy": 2, "mla": 2, "ret0": 1,
              "ret1": 1, "ret": 2, "gqa": 2, "n2": 8, "final": 8}
ROPES = ("retq0", "retq1", "retk0", "retk1", "gq0", "gq1", "gk")
WIN = ("cq0", "cq1", "ckv", "kr", "gq0", "gq1", "gk", "retq0", "retq1", "retk0", "retk1", "retg0", "retg1",
       "vret0", "vret1", "vgqa", "hy0", "hy1", "hy2", "hy3", "hy4", "hy5")
N_WIN = len(WIN)
VALUES = ("vret0", "vret1", "vgqa")
ALL_TOKENS = ("ckv", "kr", "gk", "retk0", "retk1") + VALUES
BETWEEN = {2: [("norm", "cq")], 3: [("norm", "ckv"), ("mlp", 0)], 5: [("norm", "gq0")],
           6: [("norm", "gq1"), ("mlp", 1)], 7: [("norm", "gk")], 8: [("rope", "retq0"), ("rope", "gq0")],
           9: [("rope", "retq1"), ("rope", "gq1"), ("mlp", 2)], 10: [("rope", "retk0"), ("rope", "gk")],
           11: [("rope", "retk1")], 14: [("vturn", 0)], 15: [("vturn", 1)], 16: [("vturn", 2)]}
MOD_FIRST = 2 * KT
MOD_PER_WIN = 3
SETS = (6, 6, 6, 4)


def nets(layer):
    return ("lat", "ctx") if layer < DEPTH - 1 else ("lat",)


def width(layer):
    return TOK if layer < DEPTH - 1 else LAT


def input_schedule(layer):
    out, j = [], MOD_FIRST
    for g in range(N_WIN):
        out.append(("win", g))
        for _ in range(min(MOD_PER_WIN, N_MOD - j) if layer == 0 else 0):
            out.append(("mod", j))
            j += 1
        out += BETWEEN.get(g, [])
    return out


def output_schedule(layer, s):
    out = []
    j = s * N_MOD // len(SETS)
    for m in range(KT):
        out.append(("ffo", s, m))
        if layer < DEPTH - 1:
            for _ in range(2 if m < KT - SPLITS else 0):
                out.append(("mod", j))
                j += 1
    return out


def attention_units(layer, kind):
    return [(kind, net, h, t) for h in range(HEADS) for net in nets(layer)
            for t in range(NET_LEN[net] // P)]


def attention_steps(units):
    for i in range(len(units) + 3):
        for job, lag in (("s", 0), ("t", 2), ("pv", 3)):
            if 0 <= i - lag < len(units):
                yield job, units[i - lag]


def retention_units(layer):
    return [(net, h) for h in range(HEADS) for net in nets(layer)]


class Plan:

    def __init__(self):
        self.jobs, self.job = [], {}
        self.granules = []
        self.norm, self.unit = {}, {}
        self.splits, self.split = [], {}
        for j in range(MOD_FIRST):
            self.modulation(0, j)
        for layer in range(DEPTH):
            self.layer(layer)
        self.add_norm(DEPTH, "final")
        self.granules = [g[1:] for g in sorted(self.granules, key=lambda g: g[0])]
        self.granule = {g[0]: n for n, g in enumerate(self.granules)}
        count = {"A": 0, "V": 0}
        self.before = []
        for who in self.jobs:
            self.before.append(dict(count))
            count[who] += 1

    def add(self, who, *key):
        self.job[key] = len(self.jobs)
        self.jobs.append(who)

    def grain(self, *key, split=False):
        job = len(self.jobs) - 1
        if not split:
            self.granules.append((job, key, "job", job))
            return
        s = self.split[key] = len(self.splits)
        self.splits.append(job)
        starts = key[1] == "wout" or key[:2] == (0, "win")
        if starts and key[2] < SPLITS:
            after = job - 1 - key[2]
        else:
            after = self.splits[s - SPLITS]
        self.granules.append((after - 0.5, key, "split", s))

    def add_norm(self, layer, name):
        tiles = [n for _, _, n in self.norm.values()]
        self.norm[layer, name] = (len(tiles), sum(tiles), NORM_TILES[name])
        self.add("A", layer, "norm", name)

    def modulation(self, l, j):
        self.granules.append((len(self.jobs) - 1, (l, "mod", j), "mod", l * N_MOD + j))

    def layer(self, l):
        add, grain = self.add, self.grain
        self.add_norm(l, "n1")
        for what, i in input_schedule(l):
            if what == "win":
                add("V" if WIN[i][:2] == "hy" else "A", l, "win", i)
                grain(l, "win", i, split=True)
            elif what == "mod":
                self.modulation(l, i)
            elif what == "norm":
                self.add_norm(l, i)
            else:
                add("A" if what == "vturn" else "V", l, what, i)
        for net in nets(l):
            nt = NET_LEN[net] // P
            for t in range(nt):
                add("V", l, "filt", net, t)
            add("V", l, "l1", net)
            for i in range(nt):
                add("V", l, "spec", net, i)
            add("V", l, "nyq", net)
            for t in range(nt if net == "lat" else 1):
                grain(l, "F", net, t, "spec")
        for net in nets(l):
            nt = NET_LEN[net] // P
            for o in range(2):
                add("A", l, "turn", net, o)
                for i in range(nt // 2):
                    add("V", l, "fwd", net, o, i)
                for t in range(nt if net == "lat" else 1):
                    grain(l, "F", net, t, o)
                add("V", l, "inv", net, o)
                for t in range(nt if net == "lat" else 1):
                    grain(l, "G", net, t, o)
        units = retention_units(l)
        for i, un in enumerate(units + [None]):
            if un:
                for part in range(3 if un[0] == "lat" else 1):
                    add("V", l, "rs", *un, part)
            if i:
                add("A", l, "rpv", *units[i - 1])
        for name in ("ret0", "ret1", "hy"):
            self.add_norm(l, name)
        self.attention(l, "gqa")
        for name in ("ret", "gqa"):
            self.add_norm(l, name)
        for h in range(HEADS):
            add("A", l, "mq", h)
        grain(l, "wuq")
        for h in range(HEADS):
            add("V", l, "mqrope", h)
        add("V", l, "krrope")
        for h in range(HEADS):
            add("A", l, "mk", h)
        for part in range(2):
            add("A", l, "mv", part)
        grain(l, "wukv")
        self.attention(l, "mla")
        self.add_norm(l, "mla")
        for m in range(KT):
            add("V", l, "wout", m)
            grain(l, "wout", m, split=True)
        self.add_norm(l, "n2")
        j0 = 0
        for s, nj in enumerate(SETS):
            for j in range(j0, j0 + nj):
                add("A", l, "ffa", j)
                grain(l, "ffa", j, split=True)
                add("V", l, "ffg", j)
                grain(l, "ffg", j, split=True)
            j0 += nj
            for what, *i in output_schedule(l, s):
                if what == "mod":
                    self.modulation(l + 1, i[0])
                else:
                    add("V", l, "ffo", s, i[1])
                    grain(l, "ffo", s, i[1], split=True)

    def attention(self, l, kind):
        units = attention_units(l, kind)
        for u in units:
            self.unit[(l,) + u] = len(self.unit)
        for job, u in attention_steps(units):
            self.add("A", l, job, *u)



def hymba_block(nc, a, out):
    plan = Plan()
    n_units = len(plan.unit)
    with ExitStack() as ctx:
        def sb(name, *shape):
            return ctx.enter_context(nc.sbuf_tensor(name, [P, *shape], F32))

        def sem(name):
            return ctx.enter_context(nc.semaphore(name))

        work = sb("work", WORK)
        work_at = nc.sbuf_base - 4 * WORK
        x = sb("x_resid", KT, TOK)
        ring = sb("ring", RING, GRAN)
        ident = sb("ident", P)
        rot = sb("rot", P)
        rot_mla = sb("rot_mla", MLA_ROPE)
        ones = sb("ones", P)
        blk = sb("blk", P)
        cs = sb("cs", 2, LAT)
        zt_cs = sb("zt_cs", 2 * LAT)
        negt = sb("negt", 6)
        par = sb("par", DEPTH, N_PARAM)
        w_small = sb("w_small", DEPTH, 3 * HY_FFN)
        hb = sb("hb", TOK)
        g_final = sb("g_final", KT)
        mod = sb("mod", DEPTH, N_MOD, 2)
        gain = sb("gain", 2, KT, 2)
        sq = sb("sq", 2, TOK)
        std = sb("std", TOK)
        turned = sb("turned", LAT)
        eps = sb("eps", 1)
        lg = sb("lg", 6, 8)
        smax = sb("smax", n_units)
        nmax = sb("nmax", n_units)
        rsum = sb("rsum", n_units)
        rinv = sb("rinv", n_units)
        ps = ctx.enter_context(nc.psum_tensor("ps", [P, PAIRS, 1024], F32))

        def rounded(name, *shape):
            return nc.alloc_sbuf_tensor_at(f"{name}_r", [P, *shape], F32R, offset=work_at + 4 * AT[name])

        hh, hl = rounded("hh", KT, TOK), rounded("hl", KT, TOK)
        uh, ul = rounded("uh", 6, TOK), rounded("ul", 6, TOK)
        wsplit = rounded("wsplit", SPLITS, 2, GRAN)

        def view(name, *shape):
            n = int(np.prod(shape))
            v = work[:, AT[name]:AT[name] + n]
            if len(shape) == 2:
                v = v.rearrange("p (a b) -> p a b", a=shape[0])
            elif len(shape) == 3:
                v = v.rearrange("p (a b c) -> p a b c", a=shape[0], b=shape[1])
            return v

        retq, retk, retg = (view(n, 2, TOK) for n in ("retq", "retk", "retg"))
        gq, gk, cq, ckv, kr = view("gq", 2, TOK), view("gk", TOK), view("cq", 2, TOK), view("ckv", TOK), view("kr", TOK)
        vret, vgqa = view("vret", 6, GROUP), view("vgqa", 6, P)
        hy, y = view("hy", 6, TOK), view("yraw", KT, TOK)
        spec = {"lat": view("klat", 4, 2, HY_COLS), "ctx": view("kctx", 2, 2, HY_COLS)}
        vtok, yf = view("vtok", 4, GROUP), view("y", 8, GROUP)
        tmp0, tmp1 = view("t0", 2, GROUP), view("t1", 2, GROUP)
        absd, w4 = view("absd", 1024), view("w4", 1024)
        edec, filt = view("edec", 2, 1024), view("f", 2, 1024)
        sumabs, rn = view("sumabs", HY_COLS), view("rn", HY_COLS)
        fa, fb = view("fa", 4, HY_COLS), view("fb", 4, HY_COLS)
        ha, ht = view("ha", TOK), view("ht", TOK)
        mq, mk, vmla = view("mq", HEADS, TOK), view("mk", HEADS, TOK), view("vmla", 6, GROUP)
        prob, pt = view("prob", 3, TOK), view("pt", 2, TOK)
        rpt, dec, delta = view("rpt", 2, 6, LAT), view("dec", 2, 896 + 640), view("delta", 896)
        ut = view("ut", 2, TOK)
        cond, unused = view("cond", 2, D), view("unused", D)
        cs_mla = zt_cs[:, :].rearrange("p (a b) -> p a b", a=2)
        inputs = {f"{n}{i}": t[:, i] for n, t in (("cq", cq), ("gq", gq), ("retq", retq), ("retk", retk), ("retg", retg))
                  for i in range(2)}
        inputs.update(ckv=ckv, kr=kr, gk=gk, vret0=hy[:, 3], vret1=hy[:, 4], vgqa=hy[:, 5])
        by_token = {"vret0": vret[:, :, 0:P], "vret1": vret[:, :, P:GROUP], "vgqa": vgqa}
        inputs.update({f"hy{i}": hy[:, i] for i in range(6)})

        def param(layer, name, i=0):
            at = PARAM[name][0] + i
            return par[:, layer, at:at + 1]

        def win_width(l, name):
            return TOK if name in ALL_TOKENS else width(l)

        x_loaded, cond_loaded, const_loaded = sem("x_loaded"), sem("cond_loaded"), sem("const_loaded")
        filter_loaded, delta_loaded = sem("filter_loaded"), sem("delta_loaded")
        slot_loaded = [sem(f"slot{i}_loaded") for i in range(RING)]
        out_stored = sem("out_stored")
        job_done = sem("job_done")
        act_drained, dve_drained = sem("act_drained"), sem("dve_drained")
        drained = {"A": act_drained, "V": dve_drained}
        high_done, split_done = sem("high_done"), sem("split_done")
        ones_set = sem("ones_set")
        cond_ready, mod_done = sem("cond_ready"), sem("mod_done")
        angle_ready, sin_ready = sem("angle_ready"), sem("sin_ready")
        decay_ready, filt_ready, ab_ready = sem("decay_ready"), sem("filt_ready"), sem("ab_ready")
        abs_ready, sumabs_ready = sem("abs_ready"), sem("sumabs_ready")
        abs_part, abs_summed = sem("abs_part"), sem("abs_summed")
        squares_ready, squares_used = sem("squares_ready"), sem("squares_used")
        norm_applied = sem("norm_applied")
        h_scaled, h_rounded, h_ready = sem("h_scaled"), sem("h_rounded"), sem("h_ready")
        conv_part = sem("conv_part")
        spectrum_ready = sem("spectrum_ready")
        kpe_ready, kpe_copied = sem("kpe_ready"), sem("kpe_copied")
        nmax_ready, prob_ready = sem("nmax_ready"), sem("prob_ready")
        log_part, log_ready = sem("log_part"), sem("log_ready")
        dec_arg, dec_exp = sem("dec_arg"), sem("dec_exp")
        u_ready = sem("u_ready")
        dve_chain, act_chain = sem("dve_chain"), sem("act_chain")

        def pair(n):
            return ps[:, n % PAIRS]

        def wait_job(eng, *key):
            eng.wait_ge(job_done, plan.job[key] + 1)

        def wait_drained(eng, *key):
            n = plan.job[key]
            who = plan.jobs[n]
            eng.wait_ge(drained[who], plan.before[n][who] + 1)

        def slot(n):
            return ring[:, n % RING]

        def grid(ap, n):
            return ap.rearrange("p (k c) -> p k c", k=n)

        def columns(key):
            return SETS[key[2]] * P if key[1] == "ffo" else GRAN

        def before_norm(l, name):
            idx = plan.norm[l, name][0]
            return next((k for k in plan.norm if plan.norm[k][0] == idx - 1), None)

        SCALED = {"n1": 0, "y": KT, "n2": 2 * KT}
        split_keys = {n: k for k, n in plan.split.items()}

        block = ctx.enter_context(nc.Block())

        @block.sync
        def _(sp):
            def source(key):
                l, name = key[0], key[1]
                if name == "F":
                    return a["dft_lat"][key[3]] if key[2] == "lat" else a["dft_ctx"][0]
                if name == "G":
                    return a["dft_lat"][4 + key[3]] if key[2] == "lat" else a["dft_ctx"][1]
                if name in ("ffa", "ffg"):
                    return a["w_ffn_in"][l, 2 * key[2] + (name == "ffg")]
                if name == "ffo":
                    return a["w_ffn_out"][l, key[2], key[3], :, 0:columns(key)]
                if name in ("wuq", "wukv"):
                    return a[name][l]
                return a[{"mod": "w_mod", "win": "w_in", "wout": "w_out"}[name]][l, key[2]]

            def load(n):
                if n >= RING:
                    _, how, last = plan.granules[n - RING]
                    sp.wait_ge({"split": split_done, "job": job_done, "mod": mod_done}[how], last + 1)
                src = source(plan.granules[n][0])
                sp.dma_start(slot(n)[:, 0:src.shape[1]], src).then_inc(slot_loaded[n % RING], 16)

            n = 0
            for l in range(DEPTH):
                j0 = 0
                for nj in SETS:
                    first = plan.granule[l, "ffa", j0]
                    while n < first + RING:
                        load(n)
                        n += 1
                    s0 = plan.split[l, "ffa", j0]
                    with sp.Fori(0, nj // 2 - 1) as i:
                        for t in range(RING):
                            sp.wait_ge(split_done, s0 + t + 1 + RING * i)
                            sp.dma_start(slot(first + t), a["w_ffn_in"][l, 2 * j0 + RING + t + RING * i])\
                              .then_inc(slot_loaded[(first + t) % RING], 16)
                    n = first + 2 * nj
                    j0 += nj
            while n < len(plan.granules):
                load(n)
                n += 1
            sp.wait_ge(norm_applied, plan.norm[DEPTH, "final"][0] + 1)
            sp.dma_start(out, y[:, :, 0:LAT]).then_inc(out_stored, 16)
            sp.wait_ge(out_stored, 16)

        @block.tensor
        def _(pe):
            def begin(*key):
                n = plan.job[key]
                if n >= PAIRS:
                    who = plan.jobs[n - PAIRS]
                    pe.wait_ge(drained[who], plan.before[n - PAIRS][who] + 1)
                return pair(n)

            def arrived(*key):
                n = plan.granule[key]
                pe.wait_ge(slot_loaded[n % RING], 16 * (n // RING + 1))
                return slot(n)

            def halves(*key):
                s = plan.split[key]
                pe.wait_ge(split_done, s + 1)
                return (grid(wsplit[:, s % SPLITS, part, 0:columns(key)], columns(key) // P) for part in range(2))

            def segments(w):
                return [(c, min(c + LAT, w)) for c in range(0, w, LAT)]

            def products(w, d, k):
                wh, wl = w
                dh, dl = d
                return ((wh[:, k], dh), (wh[:, k], dl), (wl[:, k], dh))

            def norm(l, name, matrix, w):
                _, done, nt = plan.norm[l, name]
                dst = begin(l, "norm", name)
                for t in range(nt):
                    pe.wait_ge(squares_ready, done + t + 1)
                    for c0, c1 in segments(w):
                        mm = pe.matmul(dst[:, c0:c1], matrix[:, :], sq[:, (done + t) % 2, c0:c1],
                                       start=(t == 0), stop=(t == nt - 1))
                    if t < nt - 1:
                        mm.then_inc(squares_used, 1)
                mm.then_inc(job_done, 1)

            def project(dst, w, w_cols, width_, data=None, n_tiles=KT, first=None, lo=0):
                dh, dl = data or (hh, hl)
                for k in range(n_tiles):
                    if first is not None:
                        pe.wait_ge(h_ready, first + k + 1)
                    for c0, c1 in segments(width_):
                        three = ((w[0], dh), (w[0], dl), (w[1], dh))
                        for i, (wp, dp) in enumerate(three):
                            mm = pe.matmul(dst[0:w_cols, c0:c1], wp[:, k, 0:w_cols], dp[:, k, c0:c1],
                                           start=(k == 0 and i == 0), stop=(k == n_tiles - 1 and i == 2))
                return mm

            def filter_layer(l, k):
                dst = begin(l, "mlp", k)
                if k:
                    pe.wait_ge(sin_ready, 3 * l + k)
                for c0, c1 in segments(width(l)):
                    rows = HY_FFN if k else HY_EMB
                    src = hb if k else zt_cs
                    mm = pe.matmul(dst[0:HY_FFN, c0:c1], w_small[0:rows, l, k * HY_FFN:(k + 1) * HY_FFN],
                                   src[0:rows, c0:c1], start=True, stop=True)
                mm.then_inc(job_done, 1)

            def values(dst, v, weights, tiles, base, n):
                for j, kt in enumerate(tiles):
                    mm = pe.matmul(dst[base:base + HD, 0:n], v(kt), weights[:, j], start=(j == 0), stop=(j == len(tiles) - 1))
                mm.then_inc(job_done, 1)

            def attention(l, kind):
                for job, un in attention_steps(attention_units(l, kind)):
                    _, net, hd, t = un
                    n = plan.unit[(l,) + un]
                    dst = begin(l, job, *un)
                    nk = 6 if net == "lat" else 2
                    if job == "s":
                        c = NET_AT[net] + P * t
                        if kind == "mla":
                            q, keys = mq[0:MLA_D, hd, c:c + P], mk[0:MLA_D, hd]
                        else:
                            kv, r = hd // 2, hd % 2
                            q, keys = gq[HD * kv:HD * kv + HD, r, c:c + P], gk[HD * kv:HD * kv + HD]
                        if net == "lat":
                            pe.matmul(dst[:, 0:LAT], q, keys[:, 0:LAT], start=True, stop=True)
                            pe.matmul(dst[:, LAT:TOK], q, keys[:, LAT:TOK], start=True, stop=True).then_inc(job_done, 1)
                        else:
                            pe.matmul(dst[:, 0:CTX], q, keys[:, LAT:TOK], start=True, stop=True).then_inc(job_done, 1)
                    elif job == "t":
                        pe.wait_ge(prob_ready, n + 1)
                        for j in range(nk):
                            mm = pe.transpose(dst[:, j * P:(j + 1) * P], prob[:, n % 3, j * P:(j + 1) * P], ident[:, :])
                        mm.then_inc(job_done, 1)
                    else:
                        wait_drained(pe, l, "t", *un)
                        col = HD * hd if kind == "mla" else HD * (hd // 2)
                        vt = vmla if kind == "mla" else vgqa
                        values(dst, lambda kt: vt[:, kt, col:col + HD], grid(pt[:, n % 2, 0:nk * P], nk),
                               range(6) if net == "lat" else (4, 5), HD * (hd % 2), P)

            pe.wait_ge(ones_set, 2)
            for l in range(DEPTH):
                W = width(l)
                norm(l, "n1", ones, TOK)
                if l == 0:
                    pe.wait_ge(const_loaded, 16 * N_CONST)
                for what, i in input_schedule(l):
                    if what == "win":
                        name = WIN[i]
                        w = tuple(halves(l, "win", i))
                        dst = begin(l, "win", i)
                        project(dst, w, 96 if name == "kr" else P, win_width(l, name),
                                first=3 * KT * l if i == 0 else None).then_inc(job_done, 1)
                    elif what == "vturn":
                        dst = begin(l, "vturn", i)
                        wait_drained(pe, l, "win", WIN.index(VALUES[i]))
                        for t in range(TOK // P):
                            mm = pe.transpose(dst[:, t * P:(t + 1) * P], inputs[VALUES[i]][:, t * P:(t + 1) * P], ident[:, :])
                        mm.then_inc(job_done, 1)
                    elif what == "mlp":
                        filter_layer(l, i)
                    elif what == "norm":
                        norm(l, i, ones if i in ("cq", "ckv") else blk, win_width(l, i))
                    elif what == "rope":
                        dst = begin(l, "rope", i)
                        if i in ("gq0", "gq1", "gk"):
                            pe.wait_ge(norm_applied, plan.norm[l, i][0] + 1)
                        else:
                            wait_drained(pe, l, "win", WIN.index(i))
                        pe.matmul(dst[:, 0:LAT], rot[:, :], inputs[i][:, 0:LAT], start=True, stop=True).then_inc(job_done, 1)

                pe.wait_ge(sin_ready, 3 * l + 3)
                pe.wait_ge(filter_loaded, 32 * (l + 1))
                for ni, net in enumerate(nets(l)):
                    n = NET_LEN[net]
                    nt = n // P
                    for t in range(nt):
                        dst = begin(l, "filt", net, t)
                        c = NET_AT[net] + P * t
                        for half in range(2):
                            mm = pe.matmul(dst[:, half * 512:half * 512 + 512], hb[0:HY_FFN, c:c + P],
                                           w4[0:HY_FFN, half * 512:half * 512 + 512], start=True, stop=True)
                        mm.then_inc(job_done, 1)
                    dst = begin(l, "l1", net)
                    pe.wait_ge(sumabs_ready, 2 * l + ni + 1)
                    pe.matmul(dst[:, 0:HY_COLS], ones[:, :], sumabs, start=True, stop=True).then_inc(job_done, 1)
                    if net == "lat":
                        f = [arrived(l, "F", net, t, "spec") for t in range(nt)]
                    else:
                        fc = grid(arrived(l, "F", net, 0, "spec"), 2)
                        f = [fc[:, t] for t in range(nt)]
                    pe.wait_ge(ab_ready, 6 * l + (4 if ni == 0 else 6))
                    for i in range(nt):
                        dst = begin(l, "spec", net, i)
                        for part, src in ((0, fa), (1, fb)):
                            for t in range(nt):
                                mm = pe.matmul(dst[:, part * 512:part * 512 + 512],
                                               f[t][:, part * n + i * P:part * n + i * P + P], src[:, t],
                                               start=(t == 0), stop=(t == nt - 1))
                        mm.then_inc(job_done, 1)
                    dst = begin(l, "nyq", net)
                    for t in range(nt):
                        mm = pe.matmul(dst[0:1, 0:HY_COLS], f[t][:, n:n + 1], fa[:, t], start=(t == 0), stop=(t == nt - 1))
                    mm.then_inc(job_done, 1)

                for net in nets(l):
                    n, c = NET_LEN[net], NET_AT[net]
                    nt = n // P
                    for o in range(2):
                        dst = begin(l, "turn", net, o)
                        if o:
                            wait_drained(pe, l, "inv", net, 0)
                        for t in range(nt):
                            for ch in range(2):
                                mm = pe.transpose(dst[:, t * GROUP + ch * P:t * GROUP + ch * P + P],
                                                  hy[:, ch, c + t * P:c + t * P + P], ident[:, :])
                        mm.then_inc(job_done, 1)
                        if net == "lat":
                            f = [arrived(l, "F", net, t, o) for t in range(nt)]
                        else:
                            fc = grid(arrived(l, "F", net, 0, o), 2)
                            f = [fc[:, t] for t in range(nt)]
                        wait_drained(pe, l, "turn", net, o)
                        for i in range(nt // 2):
                            dst = begin(l, "fwd", net, o, i)
                            for part in range(2):
                                for q in range(2):
                                    at = part * n + (2 * i + q) * P
                                    for t in range(nt):
                                        mm = pe.matmul(dst[:, part * 512 + q * GROUP:part * 512 + (q + 1) * GROUP],
                                                       f[t][:, at:at + P], vtok[:, t], start=(t == 0), stop=(t == nt - 1))
                            mm.then_inc(job_done, 1)
                        dst = begin(l, "inv", net, o)
                        pe.wait_ge(spectrum_ready, 4 * l + 2 * nets(l).index(net) + o + 1)
                        for fi in range(2 * nt):
                            if net == "lat":
                                if fi % 2 == 0:
                                    g = grid(arrived(l, "G", net, fi // 2, o), 2)
                                gt = g[:, fi % 2]
                            else:
                                if fi == 0:
                                    g = grid(arrived(l, "G", net, 0, o), 4)
                                gt = g[:, fi]
                            for ch in range(2):
                                mm = pe.matmul(dst[:, ch * 512:ch * 512 + n], yf[:, fi, ch * P:ch * P + P], gt,
                                               start=(fi == 0), stop=(fi == 2 * nt - 1))
                        mm.then_inc(job_done, 1)

                units = retention_units(l)
                for i, un in enumerate(units + [None]):
                    if un:
                        net, hd = un
                        base, c, n = HD * (hd % 2), NET_AT[net], NET_LEN[net]
                        tiles = list(range(6)) if net == "lat" else [4, 5]
                        for part in range(len(tiles) // 2):
                            dst = begin(l, "rs", *un, part)
                            for q in range(2):
                                kt = tiles[2 * part + q]
                                mm = pe.matmul(dst[:, q * 512:q * 512 + n],
                                               retk[base:base + HD, hd // 2, kt * P:(kt + 1) * P],
                                               retq[base:base + HD, hd // 2, c:c + n], start=True, stop=True)
                            mm.then_inc(job_done, 1)
                    if i:
                        net, hd = units[i - 1]
                        n = NET_LEN[net]
                        tiles = range(6) if net == "lat" else (4, 5)
                        dst = begin(l, "rpv", net, hd)
                        wait_drained(pe, l, "rs", net, hd, len(tiles) // 2 - 1)
                        values(dst, lambda kt: vret[:, kt, HD * hd:HD * hd + HD], rpt[:, (i - 1) % 2, :, 0:n],
                               tiles, HD * (hd % 2), n)
                norm(l, "ret0", blk, W)
                norm(l, "ret1", blk, W)
                norm(l, "hy", ones, W)
                attention(l, "gqa")
                norm(l, "ret", ones, W)
                norm(l, "gqa", ones, W)

                wuq = grid(arrived(l, "wuq")[:, 0:2 * HEADS * MLA_D], 2)
                for hd in range(HEADS):
                    dst = begin(l, "mq", hd)
                    for t in range(2):
                        for c0, c1 in segments(W):
                            mm = pe.matmul(dst[0:MLA_D, c0:c1], wuq[:, t, hd * MLA_D:(hd + 1) * MLA_D],
                                           cq[:, t, c0:c1], start=(t == 0), stop=(t == 1))
                    mm.then_inc(job_done, 1)
                for hd in range(HEADS):
                    dst = begin(l, "mqrope", hd)
                    wait_drained(pe, l, "mq", hd)
                    pe.matmul(dst[64:96, 0:LAT], rot_mla[64:96, :], mq[64:96, hd, 0:LAT], start=True, stop=True)\
                      .then_inc(job_done, 1)
                dst = begin(l, "krrope")
                pe.matmul(dst[64:96, 0:LAT], rot_mla[64:96, :], kr[64:96, 0:LAT], start=True, stop=True)\
                  .then_inc(job_done, 1)
                wukv = arrived(l, "wukv")
                for hd in range(HEADS):
                    dst = begin(l, "mk", hd)
                    for c0, c1 in segments(TOK):
                        mm = pe.matmul(dst[0:HD, c0:c1], wukv[:, hd * HD:hd * HD + HD], ckv[:, c0:c1], start=True, stop=True)
                    mm.then_inc(job_done, 1)
                for part, tiles in enumerate((range(0, 4), range(4, 6))):
                    dst = begin(l, "mv", part)
                    for i, t in enumerate(tiles):
                        mm = pe.matmul(dst[:, i * GROUP:(i + 1) * GROUP], ckv[:, t * P:(t + 1) * P],
                                       wukv[:, GROUP:2 * GROUP], start=True, stop=True)
                    mm.then_inc(job_done, 1)
                pe.wait_ge(kpe_copied, l + 1)
                wait_drained(pe, l, "mk", HEADS - 1)
                wait_drained(pe, l, "mqrope", HEADS - 1)
                attention(l, "mla")
                norm(l, "mla", ones, W)

                pe.wait_ge(h_ready, 3 * KT * l + 2 * KT)
                for m in range(KT):
                    w = tuple(halves(l, "wout", m))
                    project(begin(l, "wout", m), w, P, W).then_inc(job_done, 1)
                norm(l, "n2", ones, W)
                pe.wait_ge(h_ready, 3 * KT * (l + 1))
                j0 = 0
                for s, nj in enumerate(SETS):
                    first, s0 = plan.job[l, "ffa", j0], plan.split[l, "ffa", j0]
                    count = plan.before[first]
                    pe.wait_ge(act_drained, count["A"])
                    pe.wait_ge(dve_drained, count["V"])
                    with pe.Fori(0, nj // 2) as i:
                        for t in range(PAIRS):
                            who = "AV"[t % 2]
                            pe.wait_ge(drained[who], count[who] - 1 + t // 2 + 2 * i)
                            pe.wait_ge(split_done, s0 + t + 1 + PAIRS * i)
                            w = tuple(grid(wsplit[:, (s0 + t) % SPLITS, part], KT) for part in range(2))
                            project(pair(first + t), w, P, W).then_inc(job_done, 1)
                    j0 += nj
                    pe.wait_ge(u_ready, l * NF + j0)
                    for what, *i in output_schedule(l, s):
                        if what == "ffo":
                            w = tuple(halves(l, "ffo", s, i[1]))
                            project(begin(l, "ffo", s, i[1]), w, P, W, data=(uh, ul), n_tiles=nj).then_inc(job_done, 1)
            norm(DEPTH, "final", ones, LAT)

        @block.scalar
        def _(act):
            def drain(*key):
                wait_job(act, *key)
                return pair(plan.job[key])

            links = [0]

            def link(ins):
                links[0] += 1
                ins.then_inc(act_chain, 1)
                act.wait_ge(act_chain, links[0])

            def round_high(s):
                key = split_keys[s]
                n = plan.granule[key]
                act.wait_ge(slot_loaded[n % RING], 16 * (n // RING + 1))
                if s >= SPLITS:
                    act.wait_ge(job_done, plan.splits[s - SPLITS] + 1)
                w = columns(key)
                act.activation(wsplit[:, s % SPLITS, 0, 0:w], slot(n)[:, 0:w], ACT.Copy).then_inc(high_done, 1)

            def norm(l, name, srcs, n, w, ready=None):
                idx, done, nt = plan.norm[l, name]
                prev = before_norm(l, name)
                if prev:
                    act.wait_ge(job_done, plan.job[prev[0], "norm", prev[1]] + 1)
                    act.wait_ge(norm_applied, idx)
                for t, src in enumerate(srcs):
                    if t >= 2:
                        act.wait_ge(squares_used, done - idx + t - 1)
                    if ready is not None:
                        ready(t)
                    act.activation(sq[:, (done + t) % 2, 0:w], src[:, 0:w], ACT.Square).then_inc(squares_ready, 1)
                p = drain(l, "norm", name)
                act.activation(std[:, 0:w], p[:, 0:w], ACT.Sqrt, bias=eps[:, :], scale=1.0 / n).then_inc(act_drained, 1)

            def high_parts(l, which, w):
                at = {"n1": 0, "n2": 3 * KT}[which]
                for k in range(KT):
                    n = 3 * KT * l + SCALED[which] + k
                    act.wait_ge(h_scaled, n + 1)
                    ins = act.activation(hh[:, k, 0:LAT], sq[:, k % 2, 0:LAT], ACT.Identity, bias=mod[:, l, at + k, 0:1])
                    if w > LAT:
                        ins = act.activation(hh[:, k, LAT:TOK], sq[:, k % 2, LAT:TOK], ACT.Identity, bias=mod[:, l, at + k, 1:2])
                    ins.then_inc(h_rounded, 1)

            def attention(l, kind, tile0, scale):
                for job, un in attention_steps(attention_units(l, kind)):
                    _, net, hd, t = un
                    n = plan.unit[(l,) + un]
                    p = drain(l, job, *un)
                    if job == "s":
                        wide = TOK if net == "lat" else CTX
                        act.wait_ge(nmax_ready, n + 1)
                        if n >= 3:
                            prev = next(k for k in plan.unit if plan.unit[k] == n - 3)
                            wait_job(act, prev[0], "t", *prev[1:])
                        act.activation(prob[:, n % 3, 0:wide], p[:, 0:wide], ACT.Exp, bias=nmax[:, n:n + 1],
                                       scale=scale, accum_out=rsum[:, n:n + 1]).then_inc(act_drained, 1)
                    elif job == "t":
                        wide = TOK if net == "lat" else CTX
                        act.activation(pt[:, n % 2, 0:wide], p[:, 0:wide], ACT.Copy).then_inc(act_drained, 1)
                    else:
                        base, c = HD * (hd % 2), NET_AT[net] + P * t
                        act.activation(y[base:base + HD, tile0 + hd // 2, c:c + P], p[base:base + HD, 0:P],
                                       ACT.Copy).then_inc(act_drained, 1)

            act.dma_start(cond, a["cond"]).then_inc(cond_loaded, 16)
            act.dma_start(par[:, :, :], a["par"]).then_inc(cond_loaded, 16)
            act.dma_start(x[:, :, :], a["x"]).then_inc(x_loaded, 16)
            for dst, name in ((ident, "ident"), (rot, "rot"), (rot_mla, "rot_mla"), (blk, "blk"),
                              (cs, "cs"), (zt_cs, "zt_cs"), (negt, "negt"), (g_final, "g_final"), (w_small, "w_small")):
                act.dma_start(dst[tuple(slice(None) for _ in dst.shape)], a[name]).then_inc(const_loaded, 16)

            act.wait_ge(cond_loaded, 32)
            act.activation(cond, cond, ACT.Silu).then_inc(cond_ready, 1)
            act.wait_ge(x_loaded, 16)
            act.wait_ge(ones_set, 2)
            for l in range(DEPTH):
                W = width(l)
                norm(l, "n1", [x[:, k] for k in range(KT)], D, TOK,
                     ready=(lambda k: wait_drained(act, l - 1, "ffo", len(SETS) - 1, k)) if l else None)
                high_parts(l, "n1", TOK)
                if l == 0:
                    round_high(0)
                    round_high(1)
                at = PARAM["decay"][0]
                link(act.activation(lg[:, 1, :], par[:, l, at:at + 8], ACT.Abs))
                act.activation(lg[:, 2, :], lg[:, 1, :], ACT.Exp, scale=-1.0).then_inc(log_part, 1)
                act.wait_ge(log_ready, 2 * l + 1)
                act.activation(lg[:, 4, :], lg[:, 3, :], ACT.Ln).then_inc(log_part, 1)
                for what, i in input_schedule(l):
                    if what == "win":
                        name = WIN[i]
                        p = drain(l, "win", i)
                        w = win_width(l, name)
                        dst = inputs[name]
                        if name[:2] == "hy":
                            g = int(name[2])
                            act.activation(dst[:, 0:W], p[:, 0:W], ACT.Identity, bias=param(l, "conv_b", g),
                                           scale=param(l, "conv_w", 6 + g)).then_inc(conv_part, 1)
                        else:
                            rows = slice(64, 96) if name == "kr" else slice(0, P)
                            act.activation(dst[rows, 0:w], p[rows, 0:w], ACT.Silu if name[:4] == "retg" else ACT.Copy,
                                           scale=RET_K_SCALE if name[:4] == "retk" else 1.0).then_inc(act_drained, 1)
                        if i + SPLITS < N_WIN:
                            round_high(plan.split[l, "win", i] + SPLITS)
                    elif what == "vturn":
                        p = drain(l, "vturn", i)
                        act.activation(by_token[VALUES[i]], p[:, 0:TOK].rearrange("p (t c) -> p t c", t=6), ACT.Copy)\
                           .then_inc(act_drained, 1)
                    elif what == "norm":
                        tiles = ("cq0", "cq1") if i == "cq" else (i,)
                        n = {"cq": GROUP, "ckv": P}.get(i, HD)
                        for name in tiles:
                            wait_drained(act, l, "win", WIN.index(name))
                        norm(l, i, [inputs[name] for name in tiles], n, win_width(l, i))
                    elif what == "mlp":
                        act.wait_ge(angle_ready, 3 * l + i + 1)
                        act.activation(hb[0:HY_FFN, 0:W], ht[0:HY_FFN, 0:W], ACT.Sin).then_inc(sin_ready, 1)
                wait_job(act, l, "win", N_WIN - 1)
                act.dma_start(w4[0:HY_FFN], a["w4"][l]).then_inc(filter_loaded, 16)
                act.dma_start(absd, a["absd"]).then_inc(filter_loaded, 16)
                act.wait_ge(filter_loaded, 32 * (l + 1))
                s = 6 * l
                tiles = [(net, t) for net in nets(l) for t in range(NET_LEN[net] // P)]

                def decay(i):
                    net, t = tiles[i]
                    if i >= 2:
                        act.wait_ge(filt_ready, s + i - 1)
                    tt = t + (4 if net == "ctx" else 0)
                    act.activation(edec[:, i % 2], absd, ACT.Exp, scale=negt[:, tt:tt + 1]).then_inc(decay_ready, 1)

                decay(0)
                for i in range(len(tiles)):
                    if i + 1 < len(tiles):
                        decay(i + 1)
                    act.wait_ge(ab_ready, s + i + 1)
                    act.activation(filt[:, i % 2], filt[:, i % 2], ACT.Abs).then_inc(abs_ready, 1)
                for net in nets(l):
                    nt = NET_LEN[net] // P
                    for o in range(2):
                        p = drain(l, "turn", net, o)
                        act.activation(vtok[:, 0:nt], p[:, 0:nt * GROUP].rearrange("p (t c) -> p t c", t=nt), ACT.Copy)\
                           .then_inc(act_drained, 1)
                wait_drained(act, l, "inv", nets(l)[-1], 1)
                act.dma_start(delta, a["delta"]).then_inc(delta_loaded, 16)
                act.wait_ge(delta_loaded, 16 * (l + 1))
                units = retention_units(l)

                def table(hd):
                    act.wait_ge(dec_arg, HEADS * l + hd + 1)
                    link(act.activation(dec[:, hd % 2, 0:896], dec[:, hd % 2, 0:896], ACT.Exp))
                    act.activation(dec[:, hd % 2, 896:1536], delta[:, 256:896], ACT.Exp, bias=lg[:, 5, hd:hd + 1],
                                   scale=lg[:, 0, hd:hd + 1])
                    act.activation(sq[:, 0, 0:640], delta[:, 256:896], ACT.Exp, bias=lg[:, 5, 4 + hd:5 + hd],
                                   scale=lg[:, 1, 4 + hd:5 + hd]).then_inc(dec_exp, 1)

                table(0)
                for net, hd in units:
                    if net == "lat" and hd + 1 < HEADS:
                        table(hd + 1)
                    base, c, m = HD * (hd % 2), NET_AT[net], NET_LEN[net]
                    p = drain(l, "rpv", net, hd)
                    act.activation(y[base:base + HD, 4 + hd // 2, c:c + m], p[base:base + HD, 0:m], ACT.Copy)\
                       .then_inc(act_drained, 1)
                wait_drained(act, l, "rpv", *units[-1])
                norm(l, "ret0", [y[:, 4]], HD, W)
                norm(l, "ret1", [y[:, 5]], HD, W)
                norm(l, "hy", [y[:, 0], y[:, 1]], GROUP, W)
                attention(l, "gqa", 6, GQA_SCALE)
                wait_drained(act, l, "pv", *attention_units(l, "gqa")[-1])
                norm(l, "ret", [y[:, 4], y[:, 5]], GROUP, W)
                norm(l, "gqa", [y[:, 6], y[:, 7]], GROUP, W)
                for hd in range(HEADS):
                    p = drain(l, "mq", hd)
                    act.activation(mq[0:MLA_D, hd, 0:W], p[0:MLA_D, 0:W], ACT.Copy).then_inc(act_drained, 1)
                for hd in range(HEADS):
                    p = drain(l, "mk", hd)
                    act.activation(mk[0:HD, hd, :], p[0:HD, 0:TOK], ACT.Copy).then_inc(act_drained, 1)
                for part, (t0, t1) in enumerate(((0, 4), (4, 6))):
                    p = drain(l, "mv", part)
                    act.activation(vmla[:, t0:t1], p[:, 0:(t1 - t0) * GROUP].rearrange("p (t c) -> p t c", c=GROUP), ACT.Copy)\
                       .then_inc(act_drained, 1)
                attention(l, "mla", 2, MLA_SCALE)
                wait_drained(act, l, "pv", *attention_units(l, "mla")[-1])
                for t in (0, 1, 4, 5, 6, 7):
                    n = 3 * KT * l + KT + (0, 1, 4, 5, 6, 7).index(t)
                    act.wait_ge(h_scaled, n + 1)
                    act.activation(hh[:, t, 0:W], y[:, t, 0:W], ACT.Copy).then_inc(h_rounded, 1)
                norm(l, "mla", [y[:, 2], y[:, 3]], GROUP, W)
                for t in (2, 3):
                    act.wait_ge(h_scaled, 3 * KT * l + KT + 6 + t - 1)
                    act.activation(hh[:, t, 0:W], y[:, t, 0:W], ACT.Copy).then_inc(h_rounded, 1)
                act.wait_ge(h_ready, 3 * KT * l + 2 * KT)
                s = plan.split[l, "wout", 0]
                round_high(s)
                round_high(s + 1)
                if l < DEPTH - 1:
                    act.dma_start(cond, a["cond"]).then_inc(cond_loaded, 16)
                    act.wait_ge(cond_loaded, 16 * (l + 3))
                    act.activation(cond, cond, ACT.Silu).then_inc(cond_ready, 1)
                for m in range(KT):
                    wait_job(act, l, "wout", m)
                    round_high(s + m + SPLITS)
                norm(l, "n2", [x[:, k] for k in range(KT)], D, W,
                     ready=lambda k: wait_drained(act, l, "wout", k))
                high_parts(l, "n2", W)
                j0 = 0
                for st, nj in enumerate(SETS):
                    first, s0 = plan.job[l, "ffa", j0], plan.split[l, "ffa", j0]
                    g0 = plan.granule[l, "ffa", j0]
                    used = plan.before[first]["V"]

                    def gates(i, last):
                        for t in range(PAIRS):
                            act.wait_ge(job_done, first + t + 1 + PAIRS * i)
                            if t % 2 == 0:
                                act.wait_ge(dve_drained, used + t // 2 - 1 + 2 * i)
                                act.activation(sq[:, t // 2, 0:W], pair(first + t)[:, 0:W], ACT.Silu).then_inc(act_drained, 1)
                            if last and t >= PAIRS - SPLITS:
                                round_high(plan.split[l, "ffo", st, t - (PAIRS - SPLITS)])
                            else:
                                g = g0 + t + SPLITS
                                act.wait_ge(slot_loaded[g % RING], 16 * (g // RING + 1) + 16 * i)
                                act.activation(wsplit[:, (s0 + t) % SPLITS, 0], slot(g), ACT.Copy).then_inc(high_done, 1)

                    with act.Fori(0, nj // 2 - 1) as i:
                        gates(i, False)
                    gates(nj // 2 - 1, True)
                    j0 += nj
                    for what, *i in output_schedule(l, st):
                        if what == "ffo":
                            wait_job(act, l, "ffo", st, i[1])
                            nxt = plan.split[l, "ffo", st, i[1]] + SPLITS
                            if nxt < len(plan.splits):
                                round_high(nxt)
            norm(DEPTH, "final", [x[:, k] for k in range(KT)], D, LAT,
                 ready=lambda k: wait_drained(act, DEPTH - 1, "ffo", len(SETS) - 1, k))

        @block.gpsimd
        def _(pool):
            pool.memset(ones[:, :], 1.0).then_inc(ones_set, 1)
            pool.memset(eps[:, :], EPS).then_inc(ones_set, 1)
            parts = 0
            for l in range(DEPTH):
                s = 6 * l
                i = 0
                for ni, net in enumerate(nets(l)):
                    if ni:
                        wait_job(pool, l, "l1", nets(l)[0])
                    for t in range(NET_LEN[net] // P):
                        pool.wait_ge(abs_ready, s + 1)
                        f = filt[:, i % 2]
                        if t == 0:
                            pool.tensor_tensor(sumabs, f[:, 0:512], f[:, 512:1024], ALU.add).then_inc(abs_part, 1)
                            parts += 1
                        else:
                            for half in range(2):
                                pool.tensor_tensor(sumabs, sumabs, f[:, half * 512:half * 512 + 512], ALU.add).then_inc(abs_part, 1)
                                parts += 1
                                if not half:
                                    pool.wait_ge(abs_part, parts)
                        pool.wait_ge(abs_part, parts)
                        pool.engine_nop().then_inc(abs_summed, 1)
                        i += 1
                        s += 1
                    pool.engine_nop().then_inc(sumabs_ready, 1)
                pool.wait_ge(kpe_ready, l + 1)
                for hd in range(HEADS):
                    ins = pool.tensor_copy(mk[64:96, hd, :], kr[64:96, :])
                ins.then_inc(kpe_copied, 1)

        @block.vector
        def _(dve):
            def drain(*key):
                wait_job(dve, *key)
                return pair(plan.job[key])

            links = [0]

            def link(ins, turns=0):
                links[0] += 1
                ins.then_inc(dve_chain, 1)
                dve.wait_ge(dve_chain, links[0] + turns)

            def signal(what):
                dve.engine_nop().then_inc(what, 1)

            def split_low(s):
                key = split_keys[s]
                n, w = plan.granule[key], columns(key)
                dve.wait_ge(high_done, s + 1)
                part = wsplit[:, s % SPLITS]
                dve.tensor_tensor(part[:, 1, 0:w], slot(n)[:, 0:w], part[:, 0, 0:w].bitcast(F32), ALU.subtract)\
                   .then_inc(split_done, 1)

            def modulation(l, j):
                n, m = plan.granule[l, "mod", j], l * N_MOD + j
                dve.wait_ge(slot_loaded[n % RING], 16 * (n // RING + 1))
                if m:
                    dve.wait_ge(mod_done, m)
                for c, products in ((0, unused), (1, slot(n))):
                    ins = dve.tensor_tensor_reduce(products, slot(n), cond[:, c], 1.0, param(l, "b_mod", j), ALU.mult, ALU.add,
                                                   accum_out=mod[:, l, j, c:c + 1])
                ins.then_inc(mod_done, 1)

            def scales(l, name, w):
                n = plan.job[l, "norm", name]
                dve.wait_ge(act_drained, plan.before[n]["A"] + 1)
                link(dve.reciprocal(std[:,0:w],std[:,0:w]))

            def norm(l, name, tiles, gains, w, gate=None, into=None):
                scales(l, name, w)
                for t, g, dst in zip(tiles, gains, into or tiles):
                    ins = dve.scalar_tensor_tensor(dst[:, 0:w], t[:, 0:w], g, std[:, 0:w], ALU.mult, ALU.mult)
                    if gate is not None:
                        link(ins)
                        ins = dve.tensor_tensor(t[:, 0:w], t[:, 0:w], gate[:, 0:w], ALU.mult)
                ins.then_inc(norm_applied, 1)

            def group_norm(l, name, at, n, w):
                scales(l, name, w)
                for i in range(2):
                    dve.scalar_tensor_tensor(y[:, at + i, 0:w], y[:, at + i, 0:w], param(l, "g_out", at + i), std[:, 0:w],
                                             ALU.mult, ALU.mult).then_inc(h_scaled, 1)
                dve.wait_ge(h_scaled, 3 * KT * l + KT + n + 2)
                signal(norm_applied)

            def low_parts(l, which, w):
                scales(l, which, w)
                at = {"n1": 0, "n2": 3 * KT}[which]
                base = 3 * KT * l + SCALED[which]
                segs = [(0, 0, LAT), (1, LAT, TOK)][:1 + (w > LAT)]

                def low(k):
                    dve.wait_ge(h_rounded, base + k + 1)
                    for s, c0, c1 in segs:
                        ins = dve.scalar_tensor_tensor(hl[:, k, c0:c1], sq[:, k % 2, c0:c1], mod[:, l, at + k, s:s + 1],
                                                       hh[:, k, c0:c1].bitcast(F32), ALU.add, ALU.subtract)
                    ins.then_inc(h_ready, 1)

                for k in range(KT):
                    if k >= 2:
                        dve.wait_ge(h_ready, base + k - 1)
                    for s, c0, c1 in segs:
                        ins = dve.scalar_tensor_tensor(sq[:, k % 2, c0:c1], x[:, k, c0:c1],
                                                       gain[:, int(which == "n2"), k, s:s + 1], std[:, c0:c1],
                                                       ALU.mult, ALU.mult)
                    ins.then_inc(h_scaled, 1)
                    if k:
                        low(k - 1)
                low(KT - 1)
                dve.wait_ge(h_ready, base + KT)
                signal(norm_applied)

            def gains(l, which):
                name, at = (("g_attn", KT), ("g_ffn", 4 * KT))[which]
                g0 = PARAM[name][0]
                link(dve.scalar_tensor_tensor(gain[:, which], mod[:, l, at:at + KT, :], 1.0,
                                              par[:, l, g0:g0 + KT, None].to_broadcast([P, KT, 2]), ALU.add, ALU.mult))

            def attention(l, kind, scale):
                units = attention_units(l, kind)
                for i, un in enumerate(units + [None]):
                    if un:
                        n = plan.unit[(l,) + un]
                        wide = TOK if un[1] == "lat" else CTX
                        p = drain(l, "s", *un)
                        link(dve.reduce_max(smax[:, n:n + 1], p[:, 0:wide], AX))
                        dve.tensor_scalar(nmax[:, n:n + 1], smax[:, n:n + 1], -scale, None, ALU.mult).then_inc(nmax_ready, 1)
                    if i:
                        prev = units[i - 1]
                        n = plan.unit[(l,) + prev]
                        wide = TOK if prev[1] == "lat" else CTX
                        wait_drained(dve, l, "s", *prev)
                        link(dve.reciprocal(rinv[:, n:n + 1], rsum[:, n:n + 1]))
                        dve.tensor_scalar(prob[:, n % 3, 0:wide], prob[:, n % 3, 0:wide], rinv[:, n:n + 1], None, ALU.mult)\
                           .then_inc(prob_ready, 1)

            def residual(l, m, at, w, *key):
                p = drain(l, *key)
                for s, (c0, c1) in enumerate(((0, LAT), (LAT, TOK))[:1 + (w > LAT)]):
                    ins = dve.scalar_tensor_tensor(x[:, m, c0:c1], p[:, c0:c1], mod[:, l, at + m, s:s + 1], x[:, m, c0:c1],
                                                   ALU.mult, ALU.add)
                ins.then_inc(dve_drained, 1)

            def rotate(src, dst_ps, table, rows):
                dve.tensor_tensor(src[rows, 0:LAT], src[rows, 0:LAT], table[rows, 0, :], ALU.mult)
                link(dve.tensor_tensor(turned[rows, :], dst_ps[rows, 0:LAT], table[rows, 1, :], ALU.mult))
                link(dve.tensor_tensor(src[rows, 0:LAT], src[rows, 0:LAT], turned[rows, :], ALU.add))

            dve.wait_ge(cond_loaded, 32)
            dve.wait_ge(cond_ready, 1)
            for j in range(MOD_FIRST):
                modulation(0, j)
            dve.wait_ge(const_loaded, 16 * N_CONST)
            for l in range(DEPTH):
                W = width(l)
                dve.wait_ge(mod_done, l * N_MOD + (N_MOD if l else MOD_FIRST))
                gains(l, 0)
                low_parts(l, "n1", TOK)
                if l == 0:
                    split_low(0)
                    split_low(1)
                at = PARAM["decay"][0]
                dve.wait_ge(log_part, 2 * l + 1)
                dve.tensor_scalar(lg[:, 3, :], lg[:, 2, :], 1.0, None, ALU.add).then_inc(log_ready, 1)
                dve.wait_ge(log_part, 2 * l + 2)
                link(dve.tensor_scalar(lg[:, 0, :], par[:, l, at:at + 8], 0.0, None, ALU.min))
                link(dve.tensor_tensor(lg[:, 0, :], lg[:, 0, :], lg[:, 4, :], ALU.subtract))
                dve.tensor_scalar(lg[:, 1, :], lg[:, 0, :], -1.0, None, ALU.mult)
                dve.tensor_scalar(lg[:, 5, 0:4], lg[:, 0, 0:4], float(CTX), None, ALU.mult)
                link(dve.tensor_scalar(lg[:, 5, 4:8], lg[:, 0, 4:8], float(LAT), None, ALU.mult))
                signal(log_ready)
                for what, i in input_schedule(l):
                    if what == "win":
                        name = WIN[i]
                        if name[:2] == "hy":
                            g = int(name[2])
                            p = drain(l, "win", i)
                            dve.wait_ge(conv_part, 6 * l + g + 1)
                            for net in nets(l):
                                c0, c1 = NET_AT[net], NET_AT[net] + NET_LEN[net]
                                link(dve.scalar_tensor_tensor(hy[:, g, c0 + 1:c1], p[:, c0:c1 - 1], param(l, "conv_w", g),
                                                              hy[:, g, c0 + 1:c1], ALU.mult, ALU.add))
                                ins = dve.scalar_tensor_tensor(hy[:, g, c0:c1 - 1], p[:, c0 + 1:c1], param(l, "conv_w", 12 + g),
                                                               hy[:, g, c0:c1 - 1], ALU.mult, ALU.add)
                            ins.then_inc(dve_drained, 1)
                        if i + SPLITS < N_WIN:
                            split_low(plan.split[l, "win", i] + SPLITS)
                    elif what == "mod":
                        modulation(l, i)
                    elif what == "norm":
                        tiles, gs = {"cq": (("cq0", "cq1"), ("g_q", "g_q")), "ckv": (("ckv",), ("g_kv",)),
                                     "gk": (("gk",), ("g_gk",))}.get(i, ((i,), ("g_gq",)))
                        norm(l, i, [inputs[t] for t in tiles],
                             [param(l, g, n if i == "cq" else 0) for n, g in enumerate(gs)], win_width(l, i))
                    elif what == "rope":
                        rotate(inputs[i], drain(l, "rope", i), cs, slice(0, P))
                        signal(dve_drained)
                    elif what == "mlp":
                        p = drain(l, "mlp", i)
                        rows = slice(0, HY_FFN)
                        link(dve.tensor_scalar(ha[rows, 0:W], p[rows, 0:W], param(l, f"b{i + 1}")[rows], param(l, "freq")[rows],
                                               ALU.add, ALU.mult))
                        if i:
                            dve.wait_ge(sin_ready, 3 * l + i)
                        link(dve.tensor_scalar(ht[rows, 0:W], ha[rows, 0:W], INV_2PI, MAGIC, ALU.mult, ALU.add))
                        link(dve.tensor_scalar(ht[rows, 0:W], ht[rows, 0:W], MAGIC, None, ALU.subtract))
                        link(dve.scalar_tensor_tensor(ha[rows, 0:W], ht[rows, 0:W], -TWO_PI_HI, ha[rows, 0:W], ALU.mult, ALU.add))
                        link(dve.scalar_tensor_tensor(ht[rows, 0:W], ht[rows, 0:W], -TWO_PI_LO, ha[rows, 0:W], ALU.mult, ALU.add))
                        link(dve.tensor_scalar(ht[rows, 0:W], ht[rows, 0:W], PI_BELOW, -PI_BELOW, ALU.min, ALU.max))
                        signal(angle_ready)
                        signal(dve_drained)
                if l == 0:
                    dve.wait_ge(mod_done, N_MOD)
                wait_job(dve, l, "win", N_WIN - 1)
                i = 0
                for net in nets(l):
                    nt = NET_LEN[net] // P
                    for t in range(nt):
                        s = 6 * l + i
                        p = drain(l, "filt", net, t)
                        dve.wait_ge(decay_ready, s + 1)
                        if i >= 2:
                            dve.wait_ge(abs_summed, s - 1)
                        f = filt[:, i % 2]
                        link(dve.scalar_tensor_tensor(f, edec[:, i % 2], 0.05, p, ALU.add, ALU.mult))
                        if t == 0:
                            link(dve.memset(f[0:1, 512:1024], 0.0))
                        signal(filt_ready)
                        signal(dve_drained)
                        if t == 0 and net != "lat":
                            wait_job(dve, l, "nyq", "lat")
                        link(dve.tensor_tensor(fa[:, t], f[:, 0:512], f[:, 512:1024], ALU.add))
                        dve.tensor_tensor(fb[:, t], f[:, 0:512], f[:, 512:1024], ALU.subtract).then_inc(ab_ready, 1)
                        i += 1
                    p = drain(l, "l1", net)
                    link(dve.reciprocal(rn, p[:, 0:512]))
                    signal(dve_drained)
                    for q in range(nt):
                        p = drain(l, "spec", net, q)
                        link(dve.tensor_tensor(spec[net][:, q], p.rearrange("p (a b) -> p a b", a=2),
                                               rn[:, None, :].to_broadcast([P, 2, HY_COLS]), ALU.mult))
                        signal(dve_drained)
                    p = drain(l, "nyq", net)
                    link(dve.tensor_tensor(spec[net][0:1, 0, 1, :], p[0:1, 0:512], rn[0:1, :], ALU.mult))
                    signal(dve_drained)
                for net in nets(l):
                    n, c = NET_LEN[net], NET_AT[net]
                    nt = n // P
                    for o in range(2):
                        for i in range(nt // 2):
                            p = drain(l, "fwd", net, o, i)
                            ur, ui = (p[:, q * 512:q * 512 + 512].rearrange("p (a b) -> p a b", a=2) for q in range(2))
                            kre, kim = (spec[net][:, 2 * i:2 * i + 2, q, o * GROUP:(o + 1) * GROUP] for q in range(2))
                            yr, yi = yf[:, 2 * i:2 * i + 2], yf[:, nt + 2 * i:nt + 2 * i + 2]
                            dve.tensor_tensor(yr, ur, kre, ALU.mult)
                            dve.tensor_tensor(tmp0, ui, kim, ALU.mult)
                            dve.tensor_tensor(yi, ur, kim, ALU.mult)
                            link(dve.tensor_tensor(tmp1, ui, kre, ALU.mult))
                            dve.tensor_tensor(yr, yr, tmp0, ALU.subtract)
                            link(dve.tensor_tensor(yi, yi, tmp1, ALU.add))
                            if i == 0:
                                dve.tensor_tensor(yr[0:1, 0], ur[0:1, 0], kre[0:1, 0], ALU.mult)
                                link(dve.tensor_tensor(yi[0:1, 0], ui[0:1, 0], kim[0:1, 0], ALU.mult))
                            signal(dve_drained)
                        signal(spectrum_ready)
                        p = drain(l, "inv", net, o)
                        for ch in range(2):
                            v = hy[:, ch, c:c + n]
                            gate = hy[:, 2 + 2 * o + ch, c:c + n]
                            dst = y[:, ch, c:c + n] if o else v
                            link(dve.scalar_tensor_tensor(v, v, param(l, "hy_bias", 2 * o + ch), p[:, ch * 512:ch * 512 + n],
                                                          ALU.mult, ALU.add))
                            link(dve.tensor_tensor(dst, v, gate, ALU.mult))
                        signal(dve_drained)

                def arguments(hd):
                    t = dec[:, hd % 2]
                    link(dve.tensor_scalar(t[:, 0:896], delta, 0.0, lg[:, 0, hd:hd + 1], ALU.max, ALU.mult))
                    link(dve.tensor_scalar(sq[:, 1, 0:768], delta[:, 0:768], 0.0, lg[:, 1, 4 + hd:5 + hd], ALU.min, ALU.mult))
                    link(dve.tensor_tensor(t[:, 0:768], t[:, 0:768], sq[:, 1, 0:768], ALU.add))
                    signal(dec_arg)

                def finish(hd):
                    t = dec[:, hd % 2]
                    dve.wait_ge(dec_exp, HEADS * l + hd + 1)
                    link(dve.tensor_tensor(t[:, 384:512], t[:, 384:512], ident[:, :], ALU.add))
                    link(dve.tensor_tensor(t[:, 896:1536], t[:, 896:1536], sq[:, 0, 0:640], ALU.add))

                dve.wait_ge(delta_loaded, 16 * (l + 1))
                arguments(0)
                units = retention_units(l)
                for n, (net, hd) in enumerate(units):
                    if net == "lat":
                        finish(hd)
                        if hd + 1 < HEADS:
                            if hd:
                                wait_drained(dve, l, "rs", nets(l)[-1], hd - 1, 2 if W == LAT else 0)
                            arguments(hd + 1)
                    m = NET_LEN[net]
                    tiles = list(range(6)) if net == "lat" else [4, 5]
                    for part in range(len(tiles) // 2):
                        p = drain(l, "rs", net, hd, part)
                        for q in range(2):
                            kt = tiles[2 * part + q]
                            if net == "lat" and kt >= 4:
                                at = 896 + 384 - 256 - P * (kt - 4)
                            elif net == "lat":
                                at = 384 - P * kt
                            else:
                                at = 384 - P * (kt - 4)
                            ins = dve.tensor_tensor(rpt[:, n % 2, 2 * part + q, 0:m], p[:, q * 512:q * 512 + m],
                                                    dec[:, hd % 2, at:at + m], ALU.mult)
                        ins.then_inc(dve_drained, 1)
                norm(l, "ret0", [y[:, 4]], [param(l, "g_ret", 0)], W, gate=retg[:, 0])
                norm(l, "ret1", [y[:, 5]], [param(l, "g_ret", 1)], W, gate=retg[:, 1])
                group_norm(l, "hy", 0, 0, W)
                attention(l, "gqa", GQA_SCALE)
                group_norm(l, "ret", 4, 2, W)
                group_norm(l, "gqa", 6, 4, W)
                rows = slice(64, 96)
                for hd in range(HEADS):
                    rotate(mq[:, hd], drain(l, "mqrope", hd), cs_mla, rows)
                    signal(dve_drained)
                rotate(kr, drain(l, "krrope"), cs_mla, rows)
                signal(kpe_ready)
                signal(dve_drained)
                attention(l, "mla", MLA_SCALE)
                base = 3 * KT * l + KT
                for n, t in enumerate((0, 1, 4, 5, 6, 7, 2, 3)):
                    if t == 2:
                        group_norm(l, "mla", 2, 6, W)
                    dve.wait_ge(h_rounded, base + n + 1)
                    dve.tensor_tensor(hl[:, t, 0:W], y[:, t, 0:W], hh[:, t, 0:W].bitcast(F32), ALU.subtract).then_inc(h_ready, 1)
                s = plan.split[l, "wout", 0]
                split_low(s)
                split_low(s + 1)
                for m in range(KT):
                    residual(l, m, 2 * KT, W, "wout", m)
                    split_low(s + m + SPLITS)
                gains(l, 1)
                low_parts(l, "n2", W)
                if l < DEPTH - 1:
                    dve.wait_ge(cond_ready, l + 2)
                j0 = 0
                for st, nj in enumerate(SETS):
                    first, s0 = plan.job[l, "ffa", j0], plan.split[l, "ffa", j0]
                    g0 = plan.granule[l, "ffa", j0]
                    silus, mine = plan.before[first]["A"], plan.before[first]["V"]
                    per = 2

                    def hidden(i, last, turns):
                        for t in range(PAIRS):
                            if t % 2:
                                half = t // 2
                                dve.wait_ge(job_done, first + t + 1 + PAIRS * i)
                                dve.wait_ge(act_drained, silus + half + 1 + 2 * i)
                                dve.tensor_tensor(ut[:, half, 0:W], sq[:, half, 0:W], pair(first + t)[:, 0:W], ALU.mult)\
                                   .then_inc(dve_drained, 1)
                                dve.wait_ge(dve_drained, mine + half + 1 + 2 * i)
                                link(dve.tensor_copy(uh[:, half + 2 * i, 0:W], ut[:, half, 0:W]), turns)
                                dve.tensor_tensor(ul[:, half + 2 * i, 0:W], ut[:, half, 0:W],
                                                  uh[:, half + 2 * i, 0:W].bitcast(F32), ALU.subtract).then_inc(u_ready, 1)
                                dve.wait_ge(u_ready, l * NF + j0 + half + 1 + 2 * i)
                            if last and t >= PAIRS - SPLITS:
                                split_low(plan.split[l, "ffo", st, t - (PAIRS - SPLITS)])
                            else:
                                g = g0 + t + SPLITS
                                dve.wait_ge(high_done, s0 + t + SPLITS + 1 + PAIRS * i)
                                dve.tensor_tensor(wsplit[:, (s0 + t) % SPLITS, 1], slot(g),
                                                  wsplit[:, (s0 + t) % SPLITS, 0].bitcast(F32), ALU.subtract)\
                                   .then_inc(split_done, 1)

                    with dve.Fori(0, nj // 2 - 1) as i:
                        hidden(i, False, per * i)
                    links[0] += per * (nj // 2 - 2)
                    hidden(nj // 2 - 1, True, 0)
                    j0 += nj
                    for what, *i in output_schedule(l, st):
                        if what == "mod":
                            modulation(l + 1, i[0])
                        else:
                            residual(l, i[1], 5 * KT, W, "ffo", st, i[1])
                            nxt = plan.split[l, "ffo", st, i[1]] + SPLITS
                            if nxt < len(plan.splits):
                                split_low(nxt)
            norm(DEPTH, "final", [x[:, k] for k in range(KT)], [g_final[:, k:k + 1] for k in range(KT)], LAT,
                 into=[y[:, k] for k in range(KT)])


N_CONST = 9


def constants():
    f = np.float32
    c = {"ident": np.eye(P), "blk": np.kron(np.eye(2), np.ones((HD, HD)))}
    def turn(n):
        r = np.zeros((n, n))
        for m in range(n // 2):
            r[m + n // 2, m] = -1.0
            r[m, m + n // 2] = 1.0
        return r
    c["rot"] = np.kron(np.eye(2), turn(HD))
    c["rot_mla"] = np.zeros((P, MLA_ROPE))
    c["rot_mla"][64:96] = turn(MLA_ROPE)
    c["delta"] = np.arange(896)[None, :] - np.arange(P)[:, None] - 384.0

    def rope(dim):
        q = dim // 4
        inv = THETA ** (-np.arange(q) / q)
        tok = np.arange(LAT)
        ang = np.concatenate([inv[:, None] * (tok // GRID_W)[None], inv[:, None] * (tok % GRID_W)[None]])
        ang = np.concatenate([ang, ang])
        return np.stack([np.cos(ang), np.sin(ang)], 1)

    c["cs"] = np.tile(rope(HD), (2, 1, 1))
    bands = (HY_EMB - 1) // 2
    fb = np.linspace(1e-4, bands - 1, bands)
    zt, negt = np.zeros((P, TOK)), np.zeros((P, 6))
    for net, n in NET_LEN.items():
        t = np.linspace(0.0, 1.0, n)
        w = 2.0 * np.pi * np.arange(n) / n
        at = NET_AT[net]
        zt[0, at:at + n] = t
        zt[1:1 + bands, at:at + n] = np.cos(fb[:, None] * w)
        zt[1 + bands:HY_EMB, at:at + n] = -np.sin(fb[:, None] * w)
        negt[:, at // P:(at + n) // P] = -t.reshape(-1, P).T
        tk, fr = np.arange(n)[:, None], np.arange(n)[None, :]
        ang = np.pi * tk * fr / n
        im = -np.sin(ang)
        im[:, 0] = (-1.0) ** np.arange(n)
        fwd = np.concatenate([np.cos(ang), im], 1)
        scale = np.full((2 * n, 1), 2.0)
        scale[0] = scale[n] = 1.0
        inv = fwd.T * scale / (2 * n)
        if net == "lat":
            c["dft_lat"] = np.concatenate([fwd.reshape(4, P, 2 * n),
                                           inv.reshape(4, 2, P, n).transpose(0, 2, 1, 3).reshape(4, P, 2 * n)])
        else:
            c["dft_ctx"] = np.stack([fwd.reshape(2, P, 2 * n).transpose(1, 0, 2).reshape(P, 4 * n),
                                     inv.reshape(4, P, n).transpose(1, 0, 2).reshape(P, 4 * n)])
    c["zt_cs"], c["negt"] = np.zeros((P, 2 * LAT)), negt
    c["zt_cs"][0:HY_EMB, 0:TOK] = zt[0:HY_EMB]
    c["zt_cs"][64:96] = rope(MLA_ROPE).reshape(MLA_ROPE, 2 * LAT)
    lo, hi = np.log(1e-2) / 0.3, np.log(1e-2) / 1.5
    dl = np.abs(np.linspace(lo, hi, 4 * GROUP)).reshape(2, 2, GROUP).transpose(1, 0, 2).reshape(1, -1)
    c["absd"] = np.tile(dl, (P, 1))
    return {k: np.ascontiguousarray(v, dtype=f) for k, v in c.items()}


def layout(v):
    f = np.float32

    def grains(w):
        k, n = w.shape[0] // P, w.shape[1] // P
        return w.reshape(k, P, n, P).transpose(2, 1, 0, 3).reshape(n, P, k * P)

    def cols(w, m):
        return w.reshape(m, P).T

    o = {}
    o["x"] = np.concatenate([v["x"][0], v["ctx"][0]]).T.reshape(KT, P, TOK).transpose(1, 0, 2)
    o["cond"] = np.tile(np.stack([v["c"][0], v["c_ctx"]]), (P, 1, 1))
    o["g_final"] = cols(v["final_norm_g"], KT)
    o["w_mod"] = np.stack([v["w_mod"][l].T.reshape(N_MOD, P, D) for l in range(DEPTH)])
    q0 = 3 * GROUP
    r0 = q0 + GROUP + P + MLA_ROPE
    g0 = r0 + 4 * GROUP
    win = []
    for l in range(DEPTH):
        w = v["w_in"][l]
        kr = np.zeros((D, P), f)
        kr[:, 64:96] = w[:, r0 - MLA_ROPE:r0]
        gq = w[:, g0:g0 + GROUP].reshape(D, 2, 2, HD).transpose(0, 2, 1, 3).reshape(D, GROUP)
        win.append(grains(np.concatenate([
            w[:, q0:q0 + GROUP + P], kr, gq, w[:, g0 + GROUP:g0 + GROUP + P], w[:, r0:r0 + 2 * GROUP],
            w[:, r0 + 3 * GROUP:g0], w[:, r0 + 2 * GROUP:r0 + 3 * GROUP], w[:, g0 + GROUP + P:g0 + GROUP + 2 * P],
            w[:, 0:q0]], 1)))
    o["w_in"] = np.stack(win)
    o["w_out"] = np.stack([grains(v["w_out"][l]) for l in range(DEPTH)])
    o["w_ffn_in"] = np.stack([grains(v["w_ffn_in"][l]).reshape(2, NF, P, D).transpose(1, 0, 2, 3).reshape(2 * NF, P, D)
                              for l in range(DEPTH)])
    o["w_ffn_out"] = np.zeros((DEPTH, len(SETS), KT, P, max(SETS) * P), f)
    for l in range(DEPTH):
        j0 = 0
        for s, nj in enumerate(SETS):
            blocks = v["w_ffn_out"][l][j0 * P:(j0 + nj) * P].reshape(nj, P, KT, P).transpose(2, 1, 0, 3)
            o["w_ffn_out"][l, s, :, :, 0:nj * P] = blocks.reshape(KT, P, nj * P)
            j0 += nj
    o["w_small"] = np.zeros((P, DEPTH, 3 * HY_FFN), f)
    o["w_small"][0:HY_EMB, :, 0:HY_FFN] = v["hy_w1"].transpose(1, 0, 2)
    o["w_small"][0:HY_FFN, :, HY_FFN:2 * HY_FFN] = v["hy_w2"].transpose(1, 0, 2)
    o["w_small"][0:HY_FFN, :, 2 * HY_FFN:] = v["hy_w3"].transpose(1, 0, 2)
    o["w4"] = v["hy_w4"].reshape(DEPTH, HY_FFN, 2, 2, GROUP).transpose(0, 1, 3, 2, 4).reshape(DEPTH, HY_FFN, 1024)
    o["wuq"] = v["mla_w_uq"].reshape(DEPTH, 2, P, HEADS * MLA_D).transpose(0, 2, 1, 3).reshape(DEPTH, P, -1)
    o["wukv"] = v["mla_w_ukv"].reshape(DEPTH, P, HEADS, 2, HD).transpose(0, 1, 3, 2, 4).reshape(DEPTH, P, 2 * GROUP)

    def pad(w):
        z = np.zeros((P, 1), f)
        z[:len(w), 0] = w
        return z

    par = np.zeros((P, DEPTH, N_PARAM), f)
    for l in range(DEPTH):
        for name, val in (
                ("b_mod", cols(v["b_mod"][l], N_MOD)), ("g_attn", cols(v["norm_attn_g"][l], KT)),
                ("g_ffn", cols(v["norm_ffn_g"][l], KT)), ("conv_b", cols(v["hy_conv_b"][l], 6)),
                ("conv_w", cols(v["hy_conv_w"][l].reshape(-1), 18)), ("hy_bias", cols(v["hy_bias"][l].reshape(-1), 4)),
                ("g_q", cols(v["mla_q_norm_g"][l], 2)), ("g_kv", cols(v["mla_kv_norm_g"][l], 1)),
                ("g_ret", cols(v["ret_norm_g"][l], 2)), ("g_out", cols(v["out_norm_g"][l], 8)),
                ("g_gq", np.tile(v["gqa_q_norm_g"][l], 2)[:, None]), ("g_gk", np.tile(v["gqa_k_norm_g"][l], 2)[:, None]),
                ("decay", np.tile(v["ret_decay"][l].reshape(1, 8), (P, 1))),
                ("b1", pad(v["hy_b1"][l])), ("b2", pad(v["hy_b2"][l])), ("b3", pad(v["hy_b3"][l])),
                ("freq", pad(v["hy_freq"][l]))):
            at, n = PARAM[name]
            par[:, l, at:at + n] = val
    o["par"] = par
    return o


def kernel(**inputs):
    import concourse.bacc as bacc
    from concourse.bass_utils import run_bass_kernel_spmd

    nc = bacc.Bacc("TRN2", target_bir_lowering=False, num_devices=1)
    arrays = {**layout({k: np.asarray(w) for k, w in inputs.items()}), **constants()}
    arrays = {f"in_{k}": np.ascontiguousarray(w) for k, w in arrays.items()}
    aps = {k[3:]: nc.dram_tensor(k, w.shape, F32, kind="ExternalInput").ap() for k, w in arrays.items()}
    out = nc.dram_tensor("out_dram", (P, KT, LAT), F32, kind="ExternalOutput").ap()
    hymba_block(nc, aps, out)
    got = run_bass_kernel_spmd(nc, [arrays], core_ids=[0]).results[0]["out_dram"]
    return np.ascontiguousarray(got.transpose(2, 1, 0).reshape(1, LAT, D))
```

```python
from contextlib import ExitStack

import numpy as np

import concourse.bass as bass
from concourse import mybir

F32 = mybir.dt.float32
F32R = mybir.dt.float32r
ACT = mybir.ActivationFunctionType
ALU = mybir.AluOpType
AX = mybir.AxisListType.X

P = 128
D = 1024
KT = D // P
LAT, CTX = 512, 256
TOK = LAT + CTX
DEPTH = 2
GRID_W = 64
EPS = 1e-6
THETA = 10000.0
GROUP = 256
DFF = 2816
NF = DFF // P
HEADS = 4
HD = 64
MLA_ROPE = 32
MLA_D = HD + MLA_ROPE
MLA_SCALE = MLA_D ** -0.5
GQA_SCALE = HD ** -0.5
RET_K_SCALE = HD ** -0.5
N_MOD = 6 * KT
HY_EMB = 33
HY_FFN = 64
HY_COLS = 2 * GROUP
NET_LEN = {"lat": LAT, "ctx": CTX}
NET_AT = {"lat": 0, "ctx": LAT}
RING = 4
SPLITS = 2
GRAN = 1024
PAIRS = 4
MAGIC = 1.5 * 2.0 ** 23
INV_2PI = 1.0 / (2.0 * np.pi)
TWO_PI_HI = 6.28125
TWO_PI_LO = 2.0 * np.pi - TWO_PI_HI
PI_BELOW = 3.1415925

PARAM = {}
for _name, _n in (("b_mod", N_MOD), ("g_attn", KT), ("g_ffn", KT), ("conv_b", 6), ("conv_w", 18),
                  ("hy_bias", 4), ("g_q", 2), ("g_kv", 1), ("g_ret", 2), ("g_out", 8), ("g_gq", 1),
                  ("g_gk", 1), ("decay", 8), ("b1", 1), ("b2", 1), ("b3", 1), ("freq", 1)):
    PARAM[_name] = (sum(n for _, n in PARAM.values()), _n)
N_PARAM = sum(n for _, n in PARAM.values())


def lay(at, *parts):
    places = {}
    for name, n in parts:
        places[name] = at
        at += n
    return places, at


AT, R2 = lay(0, ("retq", 2 * TOK), ("retk", 2 * TOK), ("retg", 2 * TOK), ("gq", 2 * TOK), ("gk", TOK),
             ("cq", 2 * TOK), ("ckv", TOK), ("kr", TOK), ("vret", 6 * GROUP), ("vgqa", 6 * P), ("hy", 6 * TOK))
_split, WORK = lay(R2, ("hh", KT * TOK), ("hl", KT * TOK), ("yraw", KT * TOK))
AT.update(_split)
AT["wsplit"] = AT["yraw"]
_hyena, _end = lay(R2, ("klat", 8 * HY_COLS), ("kctx", 4 * HY_COLS), ("scratch", 0), ("vtok", 4 * GROUP),
                   ("y", 8 * GROUP), ("t0", 512), ("t1", 512))
assert _end <= AT["yraw"]
AT.update(_hyena)
_filt, _end = lay(AT["scratch"], ("absd", 1024), ("w4", 1024), ("edec", 2048), ("f", 2048), ("sumabs", 512),
                  ("rn", 512), ("fa", 2048), ("fb", 2048))
assert _end <= WORK
AT.update(_filt)
_ret, _end = lay(AT["hy"], ("rpt", 2 * 6 * LAT), ("dec", 2 * (896 + 640)), ("delta", 896))
assert _end <= AT["yraw"]
AT.update(_ret)
_gqa, _end = lay(AT["hy"], ("prob_gqa", 3 * TOK), ("pt_gqa", 2 * TOK))
assert _end <= R2
_mla, _end = lay(AT["vret"], ("mq", HEADS * TOK), ("mk", HEADS * TOK))
assert _end <= R2
_mla2, _end = lay(AT["gq"], ("vmla", 6 * GROUP), ("prob_mla", 3 * TOK), ("pt_mla", 2 * TOK))
assert _end <= AT["vret"]
AT["wsplit_out"] = AT["retq"]
assert AT["wsplit_out"] + SPLITS * 2 * GRAN <= AT["gq"]
AT["scaled"] = AT["hy"]
assert AT["scaled"] + 4 * TOK <= R2
for _places in (_gqa, _mla, _mla2):
    AT.update(_places)
AT["cond"], AT["unused"] = AT["wsplit"] + SPLITS * 2 * GRAN, AT["vret"] + TOK
assert AT["cond"] + 2 * D <= WORK and AT["unused"] + D <= AT["hy"]
AT["ha"], AT["ht"] = AT["hy"], AT["hy"] + TOK
_ffn, _end = lay(0, ("uh", 6 * TOK), ("ul", 6 * TOK), ("ut", 2 * TOK))
assert _end <= AT["unused"]
AT.update(_ffn)

NORM_TILES = {"cq": 2, "ckv": 1, "gq0": 1, "gq1": 1, "gk": 1, "hy": 2, "mla": 2, "ret0": 1,
              "ret1": 1, "ret": 2, "gqa": 2, "n1": 0, "n2": 0, "final": 0}
SCALED_TILES = 4
OUTPUTS = {"hy": (0, 1), "mla": (2, 3), "ret": (4, 5), "gqa": (6, 7), "ret0": (4,), "ret1": (5,)}
Y_ORDER = (0, 1, 4, 5, 6, 7, 2, 3)
ROPES = ("retq0", "retq1", "retk0", "retk1", "gq0", "gq1", "gk")
WIN = ("cq0", "cq1", "ckv", "kr", "gq0", "gq1", "gk", "retq0", "retq1", "retk0", "retk1", "retg0", "retg1",
       "vret0", "vret1", "vgqa", "hy0", "hy1", "hy2", "hy3", "hy4", "hy5")
N_WIN = len(WIN)
VALUES = ("vret0", "vret1", "vgqa")
ALL_TOKENS = ("ckv", "kr", "gk", "retk0", "retk1") + VALUES
BETWEEN = {2: [("square", "cq")], 3: [("norm", "cq")], 4: [("square", "ckv")], 5: [("norm", "ckv"), ("mlp", 0)],
           6: [("square", "gq0")], 7: [("norm", "gq0")], 8: [("square", "gq1"), ("mlp", 1)],
           9: [("norm", "gq1"), ("rope", "retq0")], 10: [("square", "gk"), ("rope", "gq0"), ("rope", "retq1")],
           11: [("norm", "gk"), ("rope", "gq1"), ("mlp", 2)], 12: [("rope", "retk0")],
           13: [("rope", "gk"), ("rope", "retk1")], 15: [("vturn", 0)], 16: [("vturn", 1)], 17: [("vturn", 2)]}
BESIDE = {"gqa": {0: [("square", "hy")], 2: [("norm", "hy")], 3: [("square", "ret0")], 5: [("norm", "ret0")],
                  6: [("square", "ret1")], 8: [("norm", "ret1")], 9: [("square", "ret")], 11: [("norm", "ret")]},
          "mla": {0: [("square", "gqa")], 1: [("high", 0)], 2: [("norm", "gqa")], 3: [("high", 1)], 4: [("high", 2)],
                  6: [("high", 3)], 7: [("high", 4)], 9: [("high", 5)]}}
MOD_FIRST = 2 * KT
MOD_PER_WIN = 3
MOD_FROM = 1
RECIPROCAL = ("cq", "ckv", "gq0", "gq1", "gk")
SETS = (6, 6, 6, 4)


def nets(layer):
    return ("lat", "ctx") if layer < DEPTH - 1 else ("lat",)


def width(layer):
    return TOK if layer < DEPTH - 1 else LAT


def input_schedule(layer):
    out, j = [], MOD_FIRST
    for g in range(N_WIN):
        out.append(("win", g))
        for _ in range(min(MOD_PER_WIN, N_MOD - j) if layer == 0 and g >= MOD_FROM else 0):
            out.append(("mod", j))
            j += 1
        out += BETWEEN.get(g, [])
    return out


def output_schedule(layer, s):
    out = []
    j = s * N_MOD // len(SETS)
    for m in range(KT):
        out.append(("ffo", s, m))
        if layer < DEPTH - 1:
            for _ in range(2 if m < KT - SPLITS else 0):
                out.append(("mod", j))
                j += 1
    return out


def attention_units(layer, kind):
    return [(kind, net, h, t) for h in range(HEADS) for net in nets(layer)
            for t in range(NET_LEN[net] // P)]


def attention_steps(layer, kind):
    units = attention_units(layer, kind)
    for i in range(len(units) + 3):
        for job, lag in (("s", 0), ("scale", 1), ("t", 2), ("pv", 3)):
            if 0 <= i - lag < len(units):
                yield job, units[i - lag]
        yield from BESIDE[kind].get(i, [])


def retention_units(layer):
    return [(net, h) for h in range(HEADS) for net in nets(layer)]


class Plan:

    def __init__(self):
        self.jobs, self.job = [], {}
        self.granules = []
        self.norm, self.unit = {}, {}
        self.splits, self.split = [], {}
        for j in range(MOD_FIRST):
            self.modulation(0, j)
        for layer in range(DEPTH):
            self.layer(layer)
        self.add_norm(DEPTH, "final")
        self.granules = [g[1:] for g in sorted(self.granules, key=lambda g: g[0])]
        self.granule = {g[0]: n for n, g in enumerate(self.granules)}
        count = {"A": 0, "V": 0}
        self.before = []
        for who in self.jobs:
            self.before.append(dict(count))
            count[who] += 1

    def add(self, who, *key):
        self.job[key] = len(self.jobs)
        self.jobs.append(who)

    def grain(self, *key, split=False):
        job = len(self.jobs) - 1
        if not split:
            self.granules.append((job, key, "job", job))
            return
        s = self.split[key] = len(self.splits)
        self.splits.append(job)
        if key[:2] == (0, "win") and key[2] < SPLITS:
            after = job - 1 - key[2]
        elif key[1] == "wout" and key[2] < SPLITS:
            after = self.before_wout + 1
        else:
            after = self.splits[s - SPLITS]
        self.granules.append((after - 0.5, key, "split", s))

    def add_norm(self, layer, name):
        tiles = [NORM_TILES[n] for _, n in self.norm]
        self.norm[layer, name] = (len(tiles), sum(tiles), sum(max(0, n - 1) for n in tiles))
        self.add("A", layer, "norm", name)

    def modulation(self, l, j):
        self.granules.append((len(self.jobs) - 1, (l, "mod", j), "mod", l * N_MOD + j))

    def layer(self, l):
        add, grain = self.add, self.grain
        self.add_norm(l, "n1")
        for what, i in input_schedule(l):
            if what == "win":
                add("V" if WIN[i][:2] == "hy" else "A", l, "win", i)
                grain(l, "win", i, split=True)
            elif what == "mod":
                self.modulation(l, i)
            elif what == "norm":
                self.add_norm(l, i)
            elif what != "square":
                add("A" if what == "vturn" else "V", l, what, i)
        for net in nets(l):
            nt = NET_LEN[net] // P
            for t in range(nt):
                add("V", l, "filt", net, t)
            add("V", l, "l1", net)
            for i in range(nt):
                add("V", l, "spec", net, i)
            add("V", l, "nyq", net)
            for t in range(nt if net == "lat" else 1):
                grain(l, "F", net, t, "spec")
        for net in nets(l):
            nt = NET_LEN[net] // P
            for o in range(2):
                add("A", l, "turn", net, o)
                for i in range(nt // 2):
                    add("V", l, "fwd", net, o, i)
                for t in range(nt if net == "lat" else 1):
                    grain(l, "F", net, t, o)
                add("V", l, "inv", net, o)
                for t in range(nt if net == "lat" else 1):
                    grain(l, "G", net, t, o)
        units = retention_units(l)
        for i, un in enumerate(units + [None]):
            if un:
                for part in range(3 if un[0] == "lat" else 1):
                    add("V", l, "rs", *un, part)
            if i:
                add("A", l, "rpv", *units[i - 1])
        self.attention(l, "gqa")
        for h in range(HEADS):
            add("A", l, "mq", h)
        grain(l, "wuq")
        for h in range(HEADS):
            add("V", l, "mqrope", h)
        add("V", l, "krrope")
        for h in range(HEADS):
            add("A", l, "mk", h)
        for part in range(2):
            add("A", l, "mv", part)
        grain(l, "wukv")
        self.before_wout = len(self.jobs) - 1
        self.attention(l, "mla")
        self.add_norm(l, "mla")
        for m in range(KT):
            add("V", l, "wout", m)
            grain(l, "wout", m, split=True)
        self.add_norm(l, "n2")
        j0 = 0
        for s, nj in enumerate(SETS):
            for j in range(j0, j0 + nj):
                add("A", l, "ffa", j)
                grain(l, "ffa", j, split=True)
                add("V", l, "ffg", j)
                grain(l, "ffg", j, split=True)
            j0 += nj
            for what, *i in output_schedule(l, s):
                if what == "mod":
                    self.modulation(l + 1, i[0])
                else:
                    add("V", l, "ffo", s, i[1])
                    grain(l, "ffo", s, i[1], split=True)

    def attention(self, l, kind):
        units = attention_units(l, kind)
        for u in units:
            self.unit[(l,) + u] = len(self.unit)
        for job, u in attention_steps(l, kind):
            if job == "norm":
                self.add_norm(l, u)
            elif job in ("s", "t", "pv"):
                self.add("A", l, job, *u)



def hymba_block(nc, a, out):
    plan = Plan()
    n_units = len(plan.unit)
    with ExitStack() as ctx:
        def sb(name, *shape):
            return ctx.enter_context(nc.sbuf_tensor(name, [P, *shape], F32))

        def sem(name):
            return ctx.enter_context(nc.semaphore(name))

        work = sb("work", WORK)
        work_at = nc.sbuf_base - 4 * WORK
        x = sb("x_resid", KT, TOK)
        ring = sb("ring", RING, GRAN)
        ident = sb("ident", P)
        rot = sb("rot", P)
        rot_mla = sb("rot_mla", MLA_ROPE)
        ones = sb("ones", P)
        blk = sb("blk", P)
        cs = sb("cs", 2, LAT)
        zt_cs = sb("zt_cs", 2 * LAT)
        negt = sb("negt", 6)
        par = sb("par", DEPTH, N_PARAM)
        w_small = sb("w_small", DEPTH, 3 * HY_FFN)
        hb = sb("hb", TOK)
        g_final = sb("g_final", KT)
        mod = sb("mod", DEPTH, N_MOD, 2)
        gain = sb("gain", 2, KT, 2)
        sq = sb("sq", 2, TOK)
        std = sb("std", TOK)
        turned = sb("turned", LAT)
        eps = sb("eps", 1)
        lg = sb("lg", 6, 8)
        smax = sb("smax", n_units)
        nmax = sb("nmax", n_units)
        rsum = sb("rsum", n_units)
        rinv = sb("rinv", n_units)
        ps = ctx.enter_context(nc.psum_tensor("ps", [P, PAIRS, 1024], F32))

        def rounded(name, *shape):
            return nc.alloc_sbuf_tensor_at(f"{name}_r", [P, *shape], F32R, offset=work_at + 4 * AT[name])

        hh, hl = rounded("hh", KT, TOK), rounded("hl", KT, TOK)
        uh, ul = rounded("uh", 6, TOK), rounded("ul", 6, TOK)
        wsplit, wsplit_out = (rounded(n, SPLITS, 2, GRAN) for n in ("wsplit", "wsplit_out"))

        def view(name, *shape):
            n = int(np.prod(shape))
            v = work[:, AT[name]:AT[name] + n]
            if len(shape) == 2:
                v = v.rearrange("p (a b) -> p a b", a=shape[0])
            elif len(shape) == 3:
                v = v.rearrange("p (a b c) -> p a b c", a=shape[0], b=shape[1])
            return v

        retq, retk, retg = (view(n, 2, TOK) for n in ("retq", "retk", "retg"))
        gq, gk, cq, ckv, kr = view("gq", 2, TOK), view("gk", TOK), view("cq", 2, TOK), view("ckv", TOK), view("kr", TOK)
        vret, vgqa = view("vret", 6, GROUP), view("vgqa", 6, P)
        hy, y = view("hy", 6, TOK), view("yraw", KT, TOK)
        spec = {"lat": view("klat", 4, 2, HY_COLS), "ctx": view("kctx", 2, 2, HY_COLS)}
        vtok, yf = view("vtok", 4, GROUP), view("y", 8, GROUP)
        tmp0, tmp1 = view("t0", 2, GROUP), view("t1", 2, GROUP)
        absd, w4 = view("absd", 1024), view("w4", 1024)
        edec, filt = view("edec", 2, 1024), view("f", 2, 1024)
        sumabs, rn = view("sumabs", HY_COLS), view("rn", HY_COLS)
        fa, fb = view("fa", 4, HY_COLS), view("fb", 4, HY_COLS)
        ha, ht = view("ha", TOK), view("ht", TOK)
        mq, mk, vmla = view("mq", HEADS, TOK), view("mk", HEADS, TOK), view("vmla", 6, GROUP)
        prob = {kind: view(f"prob_{kind}", 3, TOK) for kind in ("gqa", "mla")}
        pt = {kind: view(f"pt_{kind}", 2, TOK) for kind in ("gqa", "mla")}
        scaled = view("scaled", SCALED_TILES, TOK)
        rpt, dec, delta = view("rpt", 2, 6, LAT), view("dec", 2, 896 + 640), view("delta", 896)
        ut = view("ut", 2, TOK)
        cond, unused = view("cond", 2, D), view("unused", D)
        cs_mla = zt_cs[:, :].rearrange("p (a b) -> p a b", a=2)
        inputs = {f"{n}{i}": t[:, i] for n, t in (("cq", cq), ("gq", gq), ("retq", retq), ("retk", retk), ("retg", retg))
                  for i in range(2)}
        inputs.update(ckv=ckv, kr=kr, gk=gk, vret0=hy[:, 3], vret1=hy[:, 4], vgqa=hy[:, 5])
        by_token = {"vret0": vret[:, :, 0:P], "vret1": vret[:, :, P:GROUP], "vgqa": vgqa}
        inputs.update({f"hy{i}": hy[:, i] for i in range(6)})

        def param(layer, name, i=0):
            at = PARAM[name][0] + i
            return par[:, layer, at:at + 1]

        def win_width(l, name):
            return TOK if name in ALL_TOKENS else width(l)

        x_loaded, cond_loaded, const_loaded = sem("x_loaded"), sem("cond_loaded"), sem("const_loaded")
        filter_loaded, delta_loaded = sem("filter_loaded"), sem("delta_loaded")
        slot_loaded = [sem(f"slot{i}_loaded") for i in range(RING)]
        out_stored = sem("out_stored")
        job_done = sem("job_done")
        act_drained, dve_drained = sem("act_drained"), sem("dve_drained")
        drained = {"A": act_drained, "V": dve_drained}
        high_done, split_done = sem("high_done"), sem("split_done")
        ones_set = sem("ones_set")
        cond_ready, mod_done = sem("cond_ready"), sem("mod_done")
        angle_ready, sin_ready = sem("angle_ready"), sem("sin_ready")
        decay_ready, filt_ready, ab_ready = sem("decay_ready"), sem("filt_ready"), sem("ab_ready")
        abs_ready, sumabs_ready = sem("abs_ready"), sem("sumabs_ready")
        abs_part, abs_summed = sem("abs_part"), sem("abs_summed")
        squares_ready, squares_used = sem("squares_ready"), sem("squares_used")
        x_squared, squares_added = sem("x_squared"), sem("squares_added")
        norm_applied = sem("norm_applied")
        h_shifted, h_high = sem("h_shifted"), sem("h_high")
        h_scaled, h_rounded, h_ready = sem("h_scaled"), sem("h_rounded"), sem("h_ready")
        conv_part = sem("conv_part")
        spectrum_ready = sem("spectrum_ready")
        kpe_ready, kpe_copied = sem("kpe_ready"), sem("kpe_copied")
        nmax_ready, prob_ready = sem("nmax_ready"), sem("prob_ready")
        log_part, log_ready = sem("log_part"), sem("log_ready")
        dec_arg, dec_exp = sem("dec_arg"), sem("dec_exp")
        u_ready = sem("u_ready")
        dve_chain, act_chain = sem("dve_chain"), sem("act_chain")

        def pair(n):
            return ps[:, n % PAIRS]

        def wait_job(eng, *key):
            eng.wait_ge(job_done, plan.job[key] + 1)

        def wait_drained(eng, *key):
            n = plan.job[key]
            who = plan.jobs[n]
            eng.wait_ge(drained[who], plan.before[n][who] + 1)

        def slot(n):
            return ring[:, n % RING]

        def grid(ap, n):
            return ap.rearrange("p (k c) -> p k c", k=n)

        def columns(key):
            return SETS[key[2]] * P if key[1] == "ffo" else GRAN

        def before_norm(l, name):
            idx = plan.norm[l, name][0]
            return next((k for k in plan.norm if plan.norm[k][0] == idx - 1), None)

        SCALED = {"n1": 0, "y": KT, "n2": 2 * KT}
        split_keys = {n: k for k, n in plan.split.items()}

        def part_of(s, part):
            return (wsplit_out if split_keys[s][1] == "wout" else wsplit)[:, s % SPLITS, part]

        def over_x(l, name):
            return 2 * l + (name == "n2")

        block = ctx.enter_context(nc.Block())

        @block.sync
        def _(sp):
            def source(key):
                l, name = key[0], key[1]
                if name == "F":
                    return a["dft_lat"][key[3]] if key[2] == "lat" else a["dft_ctx"][0]
                if name == "G":
                    return a["dft_lat"][4 + key[3]] if key[2] == "lat" else a["dft_ctx"][1]
                if name in ("ffa", "ffg"):
                    return a["w_ffn_in"][l, 2 * key[2] + (name == "ffg")]
                if name == "ffo":
                    return a["w_ffn_out"][l, key[2], key[3], :, 0:columns(key)]
                if name in ("wuq", "wukv"):
                    return a[name][l]
                return a[{"mod": "w_mod", "win": "w_in", "wout": "w_out"}[name]][l, key[2]]

            def load(n):
                if n >= RING:
                    _, how, last = plan.granules[n - RING]
                    sp.wait_ge({"split": split_done, "job": job_done, "mod": mod_done}[how], last + 1)
                src = source(plan.granules[n][0])
                sp.dma_start(slot(n)[:, 0:src.shape[1]], src).then_inc(slot_loaded[n % RING], 16)

            n = 0
            for l in range(DEPTH):
                j0 = 0
                for nj in SETS:
                    first = plan.granule[l, "ffa", j0]
                    while n < first + RING:
                        load(n)
                        n += 1
                    s0 = plan.split[l, "ffa", j0]
                    with sp.Fori(0, nj // 2 - 1) as i:
                        for t in range(RING):
                            sp.wait_ge(split_done, s0 + t + 1 + RING * i)
                            sp.dma_start(slot(first + t), a["w_ffn_in"][l, 2 * j0 + RING + t + RING * i])\
                              .then_inc(slot_loaded[(first + t) % RING], 16)
                    n = first + 2 * nj
                    j0 += nj
            while n < len(plan.granules):
                load(n)
                n += 1
            sp.wait_ge(norm_applied, plan.norm[DEPTH, "final"][0] + 1)
            sp.dma_start(out, y[:, :, 0:LAT]).then_inc(out_stored, 16)
            sp.wait_ge(out_stored, 16)

        @block.tensor
        def _(pe):
            def begin(*key):
                n = plan.job[key]
                if n >= PAIRS:
                    who = plan.jobs[n - PAIRS]
                    pe.wait_ge(drained[who], plan.before[n - PAIRS][who] + 1)
                return pair(n)

            def arrived(*key):
                n = plan.granule[key]
                pe.wait_ge(slot_loaded[n % RING], 16 * (n // RING + 1))
                return slot(n)

            def halves(*key):
                s = plan.split[key]
                pe.wait_ge(split_done, s + 1)
                return (grid(part_of(s, part)[:, 0:columns(key)], columns(key) // P) for part in range(2))

            def segments(w):
                return [(c, min(c + LAT, w)) for c in range(0, w, LAT)]

            def products(w, d, k):
                wh, wl = w
                dh, dl = d
                return ((wh[:, k], dh), (wh[:, k], dl), (wl[:, k], dh))

            def norm(l, name, matrix, w):
                _, done, _ = plan.norm[l, name]
                nt = NORM_TILES[name]
                dst = begin(l, "norm", name)
                if nt == 0:
                    pe.wait_ge(squares_added, (KT - 1) * (over_x(l, name) + 1))
                    for c0, c1 in segments(w):
                        mm = pe.matmul(dst[:, c0:c1], matrix[:, :], std[:, c0:c1], start=True, stop=True)
                for t in range(nt):
                    pe.wait_ge(squares_ready, done + t + 1)
                    for c0, c1 in segments(w):
                        mm = pe.matmul(dst[:, c0:c1], matrix[:, :], sq[:, (done + t) % 2, c0:c1],
                                       start=(t == 0), stop=(t == nt - 1))
                    if t < nt - 1:
                        mm.then_inc(squares_used, 1)
                mm.then_inc(job_done, 1)

            def project(dst, w, w_cols, width_, data=None, order=tuple(range(KT)), first=None):
                dh, dl = data or (hh, hl)
                for n, k in enumerate(order):
                    if first is not None:
                        pe.wait_ge(h_ready, first + n + 1)
                    for c0, c1 in segments(width_):
                        three = ((w[0], dh), (w[0], dl), (w[1], dh))
                        for i, (wp, dp) in enumerate(three):
                            mm = pe.matmul(dst[0:w_cols, c0:c1], wp[:, k, 0:w_cols], dp[:, k, c0:c1],
                                           start=(n == 0 and i == 0), stop=(n == len(order) - 1 and i == 2))
                return mm

            def filter_layer(l, k):
                dst = begin(l, "mlp", k)
                if k:
                    pe.wait_ge(sin_ready, 3 * l + k)
                for c0, c1 in segments(width(l)):
                    rows = HY_FFN if k else HY_EMB
                    src = hb if k else zt_cs
                    mm = pe.matmul(dst[0:HY_FFN, c0:c1], w_small[0:rows, l, k * HY_FFN:(k + 1) * HY_FFN],
                                   src[0:rows, c0:c1], start=True, stop=True)
                mm.then_inc(job_done, 1)

            def values(dst, v, weights, tiles, base, n):
                for j, kt in enumerate(tiles):
                    mm = pe.matmul(dst[base:base + HD, 0:n], v(kt), weights[:, j], start=(j == 0), stop=(j == len(tiles) - 1))
                mm.then_inc(job_done, 1)

            def attention(l, kind):
                for job, un in attention_steps(l, kind):
                    if job == "norm":
                        norm(l, un, blk if un in ("ret0", "ret1") else ones, width(l))
                    if job not in ("s", "t", "pv"):
                        continue
                    _, net, hd, t = un
                    n = plan.unit[(l,) + un]
                    dst = begin(l, job, *un)
                    nk = 6 if net == "lat" else 2
                    if job == "s":
                        c = NET_AT[net] + P * t
                        if kind == "mla":
                            q, keys = mq[0:MLA_D, hd, c:c + P], mk[0:MLA_D, hd]
                        else:
                            kv, r = hd // 2, hd % 2
                            q, keys = gq[HD * kv:HD * kv + HD, r, c:c + P], gk[HD * kv:HD * kv + HD]
                        if net == "lat":
                            pe.matmul(dst[:, 0:LAT], q, keys[:, 0:LAT], start=True, stop=True)
                            pe.matmul(dst[:, LAT:TOK], q, keys[:, LAT:TOK], start=True, stop=True).then_inc(job_done, 1)
                        else:
                            pe.matmul(dst[:, 0:CTX], q, keys[:, LAT:TOK], start=True, stop=True).then_inc(job_done, 1)
                    elif job == "t":
                        pe.wait_ge(prob_ready, n + 1)
                        for j in range(nk):
                            mm = pe.transpose(dst[:, j * P:(j + 1) * P], prob[kind][:, n % 3, j * P:(j + 1) * P], ident[:, :])
                        mm.then_inc(job_done, 1)
                    else:
                        wait_drained(pe, l, "t", *un)
                        col = HD * hd if kind == "mla" else HD * (hd // 2)
                        vt = vmla if kind == "mla" else vgqa
                        values(dst, lambda kt: vt[:, kt, col:col + HD], grid(pt[kind][:, n % 2, 0:nk * P], nk),
                               range(6) if net == "lat" else (4, 5), HD * (hd % 2), P)

            pe.wait_ge(ones_set, 2)
            for l in range(DEPTH):
                W = width(l)
                norm(l, "n1", ones, TOK)
                if l == 0:
                    pe.wait_ge(const_loaded, 16 * N_CONST)
                for what, i in input_schedule(l):
                    if what == "win":
                        name = WIN[i]
                        w = tuple(halves(l, "win", i))
                        dst = begin(l, "win", i)
                        project(dst, w, 96 if name == "kr" else P, win_width(l, name),
                                first=3 * KT * l if i == 0 else None).then_inc(job_done, 1)
                    elif what == "vturn":
                        dst = begin(l, "vturn", i)
                        wait_drained(pe, l, "win", WIN.index(VALUES[i]))
                        for t in range(TOK // P):
                            mm = pe.transpose(dst[:, t * P:(t + 1) * P], inputs[VALUES[i]][:, t * P:(t + 1) * P], ident[:, :])
                        mm.then_inc(job_done, 1)
                    elif what == "mlp":
                        filter_layer(l, i)
                    elif what == "norm":
                        norm(l, i, ones if i in ("cq", "ckv") else blk, win_width(l, i))
                    elif what == "rope":
                        dst = begin(l, "rope", i)
                        if i in ("gq0", "gq1", "gk"):
                            pe.wait_ge(norm_applied, plan.norm[l, i][0] + 1)
                        else:
                            wait_drained(pe, l, "win", WIN.index(i))
                        pe.matmul(dst[:, 0:LAT], rot[:, :], inputs[i][:, 0:LAT], start=True, stop=True).then_inc(job_done, 1)

                pe.wait_ge(sin_ready, 3 * l + 3)
                pe.wait_ge(filter_loaded, 32 * (l + 1))
                for ni, net in enumerate(nets(l)):
                    n = NET_LEN[net]
                    nt = n // P
                    for t in range(nt):
                        dst = begin(l, "filt", net, t)
                        c = NET_AT[net] + P * t
                        for half in range(2):
                            mm = pe.matmul(dst[:, half * 512:half * 512 + 512], hb[0:HY_FFN, c:c + P],
                                           w4[0:HY_FFN, half * 512:half * 512 + 512], start=True, stop=True)
                        mm.then_inc(job_done, 1)
                    dst = begin(l, "l1", net)
                    pe.wait_ge(sumabs_ready, 2 * l + ni + 1)
                    pe.matmul(dst[:, 0:HY_COLS], ones[:, :], sumabs, start=True, stop=True).then_inc(job_done, 1)
                    if net == "lat":
                        f = [arrived(l, "F", net, t, "spec") for t in range(nt)]
                    else:
                        fc = grid(arrived(l, "F", net, 0, "spec"), 2)
                        f = [fc[:, t] for t in range(nt)]
                    pe.wait_ge(ab_ready, 6 * l + (4 if ni == 0 else 6))
                    for i in range(nt):
                        dst = begin(l, "spec", net, i)
                        for part, src in ((0, fa), (1, fb)):
                            for t in range(nt):
                                mm = pe.matmul(dst[:, part * 512:part * 512 + 512],
                                               f[t][:, part * n + i * P:part * n + i * P + P], src[:, t],
                                               start=(t == 0), stop=(t == nt - 1))
                        mm.then_inc(job_done, 1)
                    dst = begin(l, "nyq", net)
                    for t in range(nt):
                        mm = pe.matmul(dst[0:1, 0:HY_COLS], f[t][:, n:n + 1], fa[:, t], start=(t == 0), stop=(t == nt - 1))
                    mm.then_inc(job_done, 1)

                for net in nets(l):
                    n, c = NET_LEN[net], NET_AT[net]
                    nt = n // P
                    for o in range(2):
                        dst = begin(l, "turn", net, o)
                        if o:
                            wait_drained(pe, l, "inv", net, 0)
                        for t in range(nt):
                            for ch in range(2):
                                mm = pe.transpose(dst[:, t * GROUP + ch * P:t * GROUP + ch * P + P],
                                                  hy[:, ch, c + t * P:c + t * P + P], ident[:, :])
                        mm.then_inc(job_done, 1)
                        if net == "lat":
                            f = [arrived(l, "F", net, t, o) for t in range(nt)]
                        else:
                            fc = grid(arrived(l, "F", net, 0, o), 2)
                            f = [fc[:, t] for t in range(nt)]
                        wait_drained(pe, l, "turn", net, o)
                        for i in range(nt // 2):
                            dst = begin(l, "fwd", net, o, i)
                            for part in range(2):
                                for q in range(2):
                                    at = part * n + (2 * i + q) * P
                                    for t in range(nt):
                                        mm = pe.matmul(dst[:, part * 512 + q * GROUP:part * 512 + (q + 1) * GROUP],
                                                       f[t][:, at:at + P], vtok[:, t], start=(t == 0), stop=(t == nt - 1))
                            mm.then_inc(job_done, 1)
                        dst = begin(l, "inv", net, o)
                        pe.wait_ge(spectrum_ready, 4 * l + 2 * nets(l).index(net) + o + 1)
                        for fi in range(2 * nt):
                            if net == "lat":
                                if fi % 2 == 0:
                                    g = grid(arrived(l, "G", net, fi // 2, o), 2)
                                gt = g[:, fi % 2]
                            else:
                                if fi == 0:
                                    g = grid(arrived(l, "G", net, 0, o), 4)
                                gt = g[:, fi]
                            for ch in range(2):
                                mm = pe.matmul(dst[:, ch * 512:ch * 512 + n], yf[:, fi, ch * P:ch * P + P], gt,
                                               start=(fi == 0), stop=(fi == 2 * nt - 1))
                        mm.then_inc(job_done, 1)

                units = retention_units(l)
                for i, un in enumerate(units + [None]):
                    if un:
                        net, hd = un
                        base, c, n = HD * (hd % 2), NET_AT[net], NET_LEN[net]
                        tiles = list(range(6)) if net == "lat" else [4, 5]
                        for part in range(len(tiles) // 2):
                            dst = begin(l, "rs", *un, part)
                            for q in range(2):
                                kt = tiles[2 * part + q]
                                mm = pe.matmul(dst[:, q * 512:q * 512 + n],
                                               retk[base:base + HD, hd // 2, kt * P:(kt + 1) * P],
                                               retq[base:base + HD, hd // 2, c:c + n], start=True, stop=True)
                            mm.then_inc(job_done, 1)
                    if i:
                        net, hd = units[i - 1]
                        n = NET_LEN[net]
                        tiles = range(6) if net == "lat" else (4, 5)
                        dst = begin(l, "rpv", net, hd)
                        wait_drained(pe, l, "rs", net, hd, len(tiles) // 2 - 1)
                        values(dst, lambda kt: vret[:, kt, HD * hd:HD * hd + HD], rpt[:, (i - 1) % 2, :, 0:n],
                               tiles, HD * (hd % 2), n)
                attention(l, "gqa")

                wuq = grid(arrived(l, "wuq")[:, 0:2 * HEADS * MLA_D], 2)
                for hd in range(HEADS):
                    dst = begin(l, "mq", hd)
                    for t in range(2):
                        for c0, c1 in segments(W):
                            mm = pe.matmul(dst[0:MLA_D, c0:c1], wuq[:, t, hd * MLA_D:(hd + 1) * MLA_D],
                                           cq[:, t, c0:c1], start=(t == 0), stop=(t == 1))
                    mm.then_inc(job_done, 1)
                for hd in range(HEADS):
                    dst = begin(l, "mqrope", hd)
                    wait_drained(pe, l, "mq", hd)
                    pe.matmul(dst[64:96, 0:LAT], rot_mla[64:96, :], mq[64:96, hd, 0:LAT], start=True, stop=True)\
                      .then_inc(job_done, 1)
                dst = begin(l, "krrope")
                pe.matmul(dst[64:96, 0:LAT], rot_mla[64:96, :], kr[64:96, 0:LAT], start=True, stop=True)\
                  .then_inc(job_done, 1)
                wukv = arrived(l, "wukv")
                for hd in range(HEADS):
                    dst = begin(l, "mk", hd)
                    for c0, c1 in segments(TOK):
                        mm = pe.matmul(dst[0:HD, c0:c1], wukv[:, hd * HD:hd * HD + HD], ckv[:, c0:c1], start=True, stop=True)
                    mm.then_inc(job_done, 1)
                for part, tiles in enumerate((range(0, 4), range(4, 6))):
                    dst = begin(l, "mv", part)
                    for i, t in enumerate(tiles):
                        mm = pe.matmul(dst[:, i * GROUP:(i + 1) * GROUP], ckv[:, t * P:(t + 1) * P],
                                       wukv[:, GROUP:2 * GROUP], start=True, stop=True)
                    mm.then_inc(job_done, 1)
                pe.wait_ge(kpe_copied, l + 1)
                wait_drained(pe, l, "mk", HEADS - 1)
                wait_drained(pe, l, "mqrope", HEADS - 1)
                attention(l, "mla")
                norm(l, "mla", ones, W)

                for m in range(KT):
                    w = tuple(halves(l, "wout", m))
                    project(begin(l, "wout", m), w, P, W, order=Y_ORDER, first=None if m else 3 * KT * l + KT)\
                        .then_inc(job_done, 1)
                norm(l, "n2", ones, W)
                j0 = 0
                for s, nj in enumerate(SETS):
                    first, s0 = plan.job[l, "ffa", j0], plan.split[l, "ffa", j0]
                    count = plan.before[first]
                    pe.wait_ge(act_drained, count["A"])
                    pe.wait_ge(dve_drained, count["V"])
                    def two_tiles(i, waits):
                        for t in range(PAIRS):
                            who = "AV"[t % 2]
                            pe.wait_ge(drained[who], count[who] - 1 + t // 2 + 2 * i)
                            pe.wait_ge(split_done, s0 + t + 1 + PAIRS * i)
                            w = tuple(grid(wsplit[:, (s0 + t) % SPLITS, part], KT) for part in range(2))
                            project(pair(first + t), w, P, W, first=waits if t == 0 else None).then_inc(job_done, 1)

                    if s == 0:
                        two_tiles(0, 3 * KT * l + 2 * KT)
                    with pe.Fori(int(s == 0), nj // 2) as i:
                        two_tiles(i, None)
                    j0 += nj
                    pe.wait_ge(u_ready, l * NF + j0)
                    for what, *i in output_schedule(l, s):
                        if what == "ffo":
                            w = tuple(halves(l, "ffo", s, i[1]))
                            project(begin(l, "ffo", s, i[1]), w, P, W, data=(uh, ul), order=range(nj)).then_inc(job_done, 1)
            norm(DEPTH, "final", ones, LAT)

        @block.scalar
        def _(act):
            def drain(*key):
                wait_job(act, *key)
                return pair(plan.job[key])

            links = [0]

            def link(ins):
                links[0] += 1
                ins.then_inc(act_chain, 1)
                act.wait_ge(act_chain, links[0])

            def round_high(s):
                key = split_keys[s]
                n = plan.granule[key]
                act.wait_ge(slot_loaded[n % RING], 16 * (n // RING + 1))
                if s >= SPLITS:
                    act.wait_ge(job_done, plan.splits[s - SPLITS] + 1)
                w = columns(key)
                act.activation(part_of(s, 0)[:, 0:w], slot(n)[:, 0:w], ACT.Copy).then_inc(high_done, 1)

            def last_norm_over(l, name):
                prev = before_norm(l, name)
                if prev:
                    act.wait_ge(job_done, plan.job[prev[0], "norm", prev[1]] + 1)
                    act.wait_ge(norm_applied, plan.norm[l, name][0])

            def square(l, name, srcs, w):
                done = plan.norm[l, name][1]
                last_norm_over(l, name)
                for t, src in enumerate(srcs):
                    act.activation(sq[:, (done + t) % 2, 0:w], src[:, 0:w], ACT.Square).then_inc(squares_ready, 1)

            def square_x(l, name, k, w):
                b = over_x(l, name)
                if k == 0:
                    last_norm_over(l, name)
                elif k > 2:
                    act.wait_ge(squares_added, (KT - 1) * b + k - 2)
                dst = sq[:, k % 2] if k else std
                act.activation(dst[:, 0:w], x[:, k, 0:w], ACT.Square).then_inc(x_squared, 1)

            def root(l, name, n, w):
                p = drain(l, "norm", name)
                if name in RECIPROCAL:
                    act.activation(std[:, 0:w], p[:, 0:w], ACT.Sqrt, bias=eps[:, :], scale=1.0 / n).then_inc(act_drained, 1)
                else:
                    link(act.activation(std[:, 0:w], p[:, 0:w], ACT.Ln, bias=eps[:, :], scale=1.0 / n))
                    act.activation(std[:, 0:w], std[:, 0:w], ACT.Exp, scale=-0.5).then_inc(act_drained, 1)

            def shift_x(l, which, w):
                at = {"n1": 0, "n2": 3 * KT}[which]
                for k in range(KT):
                    n = 3 * KT * l + SCALED[which] + k
                    act.wait_ge(h_scaled, n + 1)
                    ins = act.activation(scaled[:, k % SCALED_TILES, 0:LAT], scaled[:, k % SCALED_TILES, 0:LAT], ACT.Identity, bias=mod[:, l, at + k, 0:1])
                    if w > LAT:
                        ins = act.activation(scaled[:, k % SCALED_TILES, LAT:TOK], scaled[:, k % SCALED_TILES, LAT:TOK], ACT.Identity, bias=mod[:, l, at + k, 1:2])
                    ins.then_inc(h_shifted, 1)

            def high_output(l, n):
                t, w = Y_ORDER[n], width(l)
                act.wait_ge(h_scaled, 3 * KT * l + KT + n + 1)
                act.activation(hh[:, t, 0:w], y[:, t, 0:w], ACT.Copy).then_inc(h_rounded, 1)

            def attention(l, kind, tile0, scale):
                for job, un in attention_steps(l, kind):
                    if job == "square":
                        if un == "gqa":
                            wait_drained(act, l, "pv", *attention_units(l, "gqa")[-1])
                        square(l, un, [y[:, t] for t in OUTPUTS[un]], width(l))
                    elif job == "norm":
                        root(l, un, HD if un in ("ret0", "ret1") else GROUP, width(l))
                    elif job == "high":
                        high_output(l, un)
                    if job not in ("s", "t", "pv"):
                        continue
                    _, net, hd, t = un
                    n = plan.unit[(l,) + un]
                    p = drain(l, job, *un)
                    if job == "s":
                        wide = TOK if net == "lat" else CTX
                        act.wait_ge(nmax_ready, n + 1)
                        if n >= 3:
                            prev = next(k for k in plan.unit if plan.unit[k] == n - 3)
                            wait_job(act, prev[0], "t", *prev[1:])
                        act.activation(prob[kind][:, n % 3, 0:wide], p[:, 0:wide], ACT.Exp, bias=nmax[:, n:n + 1],
                                       scale=scale, accum_out=rsum[:, n:n + 1]).then_inc(act_drained, 1)
                    elif job == "t":
                        wide = TOK if net == "lat" else CTX
                        act.activation(pt[kind][:, n % 2, 0:wide], p[:, 0:wide], ACT.Copy).then_inc(act_drained, 1)
                    else:
                        base, c = HD * (hd % 2), NET_AT[net] + P * t
                        act.activation(y[base:base + HD, tile0 + hd // 2, c:c + P], p[base:base + HD, 0:P],
                                       ACT.Copy).then_inc(act_drained, 1)

            act.dma_start(cond, a["cond"]).then_inc(cond_loaded, 16)
            act.dma_start(par[:, :, :], a["par"]).then_inc(cond_loaded, 16)
            act.dma_start(x[:, :, :], a["x"]).then_inc(x_loaded, 16)
            for dst, name in ((ident, "ident"), (rot, "rot"), (rot_mla, "rot_mla"), (blk, "blk"),
                              (cs, "cs"), (zt_cs, "zt_cs"), (negt, "negt"), (g_final, "g_final"), (w_small, "w_small")):
                act.dma_start(dst[tuple(slice(None) for _ in dst.shape)], a[name]).then_inc(const_loaded, 16)

            act.wait_ge(cond_loaded, 32)
            act.activation(cond, cond, ACT.Silu).then_inc(cond_ready, 1)
            act.wait_ge(x_loaded, 16)
            act.wait_ge(ones_set, 2)
            for l in range(DEPTH):
                W = width(l)
                for k in range(0 if l else KT):
                    square_x(l, "n1", k, TOK)
                root(l, "n1", D, TOK)
                shift_x(l, "n1", TOK)
                if l == 0:
                    round_high(0)
                    round_high(1)
                at = PARAM["decay"][0]
                link(act.activation(lg[:, 1, :], par[:, l, at:at + 8], ACT.Abs))
                act.activation(lg[:, 2, :], lg[:, 1, :], ACT.Exp, scale=-1.0).then_inc(log_part, 1)
                act.wait_ge(log_ready, 2 * l + 1)
                act.activation(lg[:, 4, :], lg[:, 3, :], ACT.Ln).then_inc(log_part, 1)
                for what, i in input_schedule(l):
                    if what == "win":
                        name = WIN[i]
                        p = drain(l, "win", i)
                        w = win_width(l, name)
                        dst = inputs[name]
                        if name[:2] == "hy":
                            g = int(name[2])
                            act.activation(dst[:, 0:W], p[:, 0:W], ACT.Identity, bias=param(l, "conv_b", g),
                                           scale=param(l, "conv_w", 6 + g)).then_inc(conv_part, 1)
                        else:
                            rows = slice(64, 96) if name == "kr" else slice(0, P)
                            act.activation(dst[rows, 0:w], p[rows, 0:w], ACT.Silu if name[:4] == "retg" else ACT.Copy,
                                           scale=RET_K_SCALE if name[:4] == "retk" else 1.0).then_inc(act_drained, 1)
                        if i + SPLITS < N_WIN:
                            round_high(plan.split[l, "win", i] + SPLITS)
                    elif what == "vturn":
                        p = drain(l, "vturn", i)
                        act.activation(by_token[VALUES[i]], p[:, 0:TOK].rearrange("p (t c) -> p t c", t=6), ACT.Copy)\
                           .then_inc(act_drained, 1)
                    elif what == "square":
                        tiles = ("cq0", "cq1") if i == "cq" else (i,)
                        wait_drained(act, l, "win", WIN.index(tiles[-1]))
                        square(l, i, [inputs[name] for name in tiles], win_width(l, i))
                    elif what == "norm":
                        root(l, i, {"cq": GROUP, "ckv": P}.get(i, HD), win_width(l, i))
                    elif what == "mlp":
                        act.wait_ge(angle_ready, 3 * l + i + 1)
                        act.activation(hb[0:HY_FFN, 0:W], ht[0:HY_FFN, 0:W], ACT.Sin).then_inc(sin_ready, 1)
                wait_job(act, l, "win", N_WIN - 1)
                act.dma_start(w4[0:HY_FFN], a["w4"][l]).then_inc(filter_loaded, 16)
                act.dma_start(absd, a["absd"]).then_inc(filter_loaded, 16)
                act.wait_ge(filter_loaded, 32 * (l + 1))
                s = 6 * l
                tiles = [(net, t) for net in nets(l) for t in range(NET_LEN[net] // P)]

                def decay(i):
                    net, t = tiles[i]
                    if i >= 2:
                        act.wait_ge(filt_ready, s + i - 1)
                    tt = t + (4 if net == "ctx" else 0)
                    act.activation(edec[:, i % 2], absd, ACT.Exp, scale=negt[:, tt:tt + 1]).then_inc(decay_ready, 1)

                decay(0)
                for i in range(len(tiles)):
                    if i + 1 < len(tiles):
                        decay(i + 1)
                    act.wait_ge(ab_ready, s + i + 1)
                    act.activation(filt[:, i % 2], filt[:, i % 2], ACT.Abs).then_inc(abs_ready, 1)
                for net in nets(l):
                    nt = NET_LEN[net] // P
                    for o in range(2):
                        p = drain(l, "turn", net, o)
                        act.activation(vtok[:, 0:nt], p[:, 0:nt * GROUP].rearrange("p (t c) -> p t c", t=nt), ACT.Copy)\
                           .then_inc(act_drained, 1)
                wait_drained(act, l, "inv", nets(l)[-1], 1)
                act.dma_start(delta, a["delta"]).then_inc(delta_loaded, 16)
                act.wait_ge(delta_loaded, 16 * (l + 1))
                units = retention_units(l)

                def table(hd):
                    act.wait_ge(dec_arg, HEADS * l + hd + 1)
                    link(act.activation(dec[:, hd % 2, 0:896], dec[:, hd % 2, 0:896], ACT.Exp))
                    act.activation(dec[:, hd % 2, 896:1536], delta[:, 256:896], ACT.Exp, bias=lg[:, 5, hd:hd + 1],
                                   scale=lg[:, 0, hd:hd + 1])
                    act.activation(sq[:, 0, 0:640], delta[:, 256:896], ACT.Exp, bias=lg[:, 5, 4 + hd:5 + hd],
                                   scale=lg[:, 1, 4 + hd:5 + hd]).then_inc(dec_exp, 1)

                table(0)
                for net, hd in units:
                    if net == "lat" and hd + 1 < HEADS:
                        table(hd + 1)
                    base, c, m = HD * (hd % 2), NET_AT[net], NET_LEN[net]
                    p = drain(l, "rpv", net, hd)
                    act.activation(y[base:base + HD, 4 + hd // 2, c:c + m], p[base:base + HD, 0:m], ACT.Copy)\
                       .then_inc(act_drained, 1)
                wait_drained(act, l, "rpv", *units[-1])
                attention(l, "gqa", 6, GQA_SCALE)
                for hd in range(HEADS):
                    p = drain(l, "mq", hd)
                    act.activation(mq[0:MLA_D, hd, 0:W], p[0:MLA_D, 0:W], ACT.Copy).then_inc(act_drained, 1)
                for hd in range(HEADS):
                    p = drain(l, "mk", hd)
                    act.activation(mk[0:HD, hd, :], p[0:HD, 0:TOK], ACT.Copy).then_inc(act_drained, 1)
                for part, (t0, t1) in enumerate(((0, 4), (4, 6))):
                    p = drain(l, "mv", part)
                    act.activation(vmla[:, t0:t1], p[:, 0:(t1 - t0) * GROUP].rearrange("p (t c) -> p t c", c=GROUP), ACT.Copy)\
                       .then_inc(act_drained, 1)
                act.wait_ge(norm_applied, plan.norm[l, "ret1"][0] + 1)
                s = plan.split[l, "wout", 0]
                round_high(s)
                round_high(s + 1)
                attention(l, "mla", 2, MLA_SCALE)
                wait_drained(act, l, "pv", *attention_units(l, "mla")[-1])
                square(l, "mla", [y[:, 2], y[:, 3]], W)
                root(l, "mla", GROUP, W)
                high_output(l, KT - 2)
                high_output(l, KT - 1)
                for m in range(KT):
                    wait_job(act, l, "wout", m)
                    if m == KT - SPLITS:
                        act.wait_ge(h_ready, 3 * KT * l + 2 * KT)
                    round_high(s + m + SPLITS)
                    if m:
                        wait_drained(act, l, "wout", m - 1)
                        square_x(l, "n2", m - 1, W)
                    if m == 2 and l < DEPTH - 1:
                        act.wait_ge(h_ready, 3 * KT * l + 2 * KT)
                        act.dma_start(cond, a["cond"]).then_inc(cond_loaded, 16)
                wait_drained(act, l, "wout", KT - 1)
                square_x(l, "n2", KT - 1, W)
                root(l, "n2", D, W)
                shift_x(l, "n2", W)
                after = "n1" if l + 1 < DEPTH else "final"
                if l < DEPTH - 1:
                    act.wait_ge(cond_loaded, 16 * (l + 3))
                    act.activation(cond, cond, ACT.Silu).then_inc(cond_ready, 1)
                j0 = 0
                for st, nj in enumerate(SETS):
                    first, s0 = plan.job[l, "ffa", j0], plan.split[l, "ffa", j0]
                    g0 = plan.granule[l, "ffa", j0]
                    used = plan.before[first]["V"]

                    def gates(i, last):
                        for t in range(PAIRS):
                            act.wait_ge(job_done, first + t + 1 + PAIRS * i)
                            if t % 2 == 0:
                                act.wait_ge(dve_drained, used + t // 2 - 1 + 2 * i)
                                act.activation(sq[:, t // 2, 0:W], pair(first + t)[:, 0:W], ACT.Silu).then_inc(act_drained, 1)
                            if last and t >= PAIRS - SPLITS:
                                round_high(plan.split[l, "ffo", st, t - (PAIRS - SPLITS)])
                            else:
                                g = g0 + t + SPLITS
                                act.wait_ge(slot_loaded[g % RING], 16 * (g // RING + 1) + 16 * i)
                                act.activation(wsplit[:, (s0 + t) % SPLITS, 0], slot(g), ACT.Copy).then_inc(high_done, 1)

                    with act.Fori(0, nj // 2 - 1) as i:
                        gates(i, False)
                    gates(nj // 2 - 1, True)
                    j0 += nj
                    for what, *i in output_schedule(l, st):
                        if what == "ffo":
                            m = i[1]
                            wait_job(act, l, "ffo", st, m)
                            nxt = plan.split[l, "ffo", st, m] + SPLITS
                            if nxt < len(plan.splits):
                                round_high(nxt)
                            if st == len(SETS) - 1:
                                for k in (m - 1, m) if m == KT - 1 else (m - 1,) if m else ():
                                    wait_drained(act, l, "ffo", st, k)
                                    square_x(l + 1, after, k, TOK if l + 1 < DEPTH else LAT)
            root(DEPTH, "final", D, LAT)

        @block.gpsimd
        def _(pool):
            pool.memset(ones[:, :], 1.0).then_inc(ones_set, 1)
            pool.memset(eps[:, :], EPS).then_inc(ones_set, 1)

            def low(dst, exact, high):
                return pool.tensor_tensor(dst, exact, high.bitcast(F32), ALU.subtract)

            def split_low(s):
                key = split_keys[s]
                n, w = plan.granule[key], columns(key)
                pool.wait_ge(high_done, s + 1)
                low(part_of(s, 1)[:, 0:w], slot(n)[:, 0:w], part_of(s, 0)[:, 0:w]).then_inc(split_done, 1)

            def add_square(l, name, k, w):
                b = over_x(l, name)
                pool.wait_ge(x_squared, KT * b + k + 1)
                if k > 1:
                    pool.wait_ge(squares_added, (KT - 1) * b + k - 1)
                pool.tensor_tensor(std[:, 0:w], std[:, 0:w], sq[:, k % 2, 0:w], ALU.add).then_inc(squares_added, 1)

            def both_parts(l, which, w):
                for k in range(KT):
                    h = scaled[:, k % SCALED_TILES, 0:w]
                    pool.wait_ge(h_shifted, KT * over_x(l, which) + k + 1)
                    pool.tensor_copy(hh[:, k, 0:w], h).then_inc(h_high, 1)
                    pool.wait_ge(h_high, KT * over_x(l, which) + k + 1)
                    low(hl[:, k, 0:w], h, hh[:, k, 0:w]).then_inc(h_ready, 1)

            def low_output(l, n):
                t, w = Y_ORDER[n], width(l)
                pool.wait_ge(h_rounded, KT * l + n + 1)
                low(hl[:, t, 0:w], y[:, t, 0:w], hh[:, t, 0:w]).then_inc(h_ready, 1)

            parts = 0
            for l in range(DEPTH):
                W = width(l)
                for k in range(1, 1 if l else KT):
                    add_square(l, "n1", k, TOK)
                both_parts(l, "n1", TOK)
                for s in range(0 if l else SPLITS):
                    split_low(s)
                for i in range(N_WIN - SPLITS):
                    split_low(plan.split[l, "win", i] + SPLITS)
                s = 6 * l
                i = 0
                for ni, net in enumerate(nets(l)):
                    if ni:
                        wait_job(pool, l, "l1", nets(l)[0])
                    for t in range(NET_LEN[net] // P):
                        pool.wait_ge(abs_ready, s + 1)
                        f = filt[:, i % 2]
                        if t == 0:
                            pool.tensor_tensor(sumabs, f[:, 0:512], f[:, 512:1024], ALU.add).then_inc(abs_part, 1)
                            parts += 1
                        else:
                            for half in range(2):
                                pool.tensor_tensor(sumabs, sumabs, f[:, half * 512:half * 512 + 512], ALU.add).then_inc(abs_part, 1)
                                parts += 1
                                if not half:
                                    pool.wait_ge(abs_part, parts)
                        pool.wait_ge(abs_part, parts)
                        pool.engine_nop().then_inc(abs_summed, 1)
                        i += 1
                        s += 1
                    pool.engine_nop().then_inc(sumabs_ready, 1)
                pool.wait_ge(kpe_ready, l + 1)
                for hd in range(HEADS):
                    ins = pool.tensor_copy(mk[64:96, hd, :], kr[64:96, :])
                ins.then_inc(kpe_copied, 1)
                pool.wait_ge(kpe_copied, l + 1)
                s = plan.split[l, "wout", 0]
                for i in range(SPLITS):
                    split_low(s + i)
                for n in range(KT):
                    low_output(l, n)
                for m in range(KT):
                    split_low(s + m + SPLITS)
                    if m > 1:
                        add_square(l, "n2", m - 1, W)
                add_square(l, "n2", KT - 1, W)
                both_parts(l, "n2", W)
                j0 = 0
                for st, nj in enumerate(SETS):
                    s0, g0 = plan.split[l, "ffa", j0], plan.granule[l, "ffa", j0]

                    def granules(i, last):
                        for t in range(PAIRS):
                            if last and t >= PAIRS - SPLITS:
                                split_low(plan.split[l, "ffo", st, t - (PAIRS - SPLITS)])
                            else:
                                pool.wait_ge(high_done, s0 + t + SPLITS + 1 + PAIRS * i)
                                part = wsplit[:, (s0 + t) % SPLITS]
                                low(part[:, 1], slot(g0 + t + SPLITS), part[:, 0]).then_inc(split_done, 1)

                    with pool.Fori(0, nj // 2 - 1) as i:
                        granules(i, False)
                    granules(nj // 2 - 1, True)
                    j0 += nj
                    for m in range(KT):
                        nxt = plan.split[l, "ffo", st, m] + SPLITS
                        if nxt < len(plan.splits):
                            split_low(nxt)
                        if st == len(SETS) - 1:
                            after, w = ("n1", TOK) if l + 1 < DEPTH else ("final", LAT)
                            for k in (m - 1, m) if m == KT - 1 else (m - 1,) if m > 1 else ():
                                add_square(l + 1, after, k, w)

        @block.vector
        def _(dve):
            def drain(*key):
                wait_job(dve, *key)
                return pair(plan.job[key])

            links = [0]

            def link(ins, turns=0):
                links[0] += 1
                ins.then_inc(dve_chain, 1)
                dve.wait_ge(dve_chain, links[0] + turns)

            def signal(what):
                dve.engine_nop().then_inc(what, 1)

            def modulation(l, j):
                n, m = plan.granule[l, "mod", j], l * N_MOD + j
                dve.wait_ge(slot_loaded[n % RING], 16 * (n // RING + 1))
                if m:
                    dve.wait_ge(mod_done, m)
                for c, products in ((0, unused), (1, slot(n))):
                    ins = dve.tensor_tensor_reduce(products, slot(n), cond[:, c], 1.0, param(l, "b_mod", j), ALU.mult, ALU.add,
                                                   accum_out=mod[:, l, j, c:c + 1])
                ins.then_inc(mod_done, 1)

            def scales(l, name, w):
                n = plan.job[l, "norm", name]
                dve.wait_ge(act_drained, plan.before[n]["A"] + 1)
                if name in RECIPROCAL:
                    link(dve.reciprocal(std[:, 0:w], std[:, 0:w]))

            def norm(l, name, tiles, gains, w, gate=None, into=None):
                scales(l, name, w)
                for t, g, dst in zip(tiles, gains, into or tiles):
                    ins = dve.scalar_tensor_tensor(dst[:, 0:w], t[:, 0:w], g, std[:, 0:w], ALU.mult, ALU.mult)
                    if gate is not None:
                        link(ins)
                        ins = dve.tensor_tensor(t[:, 0:w], t[:, 0:w], gate[:, 0:w], ALU.mult)
                ins.then_inc(norm_applied, 1)

            def group_norm(l, name, w):
                scales(l, name, w)
                for t in OUTPUTS[name]:
                    dve.scalar_tensor_tensor(y[:, t, 0:w], y[:, t, 0:w], param(l, "g_out", t), std[:, 0:w],
                                             ALU.mult, ALU.mult).then_inc(h_scaled, 1)
                dve.wait_ge(h_scaled, 3 * KT * l + KT + Y_ORDER.index(OUTPUTS[name][1]) + 1)
                signal(norm_applied)

            def scale_x(l, which, w):
                scales(l, which, w)
                base = 3 * KT * l + SCALED[which]
                segs = [(0, 0, LAT), (1, LAT, TOK)][:1 + (w > LAT)]

                for k in range(KT):
                    if k >= SCALED_TILES:
                        dve.wait_ge(h_ready, base + k - SCALED_TILES + 1)
                    for s, c0, c1 in segs:
                        ins = dve.scalar_tensor_tensor(scaled[:, k % SCALED_TILES, c0:c1], x[:, k, c0:c1],
                                                       gain[:, int(which == "n2"), k, s:s + 1], std[:, c0:c1],
                                                       ALU.mult, ALU.mult)
                    ins.then_inc(h_scaled, 1)
                dve.wait_ge(h_scaled, base + KT)
                signal(norm_applied)

            def gains(l, which):
                name, at = (("g_attn", KT), ("g_ffn", 4 * KT))[which]
                g0 = PARAM[name][0]
                link(dve.scalar_tensor_tensor(gain[:, which], mod[:, l, at:at + KT, :], 1.0,
                                              par[:, l, g0:g0 + KT, None].to_broadcast([P, KT, 2]), ALU.add, ALU.mult))

            def attention(l, kind, scale):
                for job, un in attention_steps(l, kind):
                    if job == "norm":
                        if un in ("ret0", "ret1"):
                            i = int(un[3])
                            norm(l, un, [y[:, 4 + i]], [param(l, "g_ret", i)], width(l), gate=retg[:, i])
                        else:
                            group_norm(l, un, width(l))
                    elif job == "s":
                        n = plan.unit[(l,) + un]
                        wide = TOK if un[1] == "lat" else CTX
                        p = drain(l, "s", *un)
                        link(dve.reduce_max(smax[:, n:n + 1], p[:, 0:wide], AX))
                        dve.tensor_scalar(nmax[:, n:n + 1], smax[:, n:n + 1], -scale, None, ALU.mult).then_inc(nmax_ready, 1)
                    elif job == "scale":
                        n = plan.unit[(l,) + un]
                        wide = TOK if un[1] == "lat" else CTX
                        wait_drained(dve, l, "s", *un)
                        link(dve.reciprocal(rinv[:, n:n + 1], rsum[:, n:n + 1]))
                        dve.tensor_scalar(prob[kind][:, n % 3, 0:wide], prob[kind][:, n % 3, 0:wide], rinv[:, n:n + 1], None, ALU.mult)\
                           .then_inc(prob_ready, 1)

            def residual(l, m, at, w, *key):
                p = drain(l, *key)
                for s, (c0, c1) in enumerate(((0, LAT), (LAT, TOK))[:1 + (w > LAT)]):
                    ins = dve.scalar_tensor_tensor(x[:, m, c0:c1], p[:, c0:c1], mod[:, l, at + m, s:s + 1], x[:, m, c0:c1],
                                                   ALU.mult, ALU.add)
                ins.then_inc(dve_drained, 1)

            def rotate(src, dst_ps, table, rows):
                dve.tensor_tensor(src[rows, 0:LAT], src[rows, 0:LAT], table[rows, 0, :], ALU.mult)
                link(dve.tensor_tensor(turned[rows, :], dst_ps[rows, 0:LAT], table[rows, 1, :], ALU.mult))
                link(dve.tensor_tensor(src[rows, 0:LAT], src[rows, 0:LAT], turned[rows, :], ALU.add))

            dve.wait_ge(cond_loaded, 32)
            dve.wait_ge(cond_ready, 1)
            for j in range(MOD_FIRST):
                modulation(0, j)
            dve.wait_ge(const_loaded, 16 * N_CONST)
            for l in range(DEPTH):
                W = width(l)
                dve.wait_ge(mod_done, l * N_MOD + (N_MOD if l else MOD_FIRST))
                gains(l, 0)
                scale_x(l, "n1", TOK)
                at = PARAM["decay"][0]
                dve.wait_ge(log_part, 2 * l + 1)
                dve.tensor_scalar(lg[:, 3, :], lg[:, 2, :], 1.0, None, ALU.add).then_inc(log_ready, 1)
                dve.wait_ge(log_part, 2 * l + 2)
                link(dve.tensor_scalar(lg[:, 0, :], par[:, l, at:at + 8], 0.0, None, ALU.min))
                link(dve.tensor_tensor(lg[:, 0, :], lg[:, 0, :], lg[:, 4, :], ALU.subtract))
                dve.tensor_scalar(lg[:, 1, :], lg[:, 0, :], -1.0, None, ALU.mult)
                dve.tensor_scalar(lg[:, 5, 0:4], lg[:, 0, 0:4], float(CTX), None, ALU.mult)
                link(dve.tensor_scalar(lg[:, 5, 4:8], lg[:, 0, 4:8], float(LAT), None, ALU.mult))
                signal(log_ready)
                for what, i in input_schedule(l):
                    if what == "win":
                        name = WIN[i]
                        if name[:2] == "hy":
                            g = int(name[2])
                            p = drain(l, "win", i)
                            dve.wait_ge(conv_part, 6 * l + g + 1)
                            for net in nets(l):
                                c0, c1 = NET_AT[net], NET_AT[net] + NET_LEN[net]
                                link(dve.scalar_tensor_tensor(hy[:, g, c0 + 1:c1], p[:, c0:c1 - 1], param(l, "conv_w", g),
                                                              hy[:, g, c0 + 1:c1], ALU.mult, ALU.add))
                                ins = dve.scalar_tensor_tensor(hy[:, g, c0:c1 - 1], p[:, c0 + 1:c1], param(l, "conv_w", 12 + g),
                                                               hy[:, g, c0:c1 - 1], ALU.mult, ALU.add)
                            ins.then_inc(dve_drained, 1)
                    elif what == "mod":
                        modulation(l, i)
                    elif what == "norm":
                        tiles, gs = {"cq": (("cq0", "cq1"), ("g_q", "g_q")), "ckv": (("ckv",), ("g_kv",)),
                                     "gk": (("gk",), ("g_gk",))}.get(i, ((i,), ("g_gq",)))
                        norm(l, i, [inputs[t] for t in tiles],
                             [param(l, g, n if i == "cq" else 0) for n, g in enumerate(gs)], win_width(l, i))
                    elif what == "rope":
                        rotate(inputs[i], drain(l, "rope", i), cs, slice(0, P))
                        signal(dve_drained)
                    elif what == "mlp":
                        p = drain(l, "mlp", i)
                        rows = slice(0, HY_FFN)
                        link(dve.tensor_scalar(ha[rows, 0:W], p[rows, 0:W], param(l, f"b{i + 1}")[rows], param(l, "freq")[rows],
                                               ALU.add, ALU.mult))
                        if i:
                            dve.wait_ge(sin_ready, 3 * l + i)
                        link(dve.tensor_scalar(ht[rows, 0:W], ha[rows, 0:W], INV_2PI, MAGIC, ALU.mult, ALU.add))
                        link(dve.tensor_scalar(ht[rows, 0:W], ht[rows, 0:W], MAGIC, None, ALU.subtract))
                        link(dve.scalar_tensor_tensor(ha[rows, 0:W], ht[rows, 0:W], -TWO_PI_HI, ha[rows, 0:W], ALU.mult, ALU.add))
                        link(dve.scalar_tensor_tensor(ht[rows, 0:W], ht[rows, 0:W], -TWO_PI_LO, ha[rows, 0:W], ALU.mult, ALU.add))
                        link(dve.tensor_scalar(ht[rows, 0:W], ht[rows, 0:W], PI_BELOW, -PI_BELOW, ALU.min, ALU.max))
                        signal(angle_ready)
                        signal(dve_drained)
                if l == 0:
                    dve.wait_ge(mod_done, N_MOD)
                wait_job(dve, l, "win", N_WIN - 1)
                i = 0
                for net in nets(l):
                    nt = NET_LEN[net] // P
                    for t in range(nt):
                        s = 6 * l + i
                        p = drain(l, "filt", net, t)
                        dve.wait_ge(decay_ready, s + 1)
                        if i >= 2:
                            dve.wait_ge(abs_summed, s - 1)
                        f = filt[:, i % 2]
                        link(dve.scalar_tensor_tensor(f, edec[:, i % 2], 0.05, p, ALU.add, ALU.mult))
                        if t == 0:
                            link(dve.memset(f[0:1, 512:1024], 0.0))
                        signal(filt_ready)
                        signal(dve_drained)
                        if t == 0 and net != "lat":
                            wait_job(dve, l, "nyq", "lat")
                        link(dve.tensor_tensor(fa[:, t], f[:, 0:512], f[:, 512:1024], ALU.add))
                        dve.tensor_tensor(fb[:, t], f[:, 0:512], f[:, 512:1024], ALU.subtract).then_inc(ab_ready, 1)
                        i += 1
                    p = drain(l, "l1", net)
                    link(dve.reciprocal(rn, p[:, 0:512]))
                    signal(dve_drained)
                    for q in range(nt):
                        p = drain(l, "spec", net, q)
                        link(dve.tensor_tensor(spec[net][:, q], p.rearrange("p (a b) -> p a b", a=2),
                                               rn[:, None, :].to_broadcast([P, 2, HY_COLS]), ALU.mult))
                        signal(dve_drained)
                    p = drain(l, "nyq", net)
                    link(dve.tensor_tensor(spec[net][0:1, 0, 1, :], p[0:1, 0:512], rn[0:1, :], ALU.mult))
                    signal(dve_drained)
                for net in nets(l):
                    n, c = NET_LEN[net], NET_AT[net]
                    nt = n // P
                    for o in range(2):
                        for i in range(nt // 2):
                            p = drain(l, "fwd", net, o, i)
                            ur, ui = (p[:, q * 512:q * 512 + 512].rearrange("p (a b) -> p a b", a=2) for q in range(2))
                            kre, kim = (spec[net][:, 2 * i:2 * i + 2, q, o * GROUP:(o + 1) * GROUP] for q in range(2))
                            yr, yi = yf[:, 2 * i:2 * i + 2], yf[:, nt + 2 * i:nt + 2 * i + 2]
                            dve.tensor_tensor(yr, ur, kre, ALU.mult)
                            dve.tensor_tensor(tmp0, ui, kim, ALU.mult)
                            dve.tensor_tensor(yi, ur, kim, ALU.mult)
                            link(dve.tensor_tensor(tmp1, ui, kre, ALU.mult))
                            dve.tensor_tensor(yr, yr, tmp0, ALU.subtract)
                            link(dve.tensor_tensor(yi, yi, tmp1, ALU.add))
                            if i == 0:
                                dve.tensor_tensor(yr[0:1, 0], ur[0:1, 0], kre[0:1, 0], ALU.mult)
                                link(dve.tensor_tensor(yi[0:1, 0], ui[0:1, 0], kim[0:1, 0], ALU.mult))
                            signal(dve_drained)
                        signal(spectrum_ready)
                        p = drain(l, "inv", net, o)
                        for ch in range(2):
                            v = hy[:, ch, c:c + n]
                            gate = hy[:, 2 + 2 * o + ch, c:c + n]
                            dst = y[:, ch, c:c + n] if o else v
                            link(dve.scalar_tensor_tensor(v, v, param(l, "hy_bias", 2 * o + ch), p[:, ch * 512:ch * 512 + n],
                                                          ALU.mult, ALU.add))
                            link(dve.tensor_tensor(dst, v, gate, ALU.mult))
                        signal(dve_drained)

                def arguments(hd):
                    t = dec[:, hd % 2]
                    link(dve.tensor_scalar(t[:, 0:896], delta, 0.0, lg[:, 0, hd:hd + 1], ALU.max, ALU.mult))
                    link(dve.tensor_scalar(sq[:, 1, 0:768], delta[:, 0:768], 0.0, lg[:, 1, 4 + hd:5 + hd], ALU.min, ALU.mult))
                    link(dve.tensor_tensor(t[:, 0:768], t[:, 0:768], sq[:, 1, 0:768], ALU.add))
                    signal(dec_arg)

                def finish(hd):
                    t = dec[:, hd % 2]
                    dve.wait_ge(dec_exp, HEADS * l + hd + 1)
                    link(dve.tensor_tensor(t[:, 384:512], t[:, 384:512], ident[:, :], ALU.add))
                    link(dve.tensor_tensor(t[:, 896:1536], t[:, 896:1536], sq[:, 0, 0:640], ALU.add))

                dve.wait_ge(delta_loaded, 16 * (l + 1))
                arguments(0)
                units = retention_units(l)
                for n, (net, hd) in enumerate(units):
                    if net == "lat":
                        finish(hd)
                        if hd + 1 < HEADS:
                            if hd:
                                wait_drained(dve, l, "rs", nets(l)[-1], hd - 1, 2 if W == LAT else 0)
                            arguments(hd + 1)
                    m = NET_LEN[net]
                    tiles = list(range(6)) if net == "lat" else [4, 5]
                    for part in range(len(tiles) // 2):
                        p = drain(l, "rs", net, hd, part)
                        for q in range(2):
                            kt = tiles[2 * part + q]
                            if net == "lat" and kt >= 4:
                                at = 896 + 384 - 256 - P * (kt - 4)
                            elif net == "lat":
                                at = 384 - P * kt
                            else:
                                at = 384 - P * (kt - 4)
                            ins = dve.tensor_tensor(rpt[:, n % 2, 2 * part + q, 0:m], p[:, q * 512:q * 512 + m],
                                                    dec[:, hd % 2, at:at + m], ALU.mult)
                        ins.then_inc(dve_drained, 1)
                attention(l, "gqa", GQA_SCALE)
                rows = slice(64, 96)
                for hd in range(HEADS):
                    rotate(mq[:, hd], drain(l, "mqrope", hd), cs_mla, rows)
                    signal(dve_drained)
                rotate(kr, drain(l, "krrope"), cs_mla, rows)
                signal(kpe_ready)
                signal(dve_drained)
                attention(l, "mla", MLA_SCALE)
                group_norm(l, "mla", W)
                for m in range(KT):
                    residual(l, m, 2 * KT, W, "wout", m)
                gains(l, 1)
                scale_x(l, "n2", W)
                if l < DEPTH - 1:
                    dve.wait_ge(cond_ready, l + 2)
                j0 = 0
                for st, nj in enumerate(SETS):
                    first, s0 = plan.job[l, "ffa", j0], plan.split[l, "ffa", j0]
                    g0 = plan.granule[l, "ffa", j0]
                    silus, mine = plan.before[first]["A"], plan.before[first]["V"]
                    per = 2

                    def hidden(i, turns):
                        for t in range(PAIRS):
                            if t % 2:
                                half = t // 2
                                dve.wait_ge(job_done, first + t + 1 + PAIRS * i)
                                dve.wait_ge(act_drained, silus + half + 1 + 2 * i)
                                dve.tensor_tensor(ut[:, half, 0:W], sq[:, half, 0:W], pair(first + t)[:, 0:W], ALU.mult)\
                                   .then_inc(dve_drained, 1)
                                dve.wait_ge(dve_drained, mine + half + 1 + 2 * i)
                                link(dve.tensor_copy(uh[:, half + 2 * i, 0:W], ut[:, half, 0:W]), turns)
                                dve.tensor_tensor(ul[:, half + 2 * i, 0:W], ut[:, half, 0:W],
                                                  uh[:, half + 2 * i, 0:W].bitcast(F32), ALU.subtract).then_inc(u_ready, 1)
                                dve.wait_ge(u_ready, l * NF + j0 + half + 1 + 2 * i)

                    with dve.Fori(0, nj // 2) as i:
                        hidden(i, per * i)
                    links[0] += per * (nj // 2 - 1)
                    j0 += nj
                    for what, *i in output_schedule(l, st):
                        if what == "mod":
                            modulation(l + 1, i[0])
                        else:
                            residual(l, i[1], 5 * KT, W, "ffo", st, i[1])
            norm(DEPTH, "final", [x[:, k] for k in range(KT)], [g_final[:, k:k + 1] for k in range(KT)], LAT,
                 into=[y[:, k] for k in range(KT)])


N_CONST = 9


def constants():
    f = np.float32
    c = {"ident": np.eye(P), "blk": np.kron(np.eye(2), np.ones((HD, HD)))}
    def turn(n):
        r = np.zeros((n, n))
        for m in range(n // 2):
            r[m + n // 2, m] = -1.0
            r[m, m + n // 2] = 1.0
        return r
    c["rot"] = np.kron(np.eye(2), turn(HD))
    c["rot_mla"] = np.zeros((P, MLA_ROPE))
    c["rot_mla"][64:96] = turn(MLA_ROPE)
    c["delta"] = np.arange(896)[None, :] - np.arange(P)[:, None] - 384.0

    def rope(dim):
        q = dim // 4
        inv = THETA ** (-np.arange(q) / q)
        tok = np.arange(LAT)
        ang = np.concatenate([inv[:, None] * (tok // GRID_W)[None], inv[:, None] * (tok % GRID_W)[None]])
        ang = np.concatenate([ang, ang])
        return np.stack([np.cos(ang), np.sin(ang)], 1)

    c["cs"] = np.tile(rope(HD), (2, 1, 1))
    bands = (HY_EMB - 1) // 2
    fb = np.linspace(1e-4, bands - 1, bands)
    zt, negt = np.zeros((P, TOK)), np.zeros((P, 6))
    for net, n in NET_LEN.items():
        t = np.linspace(0.0, 1.0, n)
        w = 2.0 * np.pi * np.arange(n) / n
        at = NET_AT[net]
        zt[0, at:at + n] = t
        zt[1:1 + bands, at:at + n] = np.cos(fb[:, None] * w)
        zt[1 + bands:HY_EMB, at:at + n] = -np.sin(fb[:, None] * w)
        negt[:, at // P:(at + n) // P] = -t.reshape(-1, P).T
        tk, fr = np.arange(n)[:, None], np.arange(n)[None, :]
        ang = np.pi * tk * fr / n
        im = -np.sin(ang)
        im[:, 0] = (-1.0) ** np.arange(n)
        fwd = np.concatenate([np.cos(ang), im], 1)
        scale = np.full((2 * n, 1), 2.0)
        scale[0] = scale[n] = 1.0
        inv = fwd.T * scale / (2 * n)
        if net == "lat":
            c["dft_lat"] = np.concatenate([fwd.reshape(4, P, 2 * n),
                                           inv.reshape(4, 2, P, n).transpose(0, 2, 1, 3).reshape(4, P, 2 * n)])
        else:
            c["dft_ctx"] = np.stack([fwd.reshape(2, P, 2 * n).transpose(1, 0, 2).reshape(P, 4 * n),
                                     inv.reshape(4, P, n).transpose(1, 0, 2).reshape(P, 4 * n)])
    c["zt_cs"], c["negt"] = np.zeros((P, 2 * LAT)), negt
    c["zt_cs"][0:HY_EMB, 0:TOK] = zt[0:HY_EMB]
    c["zt_cs"][64:96] = rope(MLA_ROPE).reshape(MLA_ROPE, 2 * LAT)
    lo, hi = np.log(1e-2) / 0.3, np.log(1e-2) / 1.5
    dl = np.abs(np.linspace(lo, hi, 4 * GROUP)).reshape(2, 2, GROUP).transpose(1, 0, 2).reshape(1, -1)
    c["absd"] = np.tile(dl, (P, 1))
    return {k: np.ascontiguousarray(v, dtype=f) for k, v in c.items()}


def layout(v):
    f = np.float32

    def grains(w):
        k, n = w.shape[0] // P, w.shape[1] // P
        return w.reshape(k, P, n, P).transpose(2, 1, 0, 3).reshape(n, P, k * P)

    def cols(w, m):
        return w.reshape(m, P).T

    o = {}
    o["x"] = np.concatenate([v["x"][0], v["ctx"][0]]).T.reshape(KT, P, TOK).transpose(1, 0, 2)
    o["cond"] = np.tile(np.stack([v["c"][0], v["c_ctx"]]), (P, 1, 1))
    o["g_final"] = cols(v["final_norm_g"], KT)
    o["w_mod"] = np.stack([v["w_mod"][l].T.reshape(N_MOD, P, D) for l in range(DEPTH)])
    q0 = 3 * GROUP
    r0 = q0 + GROUP + P + MLA_ROPE
    g0 = r0 + 4 * GROUP
    win = []
    for l in range(DEPTH):
        w = v["w_in"][l]
        kr = np.zeros((D, P), f)
        kr[:, 64:96] = w[:, r0 - MLA_ROPE:r0]
        gq = w[:, g0:g0 + GROUP].reshape(D, 2, 2, HD).transpose(0, 2, 1, 3).reshape(D, GROUP)
        win.append(grains(np.concatenate([
            w[:, q0:q0 + GROUP + P], kr, gq, w[:, g0 + GROUP:g0 + GROUP + P], w[:, r0:r0 + 2 * GROUP],
            w[:, r0 + 3 * GROUP:g0], w[:, r0 + 2 * GROUP:r0 + 3 * GROUP], w[:, g0 + GROUP + P:g0 + GROUP + 2 * P],
            w[:, 0:q0]], 1)))
    o["w_in"] = np.stack(win)
    o["w_out"] = np.stack([grains(v["w_out"][l]) for l in range(DEPTH)])
    o["w_ffn_in"] = np.stack([grains(v["w_ffn_in"][l]).reshape(2, NF, P, D).transpose(1, 0, 2, 3).reshape(2 * NF, P, D)
                              for l in range(DEPTH)])
    o["w_ffn_out"] = np.zeros((DEPTH, len(SETS), KT, P, max(SETS) * P), f)
    for l in range(DEPTH):
        j0 = 0
        for s, nj in enumerate(SETS):
            blocks = v["w_ffn_out"][l][j0 * P:(j0 + nj) * P].reshape(nj, P, KT, P).transpose(2, 1, 0, 3)
            o["w_ffn_out"][l, s, :, :, 0:nj * P] = blocks.reshape(KT, P, nj * P)
            j0 += nj
    o["w_small"] = np.zeros((P, DEPTH, 3 * HY_FFN), f)
    o["w_small"][0:HY_EMB, :, 0:HY_FFN] = v["hy_w1"].transpose(1, 0, 2)
    o["w_small"][0:HY_FFN, :, HY_FFN:2 * HY_FFN] = v["hy_w2"].transpose(1, 0, 2)
    o["w_small"][0:HY_FFN, :, 2 * HY_FFN:] = v["hy_w3"].transpose(1, 0, 2)
    o["w4"] = v["hy_w4"].reshape(DEPTH, HY_FFN, 2, 2, GROUP).transpose(0, 1, 3, 2, 4).reshape(DEPTH, HY_FFN, 1024)
    o["wuq"] = v["mla_w_uq"].reshape(DEPTH, 2, P, HEADS * MLA_D).transpose(0, 2, 1, 3).reshape(DEPTH, P, -1)
    o["wukv"] = v["mla_w_ukv"].reshape(DEPTH, P, HEADS, 2, HD).transpose(0, 1, 3, 2, 4).reshape(DEPTH, P, 2 * GROUP)

    def pad(w):
        z = np.zeros((P, 1), f)
        z[:len(w), 0] = w
        return z

    par = np.zeros((P, DEPTH, N_PARAM), f)
    for l in range(DEPTH):
        for name, val in (
                ("b_mod", cols(v["b_mod"][l], N_MOD)), ("g_attn", cols(v["norm_attn_g"][l], KT)),
                ("g_ffn", cols(v["norm_ffn_g"][l], KT)), ("conv_b", cols(v["hy_conv_b"][l], 6)),
                ("conv_w", cols(v["hy_conv_w"][l].reshape(-1), 18)), ("hy_bias", cols(v["hy_bias"][l].reshape(-1), 4)),
                ("g_q", cols(v["mla_q_norm_g"][l], 2)), ("g_kv", cols(v["mla_kv_norm_g"][l], 1)),
                ("g_ret", cols(v["ret_norm_g"][l], 2)), ("g_out", cols(v["out_norm_g"][l], 8)),
                ("g_gq", np.tile(v["gqa_q_norm_g"][l], 2)[:, None]), ("g_gk", np.tile(v["gqa_k_norm_g"][l], 2)[:, None]),
                ("decay", np.tile(v["ret_decay"][l].reshape(1, 8), (P, 1))),
                ("b1", pad(v["hy_b1"][l])), ("b2", pad(v["hy_b2"][l])), ("b3", pad(v["hy_b3"][l])),
                ("freq", pad(v["hy_freq"][l]))):
            at, n = PARAM[name]
            par[:, l, at:at + n] = val
    o["par"] = par
    return o


def kernel(**inputs):
    import concourse.bacc as bacc
    from concourse.bass_utils import run_bass_kernel_spmd

    nc = bacc.Bacc("TRN2", target_bir_lowering=False, num_devices=1)
    arrays = {**layout({k: np.asarray(w) for k, w in inputs.items()}), **constants()}
    arrays = {f"in_{k}": np.ascontiguousarray(w) for k, w in arrays.items()}
    aps = {k[3:]: nc.dram_tensor(k, w.shape, F32, kind="ExternalInput").ap() for k, w in arrays.items()}
    out = nc.dram_tensor("out_dram", (P, KT, LAT), F32, kind="ExternalOutput").ap()
    hymba_block(nc, aps, out)
    got = run_bass_kernel_spmd(nc, [arrays], core_ids=[0]).results[0]["out_dram"]
    return np.ascontiguousarray(got.transpose(2, 1, 0).reshape(1, LAT, D))
```

```python
from contextlib import ExitStack

import numpy as np

import concourse.bass as bass
from concourse import mybir

F32 = mybir.dt.float32
F32R = mybir.dt.float32r
ACT = mybir.ActivationFunctionType
ALU = mybir.AluOpType
AX = mybir.AxisListType.X

P = 128
D = 1024
KT = D // P
LAT, CTX = 512, 256
TOK = LAT + CTX
DEPTH = 2
GRID_W = 64
EPS = 1e-6
THETA = 10000.0
GROUP = 256
DFF = 2816
NF = DFF // P
HEADS = 4
HD = 64
MLA_ROPE = 32
MLA_D = HD + MLA_ROPE
MLA_SCALE = MLA_D ** -0.5
GQA_SCALE = HD ** -0.5
RET_K_SCALE = HD ** -0.5
N_MOD = 6 * KT
HY_EMB = 33
HY_FFN = 64
HY_COLS = 2 * GROUP
NET_LEN = {"lat": LAT, "ctx": CTX}
NET_AT = {"lat": 0, "ctx": LAT}
RING = 4
SPLITS = 2
SCALED_TILES = 4
GRAN = 1024
PAIRS = 4
MAGIC = 1.5 * 2.0 ** 23
INV_2PI = 1.0 / (2.0 * np.pi)
TWO_PI_HI = 6.28125
TWO_PI_LO = 2.0 * np.pi - TWO_PI_HI
PI_BELOW = 3.1415925

PARAM = {}
for _name, _n in (("b_mod", N_MOD), ("g_attn", KT), ("g_ffn", KT), ("conv_b", 6), ("conv_w", 18),
                  ("hy_bias", 4), ("g_q", 2), ("g_kv", 1), ("g_ret", 2), ("g_out", 8), ("g_gq", 1),
                  ("g_gk", 1), ("decay", 8), ("b1", 1), ("b2", 1), ("b3", 1), ("freq", 1)):
    PARAM[_name] = (sum(n for _, n in PARAM.values()), _n)
N_PARAM = sum(n for _, n in PARAM.values())


def lay(at, *parts):
    places = {}
    for name, n in parts:
        places[name] = at
        at += n
    return places, at


AT, R2 = lay(0, ("retq", 2 * TOK), ("retk", 2 * TOK), ("retg", 2 * TOK), ("gq", 2 * TOK), ("gk", TOK),
             ("cq", 2 * TOK), ("ckv", TOK), ("kr", TOK), ("vret", 6 * GROUP), ("vgqa", 6 * P), ("hy", 6 * TOK))
_split, WORK = lay(R2, ("hh", KT * TOK), ("hl", KT * TOK), ("yraw", KT * TOK))
AT.update(_split)
AT["wsplit"] = AT["yraw"]
_hyena, _end = lay(R2, ("klat", 8 * HY_COLS), ("kctx", 4 * HY_COLS), ("scratch", 0), ("vtok_lat", 4 * GROUP),
                   ("vtok_ctx", 2 * GROUP), ("yf_lat", 8 * GROUP), ("yf_ctx", 4 * GROUP), ("t0", 512), ("t1", 512))
assert _end <= AT["yraw"]
AT.update(_hyena)
_dft, _end = lay(AT["yraw"] + 2 * TOK, ("delta", 896), ("dft_ctx", 2 * GRAN), ("", 128), ("dec0", 896 + 640))
assert _dft["dft_ctx"] <= AT["yraw"] + 4 * TOK and _dft["dec0"] == AT["yraw"] + 6 * TOK
assert _end <= WORK
AT.update(_dft)
_filt, _end = lay(AT["scratch"], ("edec", 2048), ("f", 2048), ("fa_lat", 2048), ("fb_lat", 2048), ("fa_ctx", 1024),
                  ("fb_ctx", 1024), ("absd", 1024), ("w4", 1024))
assert _end <= WORK
AT.update(_filt)
_ret, _end = lay(AT["hy"], ("rpt", 2 * 6 * LAT), ("dec1", 896 + 640))
assert _end <= AT["yraw"]
AT.update(_ret)
_gqa, _end = lay(AT["hy"], ("prob_gqa", 3 * TOK), ("pt_gqa", 2 * TOK))
assert _end <= R2
_mla, _end = lay(AT["vret"], ("mq", HEADS * TOK), ("mk", HEADS * TOK))
assert _end <= R2
_mla2, _end = lay(AT["gq"], ("vmla", 6 * GROUP), ("prob_mla", 3 * TOK), ("pt_mla", 2 * TOK))
assert _end <= AT["vret"]
AT["wsplit_out"] = AT["retq"]
assert AT["wsplit_out"] + SPLITS * 2 * GRAN <= AT["gq"]
AT["scaled"] = AT["hy"]
assert AT["scaled"] + SCALED_TILES * TOK <= R2
for _places in (_gqa, _mla, _mla2):
    AT.update(_places)
AT["cond"], AT["unused"] = AT["wsplit"] + SPLITS * 2 * GRAN, AT["vret"] + TOK
assert AT["cond"] + 2 * D <= WORK and AT["unused"] + D <= AT["hy"]
AT["ha"], AT["ht"] = AT["hy"], AT["hy"] + TOK
_ffn, _end = lay(0, ("uh", 6 * TOK), ("ul", 6 * TOK), ("ut", 2 * TOK))
assert _end <= AT["unused"]
AT.update(_ffn)

NORM_TILES = {"cq": 2, "ckv": 1, "gq0": 1, "gq1": 1, "gk": 1, "hy": 2, "mla": 2, "ret0": 1,
              "ret1": 1, "ret": 2, "gqa": 2, "n1": 0, "n2": 0, "final": 0}
TILES = (6, 4)
OUTPUTS = {"hy": (0, 1), "mla": (2, 3), "ret": (4, 5), "gqa": (6, 7), "ret0": (4,), "ret1": (5,)}
Y_ORDER = (0, 1, 4, 5, 6, 7, 2, 3)
WIN = ("cq0", "cq1", "ckv", "kr", "gq0", "gq1", "gk", "retq0", "retq1", "retk0", "retk1", "retg0", "retg1",
       "vret0", "vret1", "vgqa", "hy0", "hy1", "hy2", "hy3", "hy4", "hy5")
N_WIN = len(WIN)
VALUES = ("vret0", "vret1", "vgqa")
ALL_TOKENS = ("ckv", "kr", "gk", "retk0", "retk1") + VALUES
BETWEEN = {2: [("square", "cq")], 3: [("norm", "cq")], 4: [("square", "ckv")], 5: [("norm", "ckv"), ("mlp", 0)],
           6: [("square", "gq0")], 7: [("norm", "gq0")], 8: [("square", "gq1"), ("mlp", 1)],
           9: [("norm", "gq1"), ("rope", "retq0")], 10: [("square", "gk"), ("rope", "gq0"), ("rope", "retq1")],
           11: [("norm", "gk"), ("rope", "gq1"), ("mlp", 2)], 12: [("rope", "retk0")],
           13: [("rope", "gk"), ("rope", "retk1")], 15: [("vturn", 0)], 16: [("vturn", 1)], 17: [("vturn", 2)]}
BESIDE = {"gqa": {0: [("square", "hy")], 2: [("norm", "hy")], 3: [("square", "ret0")], 5: [("norm", "ret0")],
                  6: [("square", "ret1")], 8: [("norm", "ret1")], 9: [("square", "ret")], 11: [("norm", "ret")]},
          "mla": {0: [("square", "gqa")], 1: [("high", 0)], 2: [("norm", "gqa")], 3: [("high", 1)], 4: [("high", 2)],
                  6: [("high", 3)], 7: [("high", 4)], 9: [("high", 5)]}}
MOD_FIRST = 2 * KT
EARLY = KT - 2
LATE_BEFORE = (2, 4)
MOD_PER_SET = (14, 14, 14, 6)
G_ORDER = (0, 2, 1, 3)
RECIPROCAL = ("cq", "ckv", "gq0", "gq1", "gk")
SETS = (6, 6, 6, 4)


def mod_number(layer, j):
    return 2 * (j % KT) + j // KT if (layer, j // MOD_FIRST) == (0, 0) else layer * N_MOD + j


def nets(layer):
    return ("lat", "ctx") if layer < DEPTH - 1 else ("lat",)


def resident(layer):
    return () if layer < DEPTH - 1 else G_ORDER[:2]


def width(layer):
    return TOK if layer < DEPTH - 1 else LAT


def input_schedule(layer):
    out, j = [], MOD_FIRST
    for g in range(N_WIN):
        out.append(("win", g))
        for _ in range(min(2 if g % 2 else 3, N_MOD - j) if layer == 0 and g else 0):
            out.append(("mod", j))
            j += 1
        out += BETWEEN.get(g, [])
    return out


def output_schedule(layer, s):
    out = []
    j0, n = sum(MOD_PER_SET[:s]), MOD_PER_SET[s]
    for m in range(KT):
        out.append(("ffo", s, m))
        if layer < DEPTH - 1 and m < KT - SPLITS:
            out += [("mod", j0 + j) for j in range(m * n // (KT - SPLITS), (m + 1) * n // (KT - SPLITS))]
    return out


def attention_units(layer, kind):
    return [(kind, net, h, t) for h in range(HEADS) for net in nets(layer)
            for t in range(NET_LEN[net] // P)]


def attention_steps(layer, kind):
    units = attention_units(layer, kind)
    for i in range(len(units) + 3):
        for job, lag in (("s", 0), ("scale", 1), ("t", 2), ("pv", 3)):
            if 0 <= i - lag < len(units):
                yield job, units[i - lag]
        yield from BESIDE[kind].get(i, [])


def retention_units(layer):
    return [(net, h) for h in range(HEADS) for net in nets(layer)]


class Plan:

    def __init__(self):
        self.jobs, self.job = [], {}
        self.granules = []
        self.norm, self.unit = {}, {}
        self.splits, self.split = [], {}
        for j in sorted(range(MOD_FIRST), key=lambda j: mod_number(0, j)):
            self.modulation(0, j)
        for layer in range(DEPTH):
            self.layer(layer)
        self.add_norm(DEPTH, "final")
        self.granules = [g[1:] for g in sorted(self.granules, key=lambda g: g[0])]
        self.granule = {g[0]: n for n, g in enumerate(self.granules)}
        count = {"A": 0, "V": 0}
        self.before = []
        for who in self.jobs:
            self.before.append(dict(count))
            count[who] += 1

    def add(self, who, *key):
        self.job[key] = len(self.jobs)
        self.jobs.append(who)

    def grain(self, *key, split=False, after=None):
        job = len(self.jobs) - 1
        if not split:
            self.granules.append((job if after is None else after, key, "job", job))
            return
        s = self.split[key] = len(self.splits)
        self.splits.append(job)
        if key[:2] == (0, "win") and key[2] < SPLITS:
            after = job - 1 - key[2]
        elif key[1] == "wout" and key[2] < SPLITS:
            after = self.before_wout + 1
        else:
            after = self.splits[s - SPLITS]
        self.granules.append((after - 0.5, key, "split", s))

    def add_norm(self, layer, name):
        tiles = [NORM_TILES[n] for _, n in self.norm]
        self.norm[layer, name] = (len(tiles), sum(tiles), sum(max(0, n - 1) for n in tiles))
        self.add("A", layer, "norm", name)

    def modulation(self, l, j):
        n = mod_number(l, j)
        after = -0.25 if 2 * EARLY <= n < MOD_FIRST else len(self.jobs) - 1
        self.granules.append((after, (l, "mod", j), "mod", n))

    def layer(self, l):
        add, grain = self.add, self.grain
        self.add_norm(l, "n1")
        for what, i in input_schedule(l):
            if what == "win":
                add("V" if WIN[i][:2] == "hy" else "A", l, "win", i)
                grain(l, "win", i, split=True)
            elif what == "mod":
                self.modulation(l, i)
            elif what == "norm":
                self.add_norm(l, i)
            elif what != "square":
                add("A" if what == "vturn" else "V", l, what, i)
        for net in nets(l)[::-1]:
            for t in range(NET_LEN[net] // P):
                add("V", l, "filt", net, t)
        for net in nets(l)[::-1]:
            for i in range(NET_LEN[net] // P):
                add("V", l, "spec", net, i)
                if i == 1:
                    add("A", l, "l1", net)
            add("V", l, "nyq", net)
            if net == "ctx":
                grain(l, "F", net, 0)
        spectra = len(self.jobs) - 1
        for o in range(2):
            for net in nets(l):
                add("A", l, "turn", net, o)
            for net in nets(l):
                for i in range(NET_LEN[net] // P // 2):
                    add("V", l, "fwd", net, o, i)
                if net == "lat":
                    for t in range(LAT // P):
                        grain(l, "F", net, t, o, after=None if o else spectra)
            for net in nets(l):
                add("V", l, "inv", net, o)
                if net == "lat":
                    for t in G_ORDER:
                        if t not in resident(l):
                            grain(l, "G", net, t, o)
        units = retention_units(l)
        for i, un in enumerate(units + [None]):
            if un:
                for part in range(3 if un[0] == "lat" else 1):
                    add("V", l, "rs", *un, part)
            if i:
                add("A", l, "rpv", *units[i - 1])
        self.attention(l, "gqa")
        add("V", l, "krrope")
        for h in range(HEADS):
            add("A", l, "mq", h)
        grain(l, "wuq")
        for h in range(HEADS):
            add("V", l, "mqrope", h)
        for h in range(HEADS):
            add("A", l, "mk", h)
        for part in range(2):
            add("A", l, "mv", part)
        grain(l, "wukv")
        self.before_wout = len(self.jobs) - 1
        self.attention(l, "mla")
        self.add_norm(l, "mla")
        for m in range(KT):
            add("V", l, "wout", m)
            grain(l, "wout", m, split=True)
        self.add_norm(l, "n2")
        j0 = 0
        for s, nj in enumerate(SETS):
            for j in range(j0, j0 + nj):
                add("A", l, "ffa", j)
                grain(l, "ffa", j, split=True)
                add("V", l, "ffg", j)
                grain(l, "ffg", j, split=True)
            j0 += nj
            for what, *i in output_schedule(l, s):
                if what == "mod":
                    self.modulation(l + 1, i[0])
                else:
                    add("V", l, "ffo", s, i[1])
                    grain(l, "ffo", s, i[1], split=True)

    def attention(self, l, kind):
        units = attention_units(l, kind)
        for u in units:
            self.unit[(l,) + u] = len(self.unit)
        for job, u in attention_steps(l, kind):
            if job == "norm":
                self.add_norm(l, u)
            elif job in ("s", "t", "pv"):
                self.add("A", l, job, *u)


def hymba_block(nc, a, out):
    plan = Plan()
    n_units = len(plan.unit)
    with ExitStack() as ctx:
        def sb(name, *shape):
            return ctx.enter_context(nc.sbuf_tensor(name, [P, *shape], F32))

        def sem(name):
            return ctx.enter_context(nc.semaphore(name))

        work = sb("work", WORK)
        work_at = nc.sbuf_base - 4 * WORK
        x = sb("x_resid", KT, TOK)
        ring = sb("ring", RING, GRAN)
        ident = sb("ident", P)
        rot = sb("rot", P)
        rot_mla = sb("rot_mla", MLA_ROPE)
        ones = sb("ones", P)
        blk = sb("blk", P)
        cs = sb("cs", 2, LAT)
        zt_cs = sb("zt_cs", 2 * LAT)
        negt = sb("negt", 6)
        par = sb("par", DEPTH, N_PARAM)
        w_small = sb("w_small", DEPTH, 3 * HY_FFN)
        hb = sb("hb", TOK)
        g_final = sb("g_final", KT)
        mod = sb("mod", DEPTH, N_MOD, 2)
        gain = sb("gain", 2, KT, 2)
        sq = sb("sq", 2, TOK)
        std = sb("std", TOK)
        turned = sb("turned", LAT)
        eps = sb("eps", 1)
        lg = sb("lg", 6, 8)
        smax = sb("smax", n_units)
        nmax = sb("nmax", n_units)
        rsum = sb("rsum", n_units)
        rinv = sb("rinv", n_units)
        ps = ctx.enter_context(nc.psum_tensor("ps", [P, PAIRS, 1024], F32))

        def rounded(name, *shape):
            return nc.alloc_sbuf_tensor_at(f"{name}_r", [P, *shape], F32R, offset=work_at + 4 * AT[name])

        hh, hl = rounded("hh", KT, TOK), rounded("hl", KT, TOK)
        uh, ul = rounded("uh", 6, TOK), rounded("ul", 6, TOK)
        wsplit, wsplit_out = (rounded(n, SPLITS, 2, GRAN) for n in ("wsplit", "wsplit_out"))

        def view(name, *shape):
            n = int(np.prod(shape))
            v = work[:, AT[name]:AT[name] + n]
            if len(shape) == 2:
                v = v.rearrange("p (a b) -> p a b", a=shape[0])
            elif len(shape) == 3:
                v = v.rearrange("p (a b c) -> p a b c", a=shape[0], b=shape[1])
            return v

        retq, retk, retg = (view(n, 2, TOK) for n in ("retq", "retk", "retg"))
        gq, gk, cq, ckv, kr = view("gq", 2, TOK), view("gk", TOK), view("cq", 2, TOK), view("ckv", TOK), view("kr", TOK)
        vret, vgqa = view("vret", 6, GROUP), view("vgqa", 6, P)
        hy, y = view("hy", 6, TOK), view("yraw", KT, TOK)
        spec = {"lat": view("klat", 4, 2, HY_COLS), "ctx": view("kctx", 2, 2, HY_COLS)}
        vtok = {"lat": view("vtok_lat", 4, GROUP), "ctx": view("vtok_ctx", 2, GROUP)}
        yf = {"lat": view("yf_lat", 8, GROUP), "ctx": view("yf_ctx", 4, GROUP)}
        dft_ctx = view("dft_ctx", 2, GRAN)
        tmp0, tmp1 = view("t0", 2, GROUP), view("t1", 2, GROUP)
        absd, w4 = view("absd", 1024), view("w4", 1024)
        edec, filt = view("edec", 2, 1024), view("f", 2, 1024)
        sumabs = {"lat": sq[:, 0, 0:HY_COLS], "ctx": sq[:, 1, 0:HY_COLS]}
        rn = {"lat": std[:, 0:HY_COLS], "ctx": turned[:, 0:HY_COLS]}
        fa = {"lat": view("fa_lat", 4, HY_COLS), "ctx": view("fa_ctx", 2, HY_COLS)}
        fb = {"lat": view("fb_lat", 4, HY_COLS), "ctx": view("fb_ctx", 2, HY_COLS)}
        ha, ht = view("ha", TOK), view("ht", TOK)
        mq, mk, vmla = view("mq", HEADS, TOK), view("mk", HEADS, TOK), view("vmla", 6, GROUP)
        prob = {kind: view(f"prob_{kind}", 3, TOK) for kind in ("gqa", "mla")}
        pt = {kind: view(f"pt_{kind}", 2, TOK) for kind in ("gqa", "mla")}
        scaled = view("scaled", SCALED_TILES, TOK)
        rpt, dec, delta = view("rpt", 2, 6, LAT), (view("dec0", 896 + 640), view("dec1", 896 + 640)), view("delta", 896)
        ut = view("ut", 2, TOK)
        cond, unused = view("cond", 2, D), view("unused", D)
        cs_mla = zt_cs[:, :].rearrange("p (a b) -> p a b", a=2)
        inputs = {f"{n}{i}": t[:, i] for n, t in (("cq", cq), ("gq", gq), ("retq", retq), ("retk", retk), ("retg", retg))
                  for i in range(2)}
        inputs.update(ckv=ckv, kr=kr, gk=gk, vret0=hy[:, 3], vret1=hy[:, 4], vgqa=hy[:, 5])
        by_token = {"vret0": vret[:, :, 0:P], "vret1": vret[:, :, P:GROUP], "vgqa": vgqa}
        inputs.update({f"hy{i}": hy[:, i] for i in range(6)})

        def param(layer, name, i=0):
            at = PARAM[name][0] + i
            return par[:, layer, at:at + 1]

        def win_width(l, name):
            return TOK if name in ALL_TOKENS else width(l)

        x_loaded, cond_loaded, const_loaded = sem("x_loaded"), sem("cond_loaded"), sem("const_loaded")
        dft_loaded = sem("dft_loaded")
        filter_loaded, delta_loaded = sem("filter_loaded"), sem("delta_loaded")
        slot_loaded = [sem(f"slot{i}_loaded") for i in range(RING)]
        out_stored = sem("out_stored")
        job_done = sem("job_done")
        act_drained, dve_drained = sem("act_drained"), sem("dve_drained")
        drained = {"A": act_drained, "V": dve_drained}
        high_done, split_done = sem("high_done"), sem("split_done")
        ones_set = sem("ones_set")
        cond_ready, mod_done = sem("cond_ready"), sem("mod_done")
        angle_ready, sin_ready = sem("angle_ready"), sem("sin_ready")
        decay_ready, filt_ready, ab_ready = sem("decay_ready"), sem("filt_ready"), sem("ab_ready")
        abs_ready, sumabs_ready = sem("abs_ready"), sem("sumabs_ready")
        abs_part, abs_summed = sem("abs_part"), sem("abs_summed")
        squares_ready, squares_used = sem("squares_ready"), sem("squares_used")
        x_squared, squares_added = sem("x_squared"), sem("squares_added")
        norm_applied = sem("norm_applied")
        h_shifted, h_high = sem("h_shifted"), sem("h_high")
        h_scaled, h_rounded, h_ready = sem("h_scaled"), sem("h_rounded"), sem("h_ready")
        conv_part = sem("conv_part")
        kpe_ready, kpe_copied = sem("kpe_ready"), sem("kpe_copied")
        nmax_ready, prob_ready = sem("nmax_ready"), sem("prob_ready")
        log_part, log_ready = sem("log_part"), sem("log_ready")
        dec_arg, dec_exp = sem("dec_arg"), sem("dec_exp")
        u_ready = sem("u_ready")
        dve_chain, act_chain = sem("dve_chain"), sem("act_chain")

        def pair(n):
            return ps[:, n % PAIRS]

        def wait_job(eng, *key):
            eng.wait_ge(job_done, plan.job[key] + 1)

        def wait_drained(eng, *key):
            n = plan.job[key]
            who = plan.jobs[n]
            eng.wait_ge(drained[who], plan.before[n][who] + 1)

        def slot(n):
            return ring[:, n % RING]

        def grid(ap, n):
            return ap.rearrange("p (k c) -> p k c", k=n)

        def columns(key):
            return SETS[key[2]] * P if key[1] == "ffo" else GRAN

        def before_norm(l, name):
            idx = plan.norm[l, name][0]
            return next((k for k in plan.norm if plan.norm[k][0] == idx - 1), None)

        SCALED = {"n1": 0, "y": KT, "n2": 2 * KT}
        split_keys = {n: k for k, n in plan.split.items()}

        def part_of(s, part):
            return (wsplit_out if split_keys[s][1] == "wout" else wsplit)[:, s % SPLITS, part]

        def over_x(l, name):
            return 2 * l + (name == "n2")

        block = ctx.enter_context(nc.Block())

        @block.sync
        def _(sp):
            def source(key):
                l, name = key[0], key[1]
                if name == "F":
                    return a["dft_lat"][key[3]] if key[2] == "lat" else a["dft_ctx"][:, 0]
                if name == "G":
                    return a["dft_lat"][4 + key[3]]
                if name in ("ffa", "ffg"):
                    return a["w_ffn_in"][l, 2 * key[2] + (name == "ffg")]
                if name == "ffo":
                    return a["w_ffn_out"][l, key[2], key[3], :, 0:columns(key)]
                if name in ("wuq", "wukv"):
                    return a[name][l]
                return a[{"mod": "w_mod", "win": "w_in", "wout": "w_out"}[name]][l, key[2]]

            def load(n):
                if n >= RING:
                    _, how, last = plan.granules[n - RING]
                    sp.wait_ge({"split": split_done, "job": job_done, "mod": mod_done}[how], last + 1)
                src = source(plan.granules[n][0])
                sp.dma_start(slot(n)[:, 0:src.shape[1]], src).then_inc(slot_loaded[n % RING], 16)

            n = 0
            for l in range(DEPTH):
                j0 = 0
                for nj in SETS:
                    first = plan.granule[l, "ffa", j0]
                    while n < first + RING:
                        load(n)
                        n += 1
                    s0 = plan.split[l, "ffa", j0]
                    with sp.Fori(0, nj // 2 - 1) as i:
                        for t in range(RING):
                            sp.wait_ge(split_done, s0 + t + 1 + RING * i)
                            sp.dma_start(slot(first + t), a["w_ffn_in"][l, 2 * j0 + RING + t + RING * i])\
                              .then_inc(slot_loaded[(first + t) % RING], 16)
                    n = first + 2 * nj
                    j0 += nj
            while n < len(plan.granules):
                load(n)
                n += 1
            sp.wait_ge(norm_applied, plan.norm[DEPTH, "final"][0] + 1)
            sp.dma_start(out, y[:, :, 0:LAT]).then_inc(out_stored, 16)
            sp.wait_ge(out_stored, 16)

        @block.tensor
        def _(pe):
            def begin(*key):
                n = plan.job[key]
                if n >= PAIRS:
                    who = plan.jobs[n - PAIRS]
                    pe.wait_ge(drained[who], plan.before[n - PAIRS][who] + 1)
                return pair(n)

            def arrived(*key):
                n = plan.granule[key]
                pe.wait_ge(slot_loaded[n % RING], 16 * (n // RING + 1))
                return slot(n)

            def halves(*key):
                s = plan.split[key]
                pe.wait_ge(split_done, s + 1)
                return (grid(part_of(s, part)[:, 0:columns(key)], columns(key) // P) for part in range(2))

            def segments(w):
                return [(c, min(c + LAT, w)) for c in range(0, w, LAT)]

            def norm(l, name, matrix, w):
                _, done, _ = plan.norm[l, name]
                nt = NORM_TILES[name]
                dst = begin(l, "norm", name)
                if nt == 0:
                    pe.wait_ge(squares_added, (KT - 2) * (over_x(l, name) + 1))
                    for c0, c1 in segments(w):
                        pe.matmul(dst[:, c0:c1], matrix[:, :], std[:, c0:c1], start=True, stop=False)
                    pe.wait_ge(x_squared, KT * (over_x(l, name) + 1))
                    for c0, c1 in segments(w):
                        mm = pe.matmul(dst[:, c0:c1], matrix[:, :], sq[:, (KT - 1) % 2, c0:c1], start=False, stop=True)
                for t in range(nt):
                    pe.wait_ge(squares_ready, done + t + 1)
                    for c0, c1 in segments(w):
                        mm = pe.matmul(dst[:, c0:c1], matrix[:, :], sq[:, (done + t) % 2, c0:c1],
                                       start=(t == 0), stop=(t == nt - 1))
                    if t < nt - 1:
                        mm.then_inc(squares_used, 1)
                mm.then_inc(job_done, 1)

            def project(dst, w, w_cols, width_, data=None, order=range(KT), first=None, ready=None):
                dh, dl = data or (hh, hl)
                for n, k in enumerate(order):
                    if first is not None:
                        pe.wait_ge(ready or h_ready, first + n + 1)
                    for c0, c1 in segments(width_):
                        three = ((w[0], dh), (w[0], dl), (w[1], dh))
                        for i, (wp, dp) in enumerate(three):
                            mm = pe.matmul(dst[0:w_cols, c0:c1], wp[:, k, 0:w_cols], dp[:, k, c0:c1],
                                           start=(n == 0 and i == 0), stop=(n == len(order) - 1 and i == 2))
                return mm

            def filter_layer(l, k):
                dst = begin(l, "mlp", k)
                if k:
                    pe.wait_ge(sin_ready, 3 * l + k)
                for c0, c1 in segments(width(l)):
                    rows = HY_FFN if k else HY_EMB
                    src = hb if k else zt_cs
                    mm = pe.matmul(dst[0:HY_FFN, c0:c1], w_small[0:rows, l, k * HY_FFN:(k + 1) * HY_FFN],
                                   src[0:rows, c0:c1], start=True, stop=True)
                mm.then_inc(job_done, 1)

            def values(dst, v, weights, tiles, base, n):
                for j, kt in enumerate(tiles):
                    mm = pe.matmul(dst[base:base + HD, 0:n], v(kt), weights[:, j], start=(j == 0), stop=(j == len(tiles) - 1))
                mm.then_inc(job_done, 1)

            def attention(l, kind):
                for job, un in attention_steps(l, kind):
                    if job == "norm":
                        norm(l, un, blk if un in ("ret0", "ret1") else ones, width(l))
                    if job not in ("s", "t", "pv"):
                        continue
                    _, net, hd, t = un
                    n = plan.unit[(l,) + un]
                    dst = begin(l, job, *un)
                    nk = 6 if net == "lat" else 2
                    if job == "s":
                        c = NET_AT[net] + P * t
                        if kind == "mla":
                            q, keys = mq[0:MLA_D, hd, c:c + P], mk[0:MLA_D, hd]
                        else:
                            kv, r = hd // 2, hd % 2
                            q, keys = gq[HD * kv:HD * kv + HD, r, c:c + P], gk[HD * kv:HD * kv + HD]
                        if net == "lat":
                            pe.matmul(dst[:, 0:LAT], q, keys[:, 0:LAT], start=True, stop=True)
                            pe.matmul(dst[:, LAT:TOK], q, keys[:, LAT:TOK], start=True, stop=True).then_inc(job_done, 1)
                        else:
                            pe.matmul(dst[:, 0:CTX], q, keys[:, LAT:TOK], start=True, stop=True).then_inc(job_done, 1)
                    elif job == "t":
                        pe.wait_ge(prob_ready, n + 1)
                        for j in range(nk):
                            mm = pe.transpose(dst[:, j * P:(j + 1) * P], prob[kind][:, n % 3, j * P:(j + 1) * P], ident[:, :])
                        mm.then_inc(job_done, 1)
                    else:
                        wait_drained(pe, l, "t", *un)
                        col = HD * hd if kind == "mla" else HD * (hd // 2)
                        vt = vmla if kind == "mla" else vgqa
                        values(dst, lambda kt: vt[:, kt, col:col + HD], grid(pt[kind][:, n % 2, 0:nk * P], nk),
                               range(6) if net == "lat" else (4, 5), HD * (hd % 2), P)

            pe.wait_ge(ones_set, 2)
            for l in range(DEPTH):
                W = width(l)
                norm(l, "n1", ones, TOK)
                if l == 0:
                    pe.wait_ge(const_loaded, 16 * N_CONST)
                for what, i in input_schedule(l):
                    if what == "win":
                        name = WIN[i]
                        w = tuple(halves(l, "win", i))
                        dst = begin(l, "win", i)
                        project(dst, w, 96 if name == "kr" else P, win_width(l, name),
                                first=3 * KT * l if i == 0 else None).then_inc(job_done, 1)
                    elif what == "vturn":
                        dst = begin(l, "vturn", i)
                        wait_drained(pe, l, "win", WIN.index(VALUES[i]))
                        for t in range(TOK // P):
                            mm = pe.transpose(dst[:, t * P:(t + 1) * P], inputs[VALUES[i]][:, t * P:(t + 1) * P], ident[:, :])
                        mm.then_inc(job_done, 1)
                    elif what == "mlp":
                        filter_layer(l, i)
                    elif what == "norm":
                        norm(l, i, ones if i in ("cq", "ckv") else blk, win_width(l, i))
                    elif what == "rope":
                        dst = begin(l, "rope", i)
                        if i in ("gq0", "gq1", "gk"):
                            pe.wait_ge(norm_applied, plan.norm[l, i][0] + 1)
                        else:
                            wait_drained(pe, l, "win", WIN.index(i))
                        pe.matmul(dst[:, 0:LAT], rot[:, :], inputs[i][:, 0:LAT], start=True, stop=True).then_inc(job_done, 1)

                pe.wait_ge(sin_ready, 3 * l + 3)
                pe.wait_ge(filter_loaded, 32 * (l + 1))
                for net in nets(l)[::-1]:
                    for t in range(NET_LEN[net] // P):
                        dst = begin(l, "filt", net, t)
                        c = NET_AT[net] + P * t
                        for half in range(2):
                            mm = pe.matmul(dst[:, half * 512:half * 512 + 512], hb[0:HY_FFN, c:c + P],
                                           w4[0:HY_FFN, half * 512:half * 512 + 512], start=True, stop=True)
                        mm.then_inc(job_done, 1)
                for ni, net in enumerate(nets(l)[::-1]):
                    n = NET_LEN[net]
                    nt = n // P
                    if net == "lat":
                        f = [arrived(l, "F", net, t, 0) for t in range(nt)]
                    else:
                        fc = grid(arrived(l, "F", net, 0), 2)
                        f = [fc[:, t] for t in range(nt)]
                    pe.wait_ge(ab_ready, 6 * l + (2 if net == "ctx" else TILES[l]))
                    for i in range(nt):
                        dst = begin(l, "spec", net, i)
                        for part, src in ((0, fa[net]), (1, fb[net])):
                            for t in range(nt):
                                mm = pe.matmul(dst[:, part * 512:part * 512 + 512],
                                               f[t][:, part * n + i * P:part * n + i * P + P], src[:, t],
                                               start=(t == 0), stop=(t == nt - 1))
                        mm.then_inc(job_done, 1)
                        if i == 1:
                            dst = begin(l, "l1", net)
                            pe.wait_ge(sumabs_ready, 2 * l + ni + 1)
                            pe.matmul(dst[:, 0:HY_COLS], ones[:, :], sumabs[net], start=True, stop=True).then_inc(job_done, 1)
                    dst = begin(l, "nyq", net)
                    for t in range(nt):
                        mm = pe.matmul(dst[0:1, 0:HY_COLS], f[t][:, n:n + 1], fa[net][:, t], start=(t == 0), stop=(t == nt - 1))
                    mm.then_inc(job_done, 1)

                for o in range(2):
                    for net in nets(l):
                        c = NET_AT[net]
                        dst = begin(l, "turn", net, o)
                        if o:
                            wait_drained(pe, l, "inv", net, 0)
                        for t in range(NET_LEN[net] // P):
                            for ch in range(2):
                                mm = pe.transpose(dst[:, t * GROUP + ch * P:t * GROUP + ch * P + P],
                                                  hy[:, ch, c + t * P:c + t * P + P], ident[:, :])
                        mm.then_inc(job_done, 1)
                    for net in nets(l):
                        n = NET_LEN[net]
                        nt = n // P
                        if net == "lat":
                            f = [arrived(l, "F", net, t, o) for t in range(nt)]
                        else:
                            pe.wait_ge(dft_loaded, 16)
                            f = [grid(dft_ctx[:, 0], 2)[:, t] for t in range(nt)]
                        wait_drained(pe, l, "turn", net, o)
                        for i in range(nt // 2):
                            dst = begin(l, "fwd", net, o, i)
                            for part in range(2):
                                for q in range(2):
                                    at = part * n + (2 * i + q) * P
                                    for t in range(nt):
                                        mm = pe.matmul(dst[:, part * 512 + q * GROUP:part * 512 + (q + 1) * GROUP],
                                                       f[t][:, at:at + P], vtok[net][:, t], start=(t == 0), stop=(t == nt - 1))
                            mm.then_inc(job_done, 1)
                    for net in nets(l):
                        n = NET_LEN[net]
                        nt = n // P
                        dst = begin(l, "inv", net, o)
                        for i in range(nt // 2):
                            wait_drained(pe, l, "fwd", net, o, i)
                            for half in (0, nt // 2):
                                if net == "ctx":
                                    g = grid(dft_ctx[:, 1], 4)
                                elif i + half in resident(l):
                                    pe.wait_ge(dft_loaded, 16 * (DEPTH - 1) + 32)
                                    g = grid(dft_ctx[:, resident(l).index(i + half)], 2)
                                else:
                                    g = grid(arrived(l, "G", net, i + half, o), 2)
                                for q in range(2):
                                    fi = 2 * (i + half) + q
                                    gt = g[:, q if net == "lat" else fi]
                                    for ch in range(2):
                                        mm = pe.matmul(dst[:, ch * 512:ch * 512 + n], yf[net][:, fi, ch * P:ch * P + P], gt,
                                                       start=(fi == 0), stop=(fi == 2 * nt - 1))
                        mm.then_inc(job_done, 1)

                units = retention_units(l)
                for i, un in enumerate(units + [None]):
                    if un:
                        net, hd = un
                        base, c, n = HD * (hd % 2), NET_AT[net], NET_LEN[net]
                        tiles = list(range(6)) if net == "lat" else [4, 5]
                        for part in range(len(tiles) // 2):
                            dst = begin(l, "rs", *un, part)
                            for q in range(2):
                                kt = tiles[2 * part + q]
                                mm = pe.matmul(dst[:, q * 512:q * 512 + n],
                                               retk[base:base + HD, hd // 2, kt * P:(kt + 1) * P],
                                               retq[base:base + HD, hd // 2, c:c + n], start=True, stop=True)
                            mm.then_inc(job_done, 1)
                    if i:
                        net, hd = units[i - 1]
                        n = NET_LEN[net]
                        tiles = range(6) if net == "lat" else (4, 5)
                        dst = begin(l, "rpv", net, hd)
                        wait_drained(pe, l, "rs", net, hd, len(tiles) // 2 - 1)
                        values(dst, lambda kt: vret[:, kt, HD * hd:HD * hd + HD], rpt[:, (i - 1) % 2, :, 0:n],
                               tiles, HD * (hd % 2), n)
                attention(l, "gqa")

                dst = begin(l, "krrope")
                pe.matmul(dst[64:96, 0:LAT], rot_mla[64:96, :], kr[64:96, 0:LAT], start=True, stop=True)\
                  .then_inc(job_done, 1)
                wuq = grid(arrived(l, "wuq")[:, 0:2 * HEADS * MLA_D], 2)
                for hd in range(HEADS):
                    dst = begin(l, "mq", hd)
                    for t in range(2):
                        for c0, c1 in segments(W):
                            mm = pe.matmul(dst[0:MLA_D, c0:c1], wuq[:, t, hd * MLA_D:(hd + 1) * MLA_D],
                                           cq[:, t, c0:c1], start=(t == 0), stop=(t == 1))
                    mm.then_inc(job_done, 1)
                for hd in range(HEADS):
                    dst = begin(l, "mqrope", hd)
                    wait_drained(pe, l, "mq", hd)
                    pe.matmul(dst[64:96, 0:LAT], rot_mla[64:96, :], mq[64:96, hd, 0:LAT], start=True, stop=True)\
                      .then_inc(job_done, 1)
                wukv = arrived(l, "wukv")
                for hd in range(HEADS):
                    dst = begin(l, "mk", hd)
                    for c0, c1 in segments(TOK):
                        mm = pe.matmul(dst[0:HD, c0:c1], wukv[:, hd * HD:hd * HD + HD], ckv[:, c0:c1], start=True, stop=True)
                    mm.then_inc(job_done, 1)
                for part, tiles in enumerate((range(0, 4), range(4, 6))):
                    dst = begin(l, "mv", part)
                    for i, t in enumerate(tiles):
                        mm = pe.matmul(dst[:, i * GROUP:(i + 1) * GROUP], ckv[:, t * P:(t + 1) * P],
                                       wukv[:, GROUP:2 * GROUP], start=True, stop=True)
                    mm.then_inc(job_done, 1)
                pe.wait_ge(kpe_copied, l + 1)
                wait_drained(pe, l, "mk", HEADS - 1)
                wait_drained(pe, l, "mqrope", HEADS - 1)
                attention(l, "mla")
                norm(l, "mla", ones, W)

                for m in range(KT):
                    w = tuple(halves(l, "wout", m))
                    project(begin(l, "wout", m), w, P, W, order=Y_ORDER, first=None if m else 3 * KT * l + KT)\
                        .then_inc(job_done, 1)
                norm(l, "n2", ones, W)
                j0 = 0
                for s, nj in enumerate(SETS):
                    first, s0 = plan.job[l, "ffa", j0], plan.split[l, "ffa", j0]
                    count = plan.before[first]
                    def two_tiles(i, looped, waits=None):
                        for t in range(PAIRS):
                            who = "AV"[t % 2]
                            if looped:
                                pe.wait_ge(drained[who], count[who] - 1 + t // 2 + 2 * i)
                            else:
                                begin(l, ("ffa", "ffg")[t % 2], j0 + t // 2)
                            pe.wait_ge(split_done, s0 + t + 1 + PAIRS * i)
                            w = tuple(grid(wsplit[:, (s0 + t) % SPLITS, part], KT) for part in range(2))
                            project(pair(first + t), w, P, W, first=waits if t == 0 else None).then_inc(job_done, 1)

                    two_tiles(0, False, None if s else 3 * KT * l + 2 * KT)
                    with pe.Fori(1, nj // 2) as i:
                        two_tiles(i, True)
                    j0 += nj
                    for what, *i in output_schedule(l, s):
                        if what == "ffo":
                            w = tuple(halves(l, "ffo", s, i[1]))
                            project(begin(l, "ffo", s, i[1]), w, P, W, data=(uh, ul), order=range(nj),
                                    first=None if i[1] else l * NF + j0 - nj, ready=u_ready).then_inc(job_done, 1)
            norm(DEPTH, "final", ones, LAT)

        @block.scalar
        def _(act):
            def drain(*key):
                wait_job(act, *key)
                return pair(plan.job[key])

            links = [0]

            def link(ins):
                links[0] += 1
                ins.then_inc(act_chain, 1)
                act.wait_ge(act_chain, links[0])

            def round_high(s):
                key = split_keys[s]
                n = plan.granule[key]
                act.wait_ge(slot_loaded[n % RING], 16 * (n // RING + 1))
                if s >= SPLITS:
                    act.wait_ge(job_done, plan.splits[s - SPLITS] + 1)
                w = columns(key)
                act.activation(part_of(s, 0)[:, 0:w], slot(n)[:, 0:w], ACT.Copy).then_inc(high_done, 1)

            def last_norm_over(l, name):
                prev = before_norm(l, name)
                if prev:
                    act.wait_ge(job_done, plan.job[prev[0], "norm", prev[1]] + 1)
                    act.wait_ge(norm_applied, plan.norm[l, name][0])

            def square(l, name, srcs, w):
                done = plan.norm[l, name][1]
                last_norm_over(l, name)
                for t, src in enumerate(srcs):
                    act.activation(sq[:, (done + t) % 2, 0:w], src[:, 0:w], ACT.Square).then_inc(squares_ready, 1)

            def square_x(l, name, k, w):
                b = over_x(l, name)
                if k == 0:
                    last_norm_over(l, name)
                elif k > 2:
                    act.wait_ge(squares_added, (KT - 2) * b + k - 2)
                dst = sq[:, k % 2] if k else std
                act.activation(dst[:, 0:w], x[:, k, 0:w], ACT.Square).then_inc(x_squared, 1)

            def root(l, name, n, w):
                p = drain(l, "norm", name)
                if name in RECIPROCAL:
                    act.activation(std[:, 0:w], p[:, 0:w], ACT.Sqrt, bias=eps[:, :], scale=1.0 / n).then_inc(act_drained, 1)
                else:
                    link(act.activation(std[:, 0:w], p[:, 0:w], ACT.Ln, bias=eps[:, :], scale=1.0 / n))
                    act.activation(std[:, 0:w], std[:, 0:w], ACT.Exp, scale=-0.5).then_inc(act_drained, 1)

            def shift_x(l, which, w):
                at = {"n1": 0, "n2": 3 * KT}[which]
                for k in range(KT):
                    act.wait_ge(h_scaled, 3 * KT * l + SCALED[which] + k + 1)
                    for s, c0, c1 in ((0, 0, LAT), (1, LAT, TOK))[:1 + (w > LAT)]:
                        tile = scaled[:, k % SCALED_TILES, c0:c1]
                        ins = act.activation(tile, tile, ACT.Identity, bias=mod[:, l, at + k, s:s + 1],
                                             scale=gain[:, int(which == "n2"), k, s:s + 1])
                    ins.then_inc(h_shifted, 1)

            def high_output(l, n):
                t, w = Y_ORDER[n], width(l)
                act.wait_ge(h_scaled, 3 * KT * l + KT + n + 1)
                act.activation(hh[:, t, 0:w], y[:, t, 0:w], ACT.Copy).then_inc(h_rounded, 1)

            def attention(l, kind, tile0, scale):
                for job, un in attention_steps(l, kind):
                    if job == "square":
                        if un == "gqa":
                            wait_drained(act, l, "pv", *attention_units(l, "gqa")[-1])
                        square(l, un, [y[:, t] for t in OUTPUTS[un]], width(l))
                    elif job == "norm":
                        root(l, un, HD if un in ("ret0", "ret1") else GROUP, width(l))
                    elif job == "high":
                        high_output(l, un)
                    if job not in ("s", "t", "pv"):
                        continue
                    _, net, hd, t = un
                    n = plan.unit[(l,) + un]
                    p = drain(l, job, *un)
                    if job == "s":
                        wide = TOK if net == "lat" else CTX
                        act.wait_ge(nmax_ready, n + 1)
                        if n >= 3:
                            prev = next(k for k in plan.unit if plan.unit[k] == n - 3)
                            wait_job(act, prev[0], "t", *prev[1:])
                        act.activation(prob[kind][:, n % 3, 0:wide], p[:, 0:wide], ACT.Exp, bias=nmax[:, n:n + 1],
                                       scale=scale, accum_out=rsum[:, n:n + 1]).then_inc(act_drained, 1)
                    elif job == "t":
                        wide = TOK if net == "lat" else CTX
                        act.activation(pt[kind][:, n % 2, 0:wide], p[:, 0:wide], ACT.Copy).then_inc(act_drained, 1)
                    else:
                        base, c = HD * (hd % 2), NET_AT[net] + P * t
                        act.activation(y[base:base + HD, tile0 + hd // 2, c:c + P], p[base:base + HD, 0:P],
                                       ACT.Copy).then_inc(act_drained, 1)

            act.dma_start(cond, a["cond"]).then_inc(cond_loaded, 16)
            act.dma_start(par[:, :, :], a["par"]).then_inc(cond_loaded, 16)
            act.dma_start(x[:, :, :], a["x"]).then_inc(x_loaded, 16)
            for dst, name in ((ident, "ident"), (rot, "rot"), (rot_mla, "rot_mla"), (blk, "blk"),
                              (cs, "cs"), (zt_cs, "zt_cs"), (negt, "negt"), (g_final, "g_final"), (w_small, "w_small")):
                act.dma_start(dst[tuple(slice(None) for _ in dst.shape)], a[name]).then_inc(const_loaded, 16)

            act.wait_ge(cond_loaded, 32)
            act.activation(cond, cond, ACT.Silu).then_inc(cond_ready, 1)
            act.wait_ge(x_loaded, 16)
            act.wait_ge(ones_set, 2)
            for l in range(DEPTH):
                W = width(l)
                for k in range(0 if l else KT):
                    square_x(l, "n1", k, TOK)
                root(l, "n1", D, TOK)
                if l == 0:
                    round_high(0)
                    round_high(1)
                shift_x(l, "n1", TOK)
                at = PARAM["decay"][0]
                link(act.activation(lg[:, 1, :], par[:, l, at:at + 8], ACT.Abs))
                act.activation(lg[:, 2, :], lg[:, 1, :], ACT.Exp, scale=-1.0).then_inc(log_part, 1)
                act.wait_ge(log_ready, 2 * l + 1)
                act.activation(lg[:, 4, :], lg[:, 3, :], ACT.Ln).then_inc(log_part, 1)
                for what, i in input_schedule(l):
                    if what == "win":
                        name = WIN[i]
                        p = drain(l, "win", i)
                        w = win_width(l, name)
                        dst = inputs[name]
                        if name[:2] == "hy":
                            g = int(name[2])
                            act.activation(dst[:, 0:W], p[:, 0:W], ACT.Identity, bias=param(l, "conv_b", g),
                                           scale=param(l, "conv_w", 6 + g)).then_inc(conv_part, 1)
                        else:
                            rows = slice(64, 96) if name == "kr" else slice(0, P)
                            act.activation(dst[rows, 0:w], p[rows, 0:w], ACT.Silu if name[:4] == "retg" else ACT.Copy,
                                           scale=RET_K_SCALE if name[:4] == "retk" else 1.0).then_inc(act_drained, 1)
                        if i + SPLITS < N_WIN:
                            round_high(plan.split[l, "win", i] + SPLITS)
                        if i == N_WIN - 4:
                            act.wait_ge(mod_done, (l + 1) * N_MOD)
                            act.dma_start(w4[0:HY_FFN], a["w4"][l]).then_inc(filter_loaded, 16)
                            act.dma_start(absd, a["absd"]).then_inc(filter_loaded, 16)
                    elif what == "vturn":
                        p = drain(l, "vturn", i)
                        act.activation(by_token[VALUES[i]], p[:, 0:TOK].rearrange("p (t c) -> p t c", t=6), ACT.Copy)\
                           .then_inc(act_drained, 1)
                    elif what == "square":
                        tiles = ("cq0", "cq1") if i == "cq" else (i,)
                        wait_drained(act, l, "win", WIN.index(tiles[-1]))
                        square(l, i, [inputs[name] for name in tiles], win_width(l, i))
                    elif what == "norm":
                        root(l, i, {"cq": GROUP, "ckv": P}.get(i, HD), win_width(l, i))
                    elif what == "mlp":
                        act.wait_ge(angle_ready, 3 * l + i + 1)
                        act.activation(hb[0:HY_FFN, 0:W], ht[0:HY_FFN, 0:W], ACT.Sin).then_inc(sin_ready, 1)
                wait_job(act, l, "win", N_WIN - 1)
                act.wait_ge(filter_loaded, 32 * (l + 1))
                s = 6 * l
                tiles = [(net, t) for net in nets(l)[::-1] for t in range(NET_LEN[net] // P)]

                def decay(i):
                    net, t = tiles[i]
                    if i >= 2:
                        act.wait_ge(filt_ready, s + i - 1)
                    tt = t + (4 if net == "ctx" else 0)
                    act.activation(edec[:, i % 2], absd, ACT.Exp, scale=negt[:, tt:tt + 1]).then_inc(decay_ready, 1)

                decay(0)
                for i in range(len(tiles)):
                    if i + 1 < len(tiles):
                        decay(i + 1)
                    act.wait_ge(ab_ready, s + i + 1)
                    act.activation(filt[:, i % 2], filt[:, i % 2], ACT.Abs).then_inc(abs_ready, 1)
                for net in nets(l)[::-1]:
                    p = drain(l, "l1", net)
                    act.activation(rn[net], p[:, 0:HY_COLS], ACT.Copy).then_inc(act_drained, 1)
                if l < DEPTH - 1:
                    wait_job(act, l, "nyq", nets(l)[0])
                    act.dma_start(dft_ctx, a["dft_ctx"]).then_inc(dft_loaded, 16)
                wait_job(act, l, "nyq", "lat")
                for n, t in enumerate(resident(l)):
                    act.dma_start(dft_ctx[:, n], a["dft_lat"][4 + t]).then_inc(dft_loaded, 16)
                act.dma_start(delta, a["delta"]).then_inc(delta_loaded, 16)

                def table(hd):
                    act.wait_ge(dec_arg, HEADS * l + hd + 1)
                    t = dec[hd % 2]
                    link(act.activation(t[:, 0:896], t[:, 0:896], ACT.Exp))
                    act.activation(t[:, 896:1536], delta[:, 256:896], ACT.Exp, bias=lg[:, 5, hd:hd + 1],
                                   scale=lg[:, 0, hd:hd + 1])
                    act.activation(sq[:, 0, 0:640], delta[:, 256:896], ACT.Exp, bias=lg[:, 5, 4 + hd:5 + hd],
                                   scale=lg[:, 1, 4 + hd:5 + hd]).then_inc(dec_exp, 1)

                for o in range(2):
                    if o:
                        act.wait_ge(delta_loaded, 16 * (l + 1))
                        table(0)
                    for net in nets(l):
                        nt = NET_LEN[net] // P
                        p = drain(l, "turn", net, o)
                        act.activation(vtok[net], p[:, 0:nt * GROUP].rearrange("p (t c) -> p t c", t=nt), ACT.Copy)\
                           .then_inc(act_drained, 1)
                units = retention_units(l)
                for net, hd in units:
                    if net == "lat" and hd + 1 < HEADS:
                        table(hd + 1)
                    base, c, m = HD * (hd % 2), NET_AT[net], NET_LEN[net]
                    p = drain(l, "rpv", net, hd)
                    act.activation(y[base:base + HD, 4 + hd // 2, c:c + m], p[base:base + HD, 0:m], ACT.Copy)\
                       .then_inc(act_drained, 1)
                wait_drained(act, l, "rpv", *units[-1])
                attention(l, "gqa", 6, GQA_SCALE)
                for hd in range(HEADS):
                    p = drain(l, "mq", hd)
                    act.activation(mq[0:MLA_D, hd, 0:W], p[0:MLA_D, 0:W], ACT.Copy).then_inc(act_drained, 1)
                for hd in range(HEADS):
                    p = drain(l, "mk", hd)
                    act.activation(mk[0:HD, hd, :], p[0:HD, 0:TOK], ACT.Copy).then_inc(act_drained, 1)
                for part, (t0, t1) in enumerate(((0, 4), (4, 6))):
                    p = drain(l, "mv", part)
                    act.activation(vmla[:, t0:t1], p[:, 0:(t1 - t0) * GROUP].rearrange("p (t c) -> p t c", c=GROUP), ACT.Copy)\
                       .then_inc(act_drained, 1)
                act.wait_ge(norm_applied, plan.norm[l, "ret1"][0] + 1)
                s = plan.split[l, "wout", 0]
                round_high(s)
                round_high(s + 1)
                attention(l, "mla", 2, MLA_SCALE)
                wait_drained(act, l, "pv", *attention_units(l, "mla")[-1])
                square(l, "mla", [y[:, 2], y[:, 3]], W)
                root(l, "mla", GROUP, W)
                high_output(l, KT - 2)
                high_output(l, KT - 1)
                for m in range(KT):
                    if m:
                        wait_drained(act, l, "wout", m - 1)
                        square_x(l, "n2", m - 1, W)
                    wait_job(act, l, "wout", m)
                    if m == KT - SPLITS:
                        act.wait_ge(h_ready, 3 * KT * l + 2 * KT)
                    round_high(s + m + SPLITS)
                    if m == 2 and l < DEPTH - 1:
                        act.wait_ge(h_ready, 3 * KT * l + 2 * KT)
                        act.dma_start(cond, a["cond"]).then_inc(cond_loaded, 16)
                wait_drained(act, l, "wout", KT - 1)
                square_x(l, "n2", KT - 1, W)
                root(l, "n2", D, W)
                shift_x(l, "n2", W)
                after = "n1" if l + 1 < DEPTH else "final"
                if l < DEPTH - 1:
                    act.wait_ge(cond_loaded, 16 * (l + 3))
                    act.activation(cond, cond, ACT.Silu).then_inc(cond_ready, 1)
                j0 = 0
                for st, nj in enumerate(SETS):
                    first, s0 = plan.job[l, "ffa", j0], plan.split[l, "ffa", j0]
                    g0 = plan.granule[l, "ffa", j0]
                    used = plan.before[first]["V"]

                    def gates(i, last):
                        for t in range(PAIRS):
                            act.wait_ge(job_done, first + t + 1 + PAIRS * i)
                            if t % 2 == 0:
                                act.wait_ge(dve_drained, used + t // 2 - 1 + 2 * i)
                                act.activation(sq[:, t // 2, 0:W], pair(first + t)[:, 0:W], ACT.Silu).then_inc(act_drained, 1)
                            if last and t >= PAIRS - SPLITS:
                                round_high(plan.split[l, "ffo", st, t - (PAIRS - SPLITS)])
                            else:
                                g = g0 + t + SPLITS
                                act.wait_ge(slot_loaded[g % RING], 16 * (g // RING + 1) + 16 * i)
                                act.activation(wsplit[:, (s0 + t) % SPLITS, 0], slot(g), ACT.Copy).then_inc(high_done, 1)

                    with act.Fori(0, nj // 2 - 1) as i:
                        gates(i, False)
                    gates(nj // 2 - 1, True)
                    j0 += nj
                    for what, *i in output_schedule(l, st):
                        if what == "ffo":
                            m = i[1]
                            last_set = st == len(SETS) - 1
                            if last_set and m:
                                wait_drained(act, l, "ffo", st, m - 1)
                                square_x(l + 1, after, m - 1, TOK if l + 1 < DEPTH else LAT)
                            wait_job(act, l, "ffo", st, m)
                            nxt = plan.split[l, "ffo", st, m] + SPLITS
                            if nxt < len(plan.splits):
                                round_high(nxt)
                            if last_set and m == KT - 1:
                                wait_drained(act, l, "ffo", st, m)
                                square_x(l + 1, after, m, TOK if l + 1 < DEPTH else LAT)
            root(DEPTH, "final", D, LAT)

        @block.gpsimd
        def _(pool):
            pool.memset(ones[:, :], 1.0).then_inc(ones_set, 1)
            pool.memset(eps[:, :], EPS).then_inc(ones_set, 1)

            def low(dst, exact, high):
                return pool.tensor_tensor(dst, exact, high.bitcast(F32), ALU.subtract)

            def split_low(s):
                key = split_keys[s]
                n, w = plan.granule[key], columns(key)
                pool.wait_ge(high_done, s + 1)
                low(part_of(s, 1)[:, 0:w], slot(n)[:, 0:w], part_of(s, 0)[:, 0:w]).then_inc(split_done, 1)

            def add_square(l, name, k, w):
                b = over_x(l, name)
                pool.wait_ge(x_squared, KT * b + k + 1)
                if k > 1:
                    pool.wait_ge(squares_added, (KT - 2) * b + k - 1)
                pool.tensor_tensor(std[:, 0:w], std[:, 0:w], sq[:, k % 2, 0:w], ALU.add).then_inc(squares_added, 1)

            def low_parts(l, which, w):
                for k in range(KT):
                    pool.wait_ge(h_high, KT * over_x(l, which) + k + 1)
                    low(hl[:, k, 0:w], scaled[:, k % SCALED_TILES, 0:w], hh[:, k, 0:w]).then_inc(h_ready, 1)

            def low_output(l, n):
                t, w = Y_ORDER[n], width(l)
                pool.wait_ge(h_rounded, KT * l + n + 1)
                low(hl[:, t, 0:w], y[:, t, 0:w], hh[:, t, 0:w]).then_inc(h_ready, 1)

            parts = 0
            for l in range(DEPTH):
                W = width(l)
                for k in range(1, 1 if l else KT - 1):
                    add_square(l, "n1", k, TOK)
                for s in range(0 if l else SPLITS):
                    split_low(s)
                low_parts(l, "n1", TOK)
                for i in range(N_WIN - SPLITS):
                    split_low(plan.split[l, "win", i] + SPLITS)
                s = 6 * l
                i = 0
                for net in nets(l)[::-1]:
                    for t in range(NET_LEN[net] // P):
                        pool.wait_ge(abs_ready, s + 1)
                        f = filt[:, i % 2]
                        if t == 0:
                            pool.tensor_tensor(sumabs[net], f[:, 0:512], f[:, 512:1024], ALU.add).then_inc(abs_part, 1)
                            parts += 1
                        else:
                            for half in range(2):
                                pool.tensor_tensor(sumabs[net], sumabs[net], f[:, half * 512:half * 512 + 512], ALU.add).then_inc(abs_part, 1)
                                parts += 1
                                if not half:
                                    pool.wait_ge(abs_part, parts)
                        pool.wait_ge(abs_part, parts)
                        pool.engine_nop().then_inc(abs_summed, 1)
                        i += 1
                        s += 1
                    pool.engine_nop().then_inc(sumabs_ready, 1)
                pool.wait_ge(kpe_ready, l + 1)
                for hd in range(HEADS):
                    ins = pool.tensor_copy(mk[64:96, hd, :], kr[64:96, :])
                ins.then_inc(kpe_copied, 1)
                pool.wait_ge(kpe_copied, l + 1)
                s = plan.split[l, "wout", 0]
                for i in range(SPLITS):
                    split_low(s + i)
                for n in range(KT):
                    low_output(l, n)
                for m in range(KT):
                    if m > 1:
                        add_square(l, "n2", m - 1, W)
                    split_low(s + m + SPLITS)
                low_parts(l, "n2", W)
                j0 = 0
                for st, nj in enumerate(SETS):
                    s0, g0 = plan.split[l, "ffa", j0], plan.granule[l, "ffa", j0]

                    def granules(i, last):
                        for t in range(PAIRS):
                            if last and t >= PAIRS - SPLITS:
                                split_low(plan.split[l, "ffo", st, t - (PAIRS - SPLITS)])
                            else:
                                pool.wait_ge(high_done, s0 + t + SPLITS + 1 + PAIRS * i)
                                part = wsplit[:, (s0 + t) % SPLITS]
                                low(part[:, 1], slot(g0 + t + SPLITS), part[:, 0]).then_inc(split_done, 1)

                    with pool.Fori(0, nj // 2 - 1) as i:
                        granules(i, False)
                    granules(nj // 2 - 1, True)
                    j0 += nj
                    for m in range(KT):
                        if st == len(SETS) - 1 and m > 1:
                            after, w = ("n1", TOK) if l + 1 < DEPTH else ("final", LAT)
                            add_square(l + 1, after, m - 1, w)
                        nxt = plan.split[l, "ffo", st, m] + SPLITS
                        if nxt < len(plan.splits):
                            split_low(nxt)

        @block.vector
        def _(dve):
            def drain(*key):
                wait_job(dve, *key)
                return pair(plan.job[key])

            links = [0]

            def link(ins, turns=0):
                links[0] += 1
                ins.then_inc(dve_chain, 1)
                dve.wait_ge(dve_chain, links[0] + turns)

            def signal(what):
                dve.engine_nop().then_inc(what, 1)

            def modulation(l, j):
                n, m = plan.granule[l, "mod", j], mod_number(l, j)
                dve.wait_ge(slot_loaded[n % RING], 16 * (n // RING + 1))
                if m:
                    dve.wait_ge(mod_done, m)
                for c, products in ((0, unused), (1, slot(n))):
                    ins = dve.tensor_tensor_reduce(products, slot(n), cond[:, c], 1.0, param(l, "b_mod", j), ALU.mult, ALU.add,
                                                   accum_out=mod[:, l, j, c:c + 1])
                ins.then_inc(mod_done, 1)

            def scales(l, name, w):
                n = plan.job[l, "norm", name]
                dve.wait_ge(act_drained, plan.before[n]["A"] + 1)
                if name in RECIPROCAL:
                    link(dve.reciprocal(std[:, 0:w], std[:, 0:w]))

            def norm(l, name, tiles, gains, w, gate=None, into=None):
                scales(l, name, w)
                for t, g, dst in zip(tiles, gains, into or tiles):
                    ins = dve.scalar_tensor_tensor(dst[:, 0:w], t[:, 0:w], g, std[:, 0:w], ALU.mult, ALU.mult)
                    if gate is not None:
                        link(ins)
                        ins = dve.tensor_tensor(t[:, 0:w], t[:, 0:w], gate[:, 0:w], ALU.mult)
                ins.then_inc(norm_applied, 1)

            def group_norm(l, name, w):
                scales(l, name, w)
                for t in OUTPUTS[name]:
                    dve.scalar_tensor_tensor(y[:, t, 0:w], y[:, t, 0:w], param(l, "g_out", t), std[:, 0:w],
                                             ALU.mult, ALU.mult).then_inc(h_scaled, 1)
                dve.wait_ge(h_scaled, 3 * KT * l + KT + Y_ORDER.index(OUTPUTS[name][1]) + 1)
                signal(norm_applied)

            def scale_x(l, which, w, between=None):
                scales(l, which, w)
                base = 3 * KT * l + SCALED[which]

                def high(k):
                    dve.wait_ge(h_shifted, KT * over_x(l, which) + k + 1)
                    dve.tensor_copy(hh[:, k, 0:w], scaled[:, k % SCALED_TILES, 0:w]).then_inc(h_high, 1)

                highs = 0
                for k in range(KT):
                    if between and k in LATE_BEFORE:
                        while highs < k:
                            high(highs)
                            highs += 1
                        between(k)
                    if k >= SCALED_TILES:
                        dve.wait_ge(h_ready, base + k - SCALED_TILES + 1)
                    dve.tensor_tensor(scaled[:, k % SCALED_TILES, 0:w], x[:, k, 0:w], std[:, 0:w], ALU.mult).then_inc(h_scaled, 1)
                    if k and highs == k - 1:
                        high(highs)
                        highs += 1
                for k in range(highs, KT):
                    high(k)
                dve.wait_ge(h_scaled, base + KT)
                signal(norm_applied)

            def gains(l, which, k0=0, k1=KT):
                name, at = (("g_attn", KT), ("g_ffn", 4 * KT))[which]
                g0 = PARAM[name][0]
                link(dve.scalar_tensor_tensor(gain[:, which, k0:k1], mod[:, l, at + k0:at + k1, :], 1.0,
                                              par[:, l, g0 + k0:g0 + k1, None].to_broadcast([P, k1 - k0, 2]),
                                              ALU.add, ALU.mult))

            def attention(l, kind, scale):
                for job, un in attention_steps(l, kind):
                    if job == "norm":
                        if un in ("ret0", "ret1"):
                            i = int(un[3])
                            norm(l, un, [y[:, 4 + i]], [param(l, "g_ret", i)], width(l), gate=retg[:, i])
                        else:
                            group_norm(l, un, width(l))
                    elif job == "s":
                        n = plan.unit[(l,) + un]
                        wide = TOK if un[1] == "lat" else CTX
                        p = drain(l, "s", *un)
                        link(dve.reduce_max(smax[:, n:n + 1], p[:, 0:wide], AX))
                        dve.tensor_scalar(nmax[:, n:n + 1], smax[:, n:n + 1], -scale, None, ALU.mult).then_inc(nmax_ready, 1)
                    elif job == "scale":
                        n = plan.unit[(l,) + un]
                        wide = TOK if un[1] == "lat" else CTX
                        wait_drained(dve, l, "s", *un)
                        link(dve.reciprocal(rinv[:, n:n + 1], rsum[:, n:n + 1]))
                        dve.tensor_scalar(prob[kind][:, n % 3, 0:wide], prob[kind][:, n % 3, 0:wide], rinv[:, n:n + 1], None, ALU.mult)\
                           .then_inc(prob_ready, 1)

            def residual(l, m, at, w, *key):
                p = drain(l, *key)
                for s, (c0, c1) in enumerate(((0, LAT), (LAT, TOK))[:1 + (w > LAT)]):
                    ins = dve.scalar_tensor_tensor(x[:, m, c0:c1], p[:, c0:c1], mod[:, l, at + m, s:s + 1], x[:, m, c0:c1],
                                                   ALU.mult, ALU.add)
                ins.then_inc(dve_drained, 1)

            def rotate(src, dst_ps, table, rows):
                dve.tensor_tensor(src[rows, 0:LAT], src[rows, 0:LAT], table[rows, 0, :], ALU.mult)
                link(dve.tensor_tensor(turned[rows, :], dst_ps[rows, 0:LAT], table[rows, 1, :], ALU.mult))
                link(dve.tensor_tensor(src[rows, 0:LAT], src[rows, 0:LAT], turned[rows, :], ALU.add))

            dve.wait_ge(cond_loaded, 32)
            dve.wait_ge(cond_ready, 1)

            def late_modulation(k):
                late = EARLY + LATE_BEFORE.index(k)
                modulation(0, late)
                modulation(0, KT + late)
                dve.wait_ge(mod_done, 2 * late + 2)
                gains(0, 0, late, late + 1)

            for k in range(EARLY):
                modulation(0, k)
                modulation(0, KT + k)
            dve.wait_ge(const_loaded, 16 * N_CONST)
            for l in range(DEPTH):
                W = width(l)
                if l == 0:
                    dve.wait_ge(mod_done, 2 * EARLY)
                    gains(l, 0, 0, EARLY)
                    scale_x(l, "n1", TOK, late_modulation)
                else:
                    dve.wait_ge(mod_done, (l + 1) * N_MOD)
                    gains(l, 0)
                    scale_x(l, "n1", TOK)
                at = PARAM["decay"][0]
                dve.wait_ge(log_part, 2 * l + 1)
                dve.tensor_scalar(lg[:, 3, :], lg[:, 2, :], 1.0, None, ALU.add).then_inc(log_ready, 1)
                dve.wait_ge(log_part, 2 * l + 2)
                link(dve.tensor_scalar(lg[:, 0, :], par[:, l, at:at + 8], 0.0, None, ALU.min))
                link(dve.tensor_tensor(lg[:, 0, :], lg[:, 0, :], lg[:, 4, :], ALU.subtract))
                dve.tensor_scalar(lg[:, 1, :], lg[:, 0, :], -1.0, None, ALU.mult)
                dve.tensor_scalar(lg[:, 5, 0:4], lg[:, 0, 0:4], float(CTX), None, ALU.mult)
                link(dve.tensor_scalar(lg[:, 5, 4:8], lg[:, 0, 4:8], float(LAT), None, ALU.mult))
                signal(log_ready)
                for what, i in input_schedule(l):
                    if what == "win":
                        name = WIN[i]
                        if name[:2] == "hy":
                            g = int(name[2])
                            p = drain(l, "win", i)
                            dve.wait_ge(conv_part, 6 * l + g + 1)
                            for net in nets(l):
                                c0, c1 = NET_AT[net], NET_AT[net] + NET_LEN[net]
                                link(dve.scalar_tensor_tensor(hy[:, g, c0 + 1:c1], p[:, c0:c1 - 1], param(l, "conv_w", g),
                                                              hy[:, g, c0 + 1:c1], ALU.mult, ALU.add))
                                ins = dve.scalar_tensor_tensor(hy[:, g, c0:c1 - 1], p[:, c0 + 1:c1], param(l, "conv_w", 12 + g),
                                                               hy[:, g, c0:c1 - 1], ALU.mult, ALU.add)
                            ins.then_inc(dve_drained, 1)
                    elif what == "mod":
                        modulation(l, i)
                    elif what == "norm":
                        tiles, gs = {"cq": (("cq0", "cq1"), ("g_q", "g_q")), "ckv": (("ckv",), ("g_kv",)),
                                     "gk": (("gk",), ("g_gk",))}.get(i, ((i,), ("g_gq",)))
                        norm(l, i, [inputs[t] for t in tiles],
                             [param(l, g, n if i == "cq" else 0) for n, g in enumerate(gs)], win_width(l, i))
                    elif what == "rope":
                        rotate(inputs[i], drain(l, "rope", i), cs, slice(0, P))
                        signal(dve_drained)
                    elif what == "mlp":
                        p = drain(l, "mlp", i)
                        rows = slice(0, HY_FFN)
                        link(dve.tensor_scalar(ha[rows, 0:W], p[rows, 0:W], param(l, f"b{i + 1}")[rows], param(l, "freq")[rows],
                                               ALU.add, ALU.mult))
                        if i:
                            dve.wait_ge(sin_ready, 3 * l + i)
                        link(dve.tensor_scalar(ht[rows, 0:W], ha[rows, 0:W], INV_2PI, MAGIC, ALU.mult, ALU.add))
                        link(dve.tensor_scalar(ht[rows, 0:W], ht[rows, 0:W], MAGIC, None, ALU.subtract))
                        link(dve.scalar_tensor_tensor(ha[rows, 0:W], ht[rows, 0:W], -TWO_PI_HI, ha[rows, 0:W], ALU.mult, ALU.add))
                        link(dve.scalar_tensor_tensor(ht[rows, 0:W], ht[rows, 0:W], -TWO_PI_LO, ha[rows, 0:W], ALU.mult, ALU.add))
                        link(dve.tensor_scalar(ht[rows, 0:W], ht[rows, 0:W], PI_BELOW, -PI_BELOW, ALU.min, ALU.max))
                        signal(angle_ready)
                        signal(dve_drained)
                if l == 0:
                    dve.wait_ge(mod_done, N_MOD)
                wait_job(dve, l, "win", N_WIN - 1)
                i = 0
                for net in nets(l)[::-1]:
                    for t in range(NET_LEN[net] // P):
                        s = 6 * l + i
                        p = drain(l, "filt", net, t)
                        dve.wait_ge(decay_ready, s + 1)
                        if i >= 2:
                            dve.wait_ge(abs_summed, s - 1)
                        f = filt[:, i % 2]
                        link(dve.scalar_tensor_tensor(f, edec[:, i % 2], 0.05, p, ALU.add, ALU.mult))
                        if t == 0:
                            link(dve.memset(f[0:1, 512:1024], 0.0))
                        signal(filt_ready)
                        signal(dve_drained)
                        link(dve.tensor_tensor(fa[net][:, t], f[:, 0:512], f[:, 512:1024], ALU.add))
                        dve.tensor_tensor(fb[net][:, t], f[:, 0:512], f[:, 512:1024], ALU.subtract).then_inc(ab_ready, 1)
                        i += 1
                for net in nets(l)[::-1]:
                    wait_drained(dve, l, "l1", net)
                    link(dve.reciprocal(rn[net], rn[net]))
                    for q in range(NET_LEN[net] // P):
                        p = drain(l, "spec", net, q)
                        link(dve.tensor_tensor(spec[net][:, q], p.rearrange("p (a b) -> p a b", a=2),
                                               rn[net][:, None, :].to_broadcast([P, 2, HY_COLS]), ALU.mult))
                        signal(dve_drained)
                    p = drain(l, "nyq", net)
                    link(dve.tensor_tensor(spec[net][0:1, 0, 1, :], p[0:1, 0:512], rn[net][0:1, :], ALU.mult))
                    signal(dve_drained)
                def arguments(hd):
                    t = dec[hd % 2]
                    link(dve.tensor_scalar(t[:, 0:896], delta, 0.0, lg[:, 0, hd:hd + 1], ALU.max, ALU.mult))
                    link(dve.tensor_scalar(sq[:, 1, 0:768], delta[:, 0:768], 0.0, lg[:, 1, 4 + hd:5 + hd], ALU.min, ALU.mult))
                    link(dve.tensor_tensor(t[:, 0:768], t[:, 0:768], sq[:, 1, 0:768], ALU.add))
                    signal(dec_arg)

                def finish(hd):
                    t = dec[hd % 2]
                    dve.wait_ge(dec_exp, HEADS * l + hd + 1)
                    link(dve.tensor_tensor(t[:, 384:512], t[:, 384:512], ident[:, :], ALU.add))
                    link(dve.tensor_tensor(t[:, 896:1536], t[:, 896:1536], sq[:, 0, 0:640], ALU.add))

                for o in range(2):
                    for net in nets(l):
                        nt = NET_LEN[net] // P
                        for i in range(nt // 2):
                            p = drain(l, "fwd", net, o, i)
                            ur, ui = (p[:, q * 512:q * 512 + 512].rearrange("p (a b) -> p a b", a=2) for q in range(2))
                            kre, kim = (spec[net][:, 2 * i:2 * i + 2, q, o * GROUP:(o + 1) * GROUP] for q in range(2))
                            yr, yi = yf[net][:, 2 * i:2 * i + 2], yf[net][:, nt + 2 * i:nt + 2 * i + 2]
                            dve.tensor_tensor(yr, ur, kre, ALU.mult)
                            dve.tensor_tensor(tmp0, ui, kim, ALU.mult)
                            dve.tensor_tensor(yi, ur, kim, ALU.mult)
                            link(dve.tensor_tensor(tmp1, ui, kre, ALU.mult))
                            dve.tensor_tensor(yr, yr, tmp0, ALU.subtract)
                            link(dve.tensor_tensor(yi, yi, tmp1, ALU.add))
                            if i == 0:
                                dve.tensor_tensor(yr[0:1, 0], ur[0:1, 0], kre[0:1, 0], ALU.mult)
                                link(dve.tensor_tensor(yi[0:1, 0], ui[0:1, 0], kim[0:1, 0], ALU.mult))
                            signal(dve_drained)
                    for net in nets(l):
                        n, c = NET_LEN[net], NET_AT[net]
                        p = drain(l, "inv", net, o)
                        for ch in range(2):
                            v = hy[:, ch, c:c + n]
                            gate = hy[:, 2 + 2 * o + ch, c:c + n]
                            dst = y[:, ch, c:c + n] if o else v
                            link(dve.scalar_tensor_tensor(v, v, param(l, "hy_bias", 2 * o + ch), p[:, ch * 512:ch * 512 + n],
                                                          ALU.mult, ALU.add))
                            link(dve.tensor_tensor(dst, v, gate, ALU.mult))
                        signal(dve_drained)
                        if o == 0 and net == "lat":
                            dve.wait_ge(delta_loaded, 16 * (l + 1))
                            arguments(0)

                units = retention_units(l)
                for n, (net, hd) in enumerate(units):
                    if net == "lat":
                        finish(hd)
                        if hd + 1 < HEADS:
                            if hd:
                                wait_drained(dve, l, "rs", nets(l)[-1], hd - 1, 2 if W == LAT else 0)
                            arguments(hd + 1)
                    m = NET_LEN[net]
                    tiles = list(range(6)) if net == "lat" else [4, 5]
                    for part in range(len(tiles) // 2):
                        p = drain(l, "rs", net, hd, part)
                        for q in range(2):
                            kt = tiles[2 * part + q]
                            if net == "lat" and kt >= 4:
                                at = 896 + 384 - 256 - P * (kt - 4)
                            elif net == "lat":
                                at = 384 - P * kt
                            else:
                                at = 384 - P * (kt - 4)
                            ins = dve.tensor_tensor(rpt[:, n % 2, 2 * part + q, 0:m], p[:, q * 512:q * 512 + m],
                                                    dec[hd % 2][:, at:at + m], ALU.mult)
                        ins.then_inc(dve_drained, 1)
                attention(l, "gqa", GQA_SCALE)
                rows = slice(64, 96)
                rotate(kr, drain(l, "krrope"), cs_mla, rows)
                signal(kpe_ready)
                signal(dve_drained)
                for hd in range(HEADS):
                    rotate(mq[:, hd], drain(l, "mqrope", hd), cs_mla, rows)
                    signal(dve_drained)
                attention(l, "mla", MLA_SCALE)
                group_norm(l, "mla", W)
                for m in range(KT):
                    residual(l, m, 2 * KT, W, "wout", m)
                gains(l, 1)
                scale_x(l, "n2", W)
                if l < DEPTH - 1:
                    dve.wait_ge(cond_ready, l + 2)
                j0 = 0
                for st, nj in enumerate(SETS):
                    first, s0 = plan.job[l, "ffa", j0], plan.split[l, "ffa", j0]
                    g0 = plan.granule[l, "ffa", j0]
                    silus, mine = plan.before[first]["A"], plan.before[first]["V"]
                    per = 2

                    def hidden(i, turns):
                        for t in range(PAIRS):
                            if t % 2:
                                half = t // 2
                                dve.wait_ge(job_done, first + t + 1 + PAIRS * i)
                                dve.wait_ge(act_drained, silus + half + 1 + 2 * i)
                                dve.tensor_tensor(ut[:, half, 0:W], sq[:, half, 0:W], pair(first + t)[:, 0:W], ALU.mult)\
                                   .then_inc(dve_drained, 1)
                                dve.wait_ge(dve_drained, mine + half + 1 + 2 * i)
                                link(dve.tensor_copy(uh[:, half + 2 * i, 0:W], ut[:, half, 0:W]), turns)
                                dve.tensor_tensor(ul[:, half + 2 * i, 0:W], ut[:, half, 0:W],
                                                  uh[:, half + 2 * i, 0:W].bitcast(F32), ALU.subtract).then_inc(u_ready, 1)
                                dve.wait_ge(u_ready, l * NF + j0 + half + 1 + 2 * i)

                    with dve.Fori(0, nj // 2) as i:
                        hidden(i, per * i)
                    links[0] += per * (nj // 2 - 1)
                    j0 += nj
                    for what, *i in output_schedule(l, st):
                        if what == "mod":
                            modulation(l + 1, i[0])
                        else:
                            residual(l, i[1], 5 * KT, W, "ffo", st, i[1])
            norm(DEPTH, "final", [x[:, k] for k in range(KT)], [g_final[:, k:k + 1] for k in range(KT)], LAT,
                 into=[y[:, k] for k in range(KT)])


N_CONST = 9


def constants():
    f = np.float32
    c = {"ident": np.eye(P), "blk": np.kron(np.eye(2), np.ones((HD, HD)))}
    def turn(n):
        r = np.zeros((n, n))
        for m in range(n // 2):
            r[m + n // 2, m] = -1.0
            r[m, m + n // 2] = 1.0
        return r
    c["rot"] = np.kron(np.eye(2), turn(HD))
    c["rot_mla"] = np.zeros((P, MLA_ROPE))
    c["rot_mla"][64:96] = turn(MLA_ROPE)
    c["delta"] = np.arange(896)[None, :] - np.arange(P)[:, None] - 384.0

    def rope(dim):
        q = dim // 4
        inv = THETA ** (-np.arange(q) / q)
        tok = np.arange(LAT)
        ang = np.concatenate([inv[:, None] * (tok // GRID_W)[None], inv[:, None] * (tok % GRID_W)[None]])
        ang = np.concatenate([ang, ang])
        return np.stack([np.cos(ang), np.sin(ang)], 1)

    c["cs"] = np.tile(rope(HD), (2, 1, 1))
    bands = (HY_EMB - 1) // 2
    fb = np.linspace(1e-4, bands - 1, bands)
    zt, negt = np.zeros((P, TOK)), np.zeros((P, 6))
    for net, n in NET_LEN.items():
        t = np.linspace(0.0, 1.0, n)
        w = 2.0 * np.pi * np.arange(n) / n
        at = NET_AT[net]
        zt[0, at:at + n] = t
        zt[1:1 + bands, at:at + n] = np.cos(fb[:, None] * w)
        zt[1 + bands:HY_EMB, at:at + n] = -np.sin(fb[:, None] * w)
        negt[:, at // P:(at + n) // P] = -t.reshape(-1, P).T
        tk, fr = np.arange(n)[:, None], np.arange(n)[None, :]
        ang = np.pi * tk * fr / n
        im = -np.sin(ang)
        im[:, 0] = (-1.0) ** np.arange(n)
        fwd = np.concatenate([np.cos(ang), im], 1)
        scale = np.full((2 * n, 1), 2.0)
        scale[0] = scale[n] = 1.0
        inv = fwd.T * scale / (2 * n)
        if net == "lat":
            c["dft_lat"] = np.concatenate([fwd.reshape(4, P, 2 * n),
                                           inv.reshape(4, 2, P, n).transpose(0, 2, 1, 3).reshape(4, P, 2 * n)])
        else:
            c["dft_ctx"] = np.stack([fwd.reshape(2, P, 2 * n).transpose(1, 0, 2).reshape(P, 4 * n),
                                     inv.reshape(4, P, n).transpose(1, 0, 2).reshape(P, 4 * n)])
    c["dft_ctx"] = c["dft_ctx"].transpose(1, 0, 2)
    c["zt_cs"], c["negt"] = np.zeros((P, 2 * LAT)), negt
    c["zt_cs"][0:HY_EMB, 0:TOK] = zt[0:HY_EMB]
    c["zt_cs"][64:96] = rope(MLA_ROPE).reshape(MLA_ROPE, 2 * LAT)
    lo, hi = np.log(1e-2) / 0.3, np.log(1e-2) / 1.5
    dl = np.abs(np.linspace(lo, hi, 4 * GROUP)).reshape(2, 2, GROUP).transpose(1, 0, 2).reshape(1, -1)
    c["absd"] = np.tile(dl, (P, 1))
    return {k: np.ascontiguousarray(v, dtype=f) for k, v in c.items()}


def layout(v):
    f = np.float32

    def grains(w):
        k, n = w.shape[0] // P, w.shape[1] // P
        return w.reshape(k, P, n, P).transpose(2, 1, 0, 3).reshape(n, P, k * P)

    def cols(w, m):
        return w.reshape(m, P).T

    o = {}
    o["x"] = np.concatenate([v["x"][0], v["ctx"][0]]).T.reshape(KT, P, TOK).transpose(1, 0, 2)
    o["cond"] = np.tile(np.stack([v["c"][0], v["c_ctx"]]), (P, 1, 1))
    o["g_final"] = cols(v["final_norm_g"], KT)
    o["w_mod"] = np.stack([v["w_mod"][l].T.reshape(N_MOD, P, D) for l in range(DEPTH)])
    q0 = 3 * GROUP
    r0 = q0 + GROUP + P + MLA_ROPE
    g0 = r0 + 4 * GROUP
    win = []
    for l in range(DEPTH):
        w = v["w_in"][l]
        kr = np.zeros((D, P), f)
        kr[:, 64:96] = w[:, r0 - MLA_ROPE:r0]
        gq = w[:, g0:g0 + GROUP].reshape(D, 2, 2, HD).transpose(0, 2, 1, 3).reshape(D, GROUP)
        win.append(grains(np.concatenate([
            w[:, q0:q0 + GROUP + P], kr, gq, w[:, g0 + GROUP:g0 + GROUP + P], w[:, r0:r0 + 2 * GROUP],
            w[:, r0 + 3 * GROUP:g0], w[:, r0 + 2 * GROUP:r0 + 3 * GROUP], w[:, g0 + GROUP + P:g0 + GROUP + 2 * P],
            w[:, 0:q0]], 1)))
    o["w_in"] = np.stack(win)
    o["w_out"] = np.stack([grains(v["w_out"][l]) for l in range(DEPTH)])
    o["w_ffn_in"] = np.stack([grains(v["w_ffn_in"][l]).reshape(2, NF, P, D).transpose(1, 0, 2, 3).reshape(2 * NF, P, D)
                              for l in range(DEPTH)])
    o["w_ffn_out"] = np.zeros((DEPTH, len(SETS), KT, P, max(SETS) * P), f)
    for l in range(DEPTH):
        j0 = 0
        for s, nj in enumerate(SETS):
            blocks = v["w_ffn_out"][l][j0 * P:(j0 + nj) * P].reshape(nj, P, KT, P).transpose(2, 1, 0, 3)
            o["w_ffn_out"][l, s, :, :, 0:nj * P] = blocks.reshape(KT, P, nj * P)
            j0 += nj
    o["w_small"] = np.zeros((P, DEPTH, 3 * HY_FFN), f)
    o["w_small"][0:HY_EMB, :, 0:HY_FFN] = v["hy_w1"].transpose(1, 0, 2)
    o["w_small"][0:HY_FFN, :, HY_FFN:2 * HY_FFN] = v["hy_w2"].transpose(1, 0, 2)
    o["w_small"][0:HY_FFN, :, 2 * HY_FFN:] = v["hy_w3"].transpose(1, 0, 2)
    o["w4"] = v["hy_w4"].reshape(DEPTH, HY_FFN, 2, 2, GROUP).transpose(0, 1, 3, 2, 4).reshape(DEPTH, HY_FFN, 1024)
    o["wuq"] = v["mla_w_uq"].reshape(DEPTH, 2, P, HEADS * MLA_D).transpose(0, 2, 1, 3).reshape(DEPTH, P, -1)
    o["wukv"] = v["mla_w_ukv"].reshape(DEPTH, P, HEADS, 2, HD).transpose(0, 1, 3, 2, 4).reshape(DEPTH, P, 2 * GROUP)

    def pad(w):
        z = np.zeros((P, 1), f)
        z[:len(w), 0] = w
        return z

    par = np.zeros((P, DEPTH, N_PARAM), f)
    for l in range(DEPTH):
        for name, val in (
                ("b_mod", cols(v["b_mod"][l], N_MOD)), ("g_attn", cols(v["norm_attn_g"][l], KT)),
                ("g_ffn", cols(v["norm_ffn_g"][l], KT)), ("conv_b", cols(v["hy_conv_b"][l], 6)),
                ("conv_w", cols(v["hy_conv_w"][l].reshape(-1), 18)), ("hy_bias", cols(v["hy_bias"][l].reshape(-1), 4)),
                ("g_q", cols(v["mla_q_norm_g"][l], 2)), ("g_kv", cols(v["mla_kv_norm_g"][l], 1)),
                ("g_ret", cols(v["ret_norm_g"][l], 2)), ("g_out", cols(v["out_norm_g"][l], 8)),
                ("g_gq", np.tile(v["gqa_q_norm_g"][l], 2)[:, None]), ("g_gk", np.tile(v["gqa_k_norm_g"][l], 2)[:, None]),
                ("decay", np.tile(v["ret_decay"][l].reshape(1, 8), (P, 1))),
                ("b1", pad(v["hy_b1"][l])), ("b2", pad(v["hy_b2"][l])), ("b3", pad(v["hy_b3"][l])),
                ("freq", pad(v["hy_freq"][l]))):
            at, n = PARAM[name]
            par[:, l, at:at + n] = val
    o["par"] = par
    return o


def kernel(**inputs):
    import concourse.bacc as bacc
    from concourse.bass_utils import run_bass_kernel_spmd

    nc = bacc.Bacc("TRN2", target_bir_lowering=False, num_devices=1)
    arrays = {**layout({k: np.asarray(w) for k, w in inputs.items()}), **constants()}
    arrays = {f"in_{k}": np.ascontiguousarray(w) for k, w in arrays.items()}
    aps = {k[3:]: nc.dram_tensor(k, w.shape, F32, kind="ExternalInput").ap() for k, w in arrays.items()}
    out = nc.dram_tensor("out_dram", (P, KT, LAT), F32, kind="ExternalOutput").ap()
    hymba_block(nc, aps, out)
    got = run_bass_kernel_spmd(nc, [arrays], core_ids=[0]).results[0]["out_dram"]
    return np.ascontiguousarray(got.transpose(2, 1, 0).reshape(1, LAT, D))
```
